# Optimizing a Trainium2 kernel written in Bass

```python
import math
import jax, jax.numpy as jnp
from jax import lax
import numpy as np

D_MODEL = 1024
BATCH = 1
SEQ = 1024
DEPTH = 1
DEC_BATCH = 8
DEC_SEQ = 1
PAST_LEN = 8192
PAGE_SIZE = 128

HG_DK = 64
HG_DV = 64
HG_HEADS = D_MODEL // 256
HG_KW = HG_HEADS * HG_DK
HG_WIDTH = HG_HEADS * HG_DV
HG_CHUNK = 16
MB_HEADDIM = 64
MB_HEADS = D_MODEL // 128
MB_DINNER = MB_HEADS * MB_HEADDIM
MB_GROUPS = 2
MB_DSTATE = 64
MB_CONV = 4
MB_CONV_DIM = MB_DINNER + 2 * MB_GROUPS * MB_DSTATE
MB_CHUNK = 128
RW_HEAD = 64
RW_HEADS = D_MODEL // 256
RW_WIDTH = RW_HEADS * RW_HEAD
RW_W_LORA = 32
RW_A_LORA = 32
RW_G_LORA = 64
RW_SHIFT_DIM = 3 * RW_WIDTH + RW_W_LORA + RW_A_LORA + RW_G_LORA
RW_GN_EPS = 64e-5
MIX_WIDTH = HG_WIDTH + MB_DINNER + RW_WIDTH
HG_IN = 2 * HG_KW + 2 * HG_WIDTH
MB_IN = MB_DINNER + MB_CONV_DIM + MB_HEADS
IN_DIM = HG_IN + MB_IN + RW_SHIFT_DIM
D_FF = ((8 * D_MODEL // 3 + 255) // 256) * 256
N_MOD = 6
RMS_EPS = 1e-6

kernel_name = "hymba_hgrn2_ssd_rwkv7_adaln_step"

def rmsnorm(x, g, eps=RMS_EPS):
    x32 = x.astype(jnp.float32)
    return x32 * lax.rsqrt(jnp.mean(x32 * x32, -1, keepdims=True) + eps) * g.astype(jnp.float32)

def pad_time(a, t_pad):
    return jnp.pad(a, [(0, 0), (0, t_pad - a.shape[1])] + [(0, 0)] * (a.ndim - 2))

def hgrn2_lower_bounds(lb_logits):
    cs = jnp.cumsum(jax.nn.softmax(lb_logits.astype(jnp.float32), axis=0), axis=0)
    return cs - cs[:1]

def hgrn2_chunked(q, k, v, logf, s0):
    bsz, t_len, nh, _ = q.shape
    L = min(HG_CHUNK, t_len)
    tp = -(-t_len // L) * L
    q, k, v, logf = (pad_time(a, tp) for a in (q, k, v, logf))
    nc = tp // L
    q, k, v, logf = (a.reshape(bsz, nc, L, nh, a.shape[-1]) for a in (q, k, v, logf))
    b = jnp.cumsum(logf, axis=2)
    causal = jnp.tril(jnp.ones((L, L), bool))
    diff = b[:, :, :, None] - b[:, :, None, :]
    decay = jnp.exp(jnp.where(causal[None, None, :, :, None, None], diff, -jnp.inf))
    att = jnp.einsum('bcthk,bcshk,bctshk->bchts', q, k, decay)
    o_intra = jnp.einsum('bchts,bcshv->bcthv', att, v)
    btot = b[:, :, -1]
    u = jnp.einsum('bcshk,bcshv->bchkv', k * jnp.exp(btot[:, :, None] - b), v)

    def step(S, inp):
        dec, uc = inp
        return dec[..., None] * S + uc, S

    s_final, s_enter = lax.scan(step, s0, (jnp.moveaxis(jnp.exp(btot), 1, 0), jnp.moveaxis(u, 1, 0)))
    s_enter = jnp.moveaxis(s_enter, 0, 1)
    o_inter = jnp.einsum('bcthk,bchkv->bcthv', q * jnp.exp(b), s_enter)
    o = (o_intra + o_inter).reshape(bsz, tp, nh, -1)[:, :t_len]
    return o, s_final

def ssd_chunked(x, dt, A, Bm, Cm, h0):
    bsz, t_len, nh, hp = x.shape
    ng, ns = Bm.shape[2], Bm.shape[3]
    rg = nh // ng
    L = min(MB_CHUNK, t_len)
    tp = -(-t_len // L) * L
    x, dt, Bm, Cm = (pad_time(a, tp) for a in (x, dt, Bm, Cm))
    nc = tp // L
    x = x.reshape(bsz, nc, L, ng, rg, hp)
    dt = dt.reshape(bsz, nc, L, ng, rg)
    Bm = Bm.reshape(bsz, nc, L, ng, ns)
    Cm = Cm.reshape(bsz, nc, L, ng, ns)
    acum = jnp.cumsum(dt * A.reshape(ng, rg), axis=2)
    causal = jnp.tril(jnp.ones((L, L), bool))
    seg = acum[:, :, :, None] - acum[:, :, None, :]
    lmat = jnp.exp(jnp.where(causal[None, None, :, :, None, None], seg, -jnp.inf))
    cb = jnp.einsum('bctgn,bcsgn->bctsg', Cm, Bm)
    xdt = x * dt[..., None]
    y_intra = jnp.einsum('bctsg,bctsgr,bcsgrp->bctgrp', cb, lmat, xdt)
    atot = acum[:, :, -1]
    states = jnp.einsum('bcsgn,bcsgr,bcsgrp->bcgrpn', Bm, jnp.exp(atot[:, :, None] - acum), xdt)

    def step(h, inp):
        dec, sc = inp
        return dec[..., None, None] * h + sc, h

    h_final, h_enter = lax.scan(step, h0.reshape(bsz, ng, rg, hp, ns),
                                (jnp.moveaxis(jnp.exp(atot), 1, 0), jnp.moveaxis(states, 1, 0)))
    h_enter = jnp.moveaxis(h_enter, 0, 1)
    y_inter = jnp.einsum('bctgn,bcgrpn,bctgr->bctgrp', Cm, h_enter, jnp.exp(acum))
    y = (y_intra + y_inter).reshape(bsz, tp, nh, hp)[:, :t_len]
    return y, h_final.reshape(bsz, nh, hp, ns)

def rwkv7_scan(r, logw, k, v, kk, a, s0):
    def step(S, inp):
        r_t, w_t, k_t, v_t, kk_t, a_t = inp
        sa = jnp.einsum('bhvk,bhk->bhv', S, -kk_t)
        S = (S * jnp.exp(w_t)[:, :, None, :] + sa[..., :, None] * (kk_t * a_t)[..., None, :]
             + v_t[..., :, None] * k_t[..., None, :])
        return S, jnp.einsum('bhvk,bhk->bhv', S, r_t)

    xs = tuple(jnp.moveaxis(t, 1, 0) for t in (r, logw, k, v, kk, a))
    s_final, out = lax.scan(step, s0, xs)
    return jnp.moveaxis(out, 0, 1), s_final

def token_mix(h, s_hg, s_ssm, s_conv, s_wkv, s_shift, lb, l, P):
    f32 = jnp.float32
    bsz, t_len, _ = h.shape
    heads = lambda t, n: t.reshape(bsz, t_len, -1, n)
    proj = h @ P['w_in'][l]
    cuts = np.cumsum([HG_KW, HG_KW, HG_WIDTH, HG_WIDTH, MB_DINNER, MB_CONV_DIM, MB_HEADS]).tolist()
    hg_q, hg_f, hg_i, hg_g, mb_z, mb_xbc, mb_dt, rw_p = jnp.split(proj, cuts, axis=-1)

    logf = jnp.logaddexp(jnp.log(lb), jnp.log1p(-lb) + jax.nn.log_sigmoid(hg_f))
    hk = (1.0 - lb) * jax.nn.sigmoid(-hg_f)
    o_hg, s_hg_new = hgrn2_chunked(heads(hg_q, HG_DK), heads(hk, HG_DK), heads(hg_i, HG_DV),
                                   heads(logf, HG_DK), s_hg.astype(f32))
    o_hg = rmsnorm(o_hg, P['hg_norm_g'][l].reshape(HG_HEADS, HG_DV)).reshape(bsz, t_len, HG_WIDTH) * jax.nn.silu(hg_g)

    xbc_full = jnp.concatenate([s_conv.astype(f32), mb_xbc], axis=1)
    conv_w = P['mb_conv_w'][l]
    xbc = sum(xbc_full[:, j:j + t_len] * conv_w[j] for j in range(MB_CONV)) + P['mb_conv_b'][l]
    xbc = jax.nn.silu(xbc)
    m_x, m_b, m_c = jnp.split(xbc, [MB_DINNER, MB_DINNER + MB_GROUPS * MB_DSTATE], axis=-1)
    dt = jax.nn.softplus(mb_dt + P['mb_dt_bias'][l])
    A = -jnp.exp(P['mb_A_log'][l].astype(f32))
    m_x = heads(m_x, MB_HEADDIM)
    y_mb, s_ssm_new = ssd_chunked(m_x, dt, A, heads(m_b, MB_DSTATE), heads(m_c, MB_DSTATE), s_ssm.astype(f32))
    y_mb = (y_mb + P['mb_D'][l][:, None] * m_x).reshape(bsz, t_len, MB_DINNER) * jax.nn.silu(mb_z)
    y_mb = rmsnorm(y_mb.reshape(bsz, t_len, MB_GROUPS, -1),
                   P['mb_norm_g'][l].reshape(MB_GROUPS, -1)).reshape(bsz, t_len, MB_DINNER)
    conv_new = xbc_full[:, t_len:]

    prev = jnp.concatenate([s_shift[:, None].astype(f32), rw_p[:, :-1]], axis=1)
    mixd = rw_p + (prev - rw_p) * P['rw_mu'][l]
    cuts_rw = np.cumsum([RW_WIDTH, RW_WIDTH, RW_WIDTH, RW_W_LORA, RW_A_LORA]).tolist()
    r, k, v, wl, al, gl = jnp.split(mixd, cuts_rw, axis=-1)
    logw = -jnp.exp(-jax.nn.softplus(-(P['rw_w0'][l] + jnp.tanh(wl) @ P['rw_w2'][l])) - 0.5)
    a = jax.nn.sigmoid(P['rw_a0'][l] + al @ P['rw_a2'][l])
    g = jax.nn.sigmoid(gl) @ P['rw_g2'][l]
    kk = heads(k * P['rw_k_k'][l], RW_HEAD)
    kk = kk * lax.rsqrt(jnp.maximum(jnp.sum(kk * kk, -1, keepdims=True), 1e-24))
    k = k * (1.0 + (a - 1.0) * P['rw_k_a'][l])
    r_h, k_h, v_h, a_h, w_h = (heads(t, RW_HEAD) for t in (r, k, v, a, logw))
    o_rw, s_wkv_new = rwkv7_scan(r_h, w_h, k_h, v_h, kk, a_h, s_wkv.astype(f32))
    mu = jnp.mean(o_rw, -1, keepdims=True)
    var = jnp.mean(jnp.square(o_rw - mu), -1, keepdims=True)
    o_rw = ((o_rw - mu) * lax.rsqrt(var + RW_GN_EPS) * P['rw_ln_g'][l].reshape(RW_HEADS, RW_HEAD)
            + P['rw_ln_b'][l].reshape(RW_HEADS, RW_HEAD))
    o_rw = o_rw + jnp.sum(r_h * k_h * P['rw_r_k'][l], -1, keepdims=True) * v_h
    o_rw = o_rw.reshape(bsz, t_len, RW_WIDTH) * g
    shift_new = rw_p[:, -1]

    mix = jnp.concatenate([o_hg, y_mb, o_rw], axis=-1) @ P['w_out'][l]
    new_states = (s_hg_new.astype(s_hg.dtype), s_ssm_new.astype(s_ssm.dtype), conv_new.astype(s_conv.dtype),
                  s_wkv_new.astype(s_wkv.dtype), shift_new.astype(s_shift.dtype))
    return mix, new_states

def trunk(x, c, st_hg, st_ssm, st_conv, st_wkv, st_shift, lb_all, P):
    outs = ([], [], [], [], [])
    c_act = jax.nn.silu(c.astype(jnp.float32))
    for l in range(DEPTH):
        mod = c_act @ P['w_ada'][l] + P['b_ada'][l]
        sh1, sc1, g1, sh2, sc2, g2 = (m[:, None, :] for m in jnp.split(mod, N_MOD, axis=-1))
        h = rmsnorm(x, P['g_norm1'][l]) * (1.0 + sc1) + sh1
        mix, states = token_mix(h, st_hg[l], st_ssm[l], st_conv[l], st_wkv[l], st_shift[l], lb_all[l], l, P)
        x = x + (g1 * mix).astype(x.dtype)
        h = rmsnorm(x, P['g_norm2'][l]) * (1.0 + sc2) + sh2
        ff = (jax.nn.silu(h @ P['w_gate'][l]) * (h @ P['w_up'][l])) @ P['w_down'][l]
        x = x + (g2 * ff).astype(x.dtype)
        for lst, s in zip(outs, states):
            lst.append(s)
    y = rmsnorm(x, P['g_final']).astype(x.dtype)
    return y, [jnp.stack(lst) for lst in outs]

def setup_inputs(seed: int = 0) -> dict:
    key = jax.random.key(seed)
    ks = iter(jax.random.split(key, 64))
    f32 = jnp.float32
    nrm = lambda shape, scale: scale * jax.random.normal(next(ks), shape, f32)
    unif = lambda shape, lo, hi: jax.random.uniform(next(ks), shape, f32, lo, hi)
    gain = lambda shape: 1.0 + nrm(shape, 0.05)
    d = {}
    d['x_prompt'] = nrm((BATCH, SEQ, D_MODEL), 1.0)
    d['x_sample'] = nrm((DEC_BATCH, DEC_SEQ, D_MODEL), 1.0)
    d['state_hgrn'] = nrm((DEPTH, DEC_BATCH, HG_HEADS, HG_DK, HG_DV), 0.5)
    d['state_ssm'] = nrm((DEPTH, DEC_BATCH, MB_HEADS, MB_HEADDIM, MB_DSTATE), 0.5)
    d['state_conv'] = nrm((DEPTH, DEC_BATCH, MB_CONV - 1, MB_CONV_DIM), 1.0)
    d['state_wkv'] = nrm((DEPTH, DEC_BATCH, RW_HEADS, RW_HEAD, RW_HEAD), 0.5)
    d['state_shift'] = nrm((DEPTH, DEC_BATCH, RW_SHIFT_DIM), 1.0)
    d['c_prompt'] = nrm((BATCH, D_MODEL), 1.0)
    d['c_sample'] = nrm((DEC_BATCH, D_MODEL), 1.0)
    d['w_ada'] = nrm((DEPTH, D_MODEL, N_MOD * D_MODEL), 0.3 * D_MODEL ** -0.5)
    d['b_ada'] = nrm((DEPTH, N_MOD * D_MODEL), 0.05)
    d['g_norm1'] = gain((DEPTH, D_MODEL))
    d['w_in'] = nrm((DEPTH, D_MODEL, IN_DIM), D_MODEL ** -0.5)
    d['hg_lb_logits'] = nrm((DEPTH, HG_KW), 1.0)
    d['hg_norm_g'] = gain((DEPTH, HG_WIDTH))
    d['mb_conv_w'] = nrm((DEPTH, MB_CONV, MB_CONV_DIM), 0.5)
    d['mb_conv_b'] = nrm((DEPTH, MB_CONV_DIM), 0.05)
    dt0 = jnp.exp(unif((DEPTH, MB_HEADS), math.log(1e-3), math.log(1e-1)))
    d['mb_dt_bias'] = dt0 + jnp.log(-jnp.expm1(-dt0))
    d['mb_A_log'] = jnp.log(unif((DEPTH, MB_HEADS), 1.0, 16.0))
    d['mb_D'] = gain((DEPTH, MB_HEADS))
    d['mb_norm_g'] = gain((DEPTH, MB_DINNER))
    d['rw_mu'] = unif((DEPTH, RW_SHIFT_DIM), 0.0, 1.0)
    d['rw_w0'] = unif((DEPTH, RW_WIDTH), -6.5, -1.5)
    d['rw_w2'] = nrm((DEPTH, RW_W_LORA, RW_WIDTH), 0.5 * RW_W_LORA ** -0.5)
    d['rw_a0'] = nrm((DEPTH, RW_WIDTH), 0.1)
    d['rw_a2'] = nrm((DEPTH, RW_A_LORA, RW_WIDTH), 0.5 * RW_A_LORA ** -0.5)
    d['rw_g2'] = nrm((DEPTH, RW_G_LORA, RW_WIDTH), RW_G_LORA ** -0.5)
    d['rw_k_k'] = 0.85 + nrm((DEPTH, RW_WIDTH), 0.05)
    d['rw_k_a'] = gain((DEPTH, RW_WIDTH))
    d['rw_r_k'] = nrm((DEPTH, RW_HEADS, RW_HEAD), 0.1)
    d['rw_ln_g'] = gain((DEPTH, RW_WIDTH))
    d['rw_ln_b'] = nrm((DEPTH, RW_WIDTH), 0.02)
    d['w_out'] = nrm((DEPTH, MIX_WIDTH, D_MODEL), MIX_WIDTH ** -0.5)
    d['g_norm2'] = gain((DEPTH, D_MODEL))
    d['w_gate'] = nrm((DEPTH, D_MODEL, D_FF), D_MODEL ** -0.5)
    d['w_up'] = nrm((DEPTH, D_MODEL, D_FF), D_MODEL ** -0.5)
    d['w_down'] = nrm((DEPTH, D_FF, D_MODEL), D_FF ** -0.5)
    d['g_final'] = gain((D_MODEL,))
    return d

def reference(x_prompt, x_sample, state_hgrn, state_ssm, state_conv, state_wkv, state_shift, c_prompt, c_sample,
              w_ada, b_ada, g_norm1, w_in, hg_lb_logits, hg_norm_g, mb_conv_w, mb_conv_b, mb_dt_bias, mb_A_log,
              mb_D, mb_norm_g, rw_mu, rw_w0, rw_w2, rw_a0, rw_a2, rw_g2, rw_k_k, rw_k_a, rw_r_k, rw_ln_g, rw_ln_b,
              w_out, g_norm2, w_gate, w_up, w_down, g_final):
    P = dict(w_ada=w_ada, b_ada=b_ada, g_norm1=g_norm1, w_in=w_in, hg_norm_g=hg_norm_g,
             mb_conv_w=mb_conv_w, mb_conv_b=mb_conv_b, mb_dt_bias=mb_dt_bias, mb_A_log=mb_A_log, mb_D=mb_D,
             mb_norm_g=mb_norm_g, rw_mu=rw_mu, rw_w0=rw_w0, rw_w2=rw_w2, rw_a0=rw_a0, rw_a2=rw_a2, rw_g2=rw_g2,
             rw_k_k=rw_k_k, rw_k_a=rw_k_a, rw_r_k=rw_r_k, rw_ln_g=rw_ln_g, rw_ln_b=rw_ln_b, w_out=w_out,
             g_norm2=g_norm2, w_gate=w_gate, w_up=w_up, w_down=w_down, g_final=g_final)
    lb_all = hgrn2_lower_bounds(hg_lb_logits)
    dtp = x_prompt.dtype
    z_hg = jnp.zeros((DEPTH, BATCH, HG_HEADS, HG_DK, HG_DV), dtp)
    z_ssm = jnp.zeros((DEPTH, BATCH, MB_HEADS, MB_HEADDIM, MB_DSTATE), dtp)
    z_conv = jnp.zeros((DEPTH, BATCH, MB_CONV - 1, MB_CONV_DIM), dtp)
    z_wkv = jnp.zeros((DEPTH, BATCH, RW_HEADS, RW_HEAD, RW_HEAD), dtp)
    z_shift = jnp.zeros((DEPTH, BATCH, RW_SHIFT_DIM), dtp)
    y_prompt, (hg_p, ssm_p, conv_p, wkv_p, shift_p) = trunk(
        x_prompt, c_prompt, z_hg, z_ssm, z_conv, z_wkv, z_shift, lb_all, P)
    y_sample, (hg_s, ssm_s, conv_s, wkv_s, shift_s) = trunk(
        x_sample, c_sample, state_hgrn, state_ssm, state_conv, state_wkv, state_shift, lb_all, P)
    return (y_prompt, y_sample, hg_p, hg_s, ssm_p, ssm_s, conv_p, conv_s, wkv_p, wkv_s, shift_p, shift_s)


_drawn_inputs = setup_inputs


def setup_inputs(seed=0):
    import zlib

    import numpy as np

    out = dict(_drawn_inputs(seed))
    spreads = {}
    factors = {'hg_norm_g': 21.568,
     'mb_D': 8.0,
     'mb_norm_g': 8.0,
     'rw_r_k': 5.042,
     'rw_ln_g': 27.024,
     'rw_ln_b': 53.617,
     'g_norm2': 6.784}
    for name, (base, spread) in spreads.items():
        noise = np.random.default_rng([zlib.crc32(name.encode()), seed]).standard_normal(out[name].shape)
        drawn = base * np.exp(spread * noise) if base else spread * noise
        out[name] = __import__('jax').numpy.asarray(drawn.astype(out[name].dtype))
    for name, factor in factors.items():
        out[name] = (out[name] * factor).astype(out[name].dtype)
    return out
```

```python
from contextlib import ExitStack

import concourse.bass as bass
from concourse import mybir

F32 = mybir.dt.float32
F32R = mybir.dt.float32r
I32 = mybir.dt.int32
ALU = mybir.AluOpType
ACT = mybir.ActivationFunctionType
AX = mybir.AxisListType

P = 128
D = 1024
KT = D // P
SEQ = 1024
NS = 8
T = SEQ + NS
NCH = 3
CH = T // NCH
BLK = 128
NB = SEQ // BLK
IN_DIM = 3208
HG0, MZ0, MX0, DT0, RW0 = 0, 1024, 1536, 2304, 2312
RW_DIM = 896
MB_CONV = 4
CONV_DIM = 768
FF = 2816
FT = FF // P
GROUPS = [6, 6, 5, 5]
MAXG = max(GROUPS)
RMS_EPS = 1e-6
GN_EPS = 64e-5
EXP_M05 = 0.6065306597126334
LN2 = 0.6931471805599453
LEVELS = [1, 2, 4, 8, 16, 32]
HLEV = [1, 2, 4, 8, 16]

IN_NAMES = ['x_prompt', 'x_sample', 'state_hgrn', 'state_ssm', 'state_conv', 'state_wkv', 'state_shift', 'c_prompt',
            'c_sample', 'w_ada', 'b_ada', 'g_norm1', 'w_in', 'hg_norm_g', 'mb_conv_w', 'mb_conv_b',
            'mb_dt_bias', 'mb_A_log', 'mb_D', 'mb_norm_g', 'rw_mu', 'rw_w0', 'rw_w2', 'rw_a0', 'rw_a2', 'rw_g2',
            'rw_k_k', 'rw_k_a', 'rw_r_k', 'rw_ln_g', 'rw_ln_b', 'w_out', 'g_norm2', 'w_gate', 'w_up', 'w_down',
            'g_final']
OUT_SHAPES = [(1, SEQ, D), (NS, 1, D), (1, 1, 4, 64, 64), (1, NS, 4, 64, 64), (1, 1, 8, 64, 64), (1, NS, 8, 64, 64),
              (1, 1, 3, CONV_DIM), (1, NS, 3, CONV_DIM), (1, 1, 4, 64, 64), (1, NS, 4, 64, 64), (1, 1, RW_DIM),
              (1, NS, RW_DIM)]

ROWS1 = [('b_ada', 48), ('g_norm1', 8), ('g_norm2', 8), ('g_final', 8), ('mb_conv_w', 24), ('mb_conv_b', 6)]
ROWS2 = [('rw_mu', 7), ('rw_w0', 2), ('rw_a0', 2), ('rw_k_k', 2), ('rw_k_a', 2), ('rw_r_k', 2), ('rw_ln_g', 2),
         ('rw_ln_b', 2), ('hg_norm_g', 2), ('mb_norm_g', 4)]
COL = {}
for _name, _n in ROWS1 + ROWS2:
    COL[_name] = sum(n for _, n in (ROWS1 + ROWS2)[:len(COL)])
NR1 = sum(n for _, n in ROWS1)
NR2 = sum(n for _, n in ROWS2)
COL['mb_D'] = NR1 + NR2

RW_DVE = ['mixed', 'squared', 'clamped', 'decays', 'operands', 'masked', 'inv0', 'inv1', 'inv2', 'inv3', 'inv4', 'inv5',
          'W1', 'U0', 'S0', 'U1', 'S1', 'o', 'centred', 'bonus', 'out']
RW_PE = ['lora', 'ssq', 'turned', 'A', 'N', 'P1', 'XY1', 'P2', 'XY2', 'P3', 'XY3', 'P4', 'XY4', 'P5', 'XY5', 'T1',
         'PT', 'W1', 'U0', 'S0', 'U1', 'S1', 'mean', 'bonus', 'var']
RW_ACT = ['lora_in', 'gates', 'rs', 'exps', 'turned', 'P1', 'P2', 'P3', 'P4', 'P5', 'T1', 'PT', 'var']
HG_DVE = ['nabs', 'logf', 'diffs', 'factors', 'masked', 'att', 'S', 'o', 'squared', 'out']
HG_PE = ['turned', 'att', 'u', 'o', 'ssq']
HG_ACT = ['soft', 'k', 'exps', 'turned', 'v', 'rs']
MB_DVE = ['xdt', 'cb', 'seg', 'm', 'y', 'S', 'z', 'out']
MB_PE = ['turned', 'acum', 'y', 'S', 'ssq']
MB_ACT = ['E2', 'L', 'squared', 'rs']
MB_POOL = ['xdte', 'ce']
PRE_DVE = ['nabs', 'dta', 'es', 'twice']
PRE_ACT = ['aexp', 'soft', 'dtexp', 'ed']
SMP_DVE = ['mixed', 'squared', 'clamped', 'vectors', 'state', 'o', 'centred', 'bonus', 'out']
SMP_PE = ['lora', 'ssq', 'tok', 'oturn', 'mean', 'bonus', 'var']
SMP_ACT = ['lora_in', 'gates', 'rs', 'wexp', 'tok', 'var']
HS_DVE = ['nabs', 'logf', 'state', 'opart', 'osum', 'squared', 'out']
HS_ACT = ['soft', 'vectors', 'tok', 'rs']
MS_DVE = ['y', 'z', 'out']
MS_ACT = ['tok', 'squared', 'rs']
MBV = 1024
RWV = MBV + 768


def step(steps, name, b=0):
    return b * len(steps) + steps.index(name) + 1



def dense_plan():
    ada = [('ada', m) for m in range(48)]
    rw = [('rw', t) for t in range(7)]
    mb = [('z', t) for t in range(4)] + [('xbc', t) for t in range(6)]
    hg = [('hgg', t) for t in range(2)] + [('hg', t) for t in range(6)]
    rest = []
    late = ada[16:]
    for i, u in enumerate(mb + hg):
        rest.append(u)
        rest += [late.pop(0) for _ in range(2) if late]
    units = ada[:16] + rw + rest
    n1 = len(units)
    units += [('out', t) for t in range(8)]
    f = 0
    for g, n in enumerate(GROUPS):
        for i in range(n):
            units += [('gate', f), ('up', f)]
            f += 1
        units += [('down', (g, d)) for d in range(KT)]
    return units, n1


def kernel_program(nc, ins, outs):
    (y_p, y_s, hg_p, hg_s, ssm_p, ssm_s, conv_p, conv_s, wkv_p, wkv_s, shift_p, shift_s) = outs
    (x_prompt, x_sample, state_hgrn, state_ssm, state_conv, state_wkv, state_shift, c_prompt, c_sample, w_ada, b_ada,
     g_norm1, w_in, hg_norm_g, mb_conv_w, mb_conv_b, mb_dt_bias, mb_A_log, mb_D, mb_norm_g, rw_mu, rw_w0, rw_w2, rw_a0,
     rw_a2, rw_g2, rw_k_k, rw_k_a, rw_r_k, rw_ln_g, rw_ln_b, w_out, g_norm2, w_gate, w_up, w_down, g_final) = ins

    def rows(x):
        return x.rearrange("o (a p) -> (o a) p", p=P)

    param_rows = {
        'b_ada': rows(b_ada), 'g_norm1': rows(g_norm1), 'g_norm2': rows(g_norm2),
        'g_final': g_final.rearrange("(a p) -> a p", p=P),
        'mb_conv_w': mb_conv_w.rearrange("o j (a p) -> (o j a) p", p=P), 'mb_conv_b': rows(mb_conv_b),
        'rw_mu': rows(rw_mu), 'rw_w0': rows(rw_w0), 'rw_a0': rows(rw_a0), 'rw_k_k': rows(rw_k_k),
        'rw_k_a': rows(rw_k_a), 'rw_r_k': rw_r_k.rearrange("o (a h) k -> (o a) (h k)", h=2), 'rw_ln_g': rows(rw_ln_g),
        'rw_ln_b': rows(rw_ln_b), 'hg_norm_g': rows(hg_norm_g), 'mb_norm_g': rows(mb_norm_g)}
    UNITS, N1 = dense_plan()
    QUANTA, FIRSTQ, LASTQ = [], {}, {}
    u = 0
    while u < len(UNITS):
        kind = UNITS[u][0]
        FIRSTQ[u] = len(QUANTA)
        if kind == 'ada':
            QUANTA.append((u, 0))
        elif kind == 'gate':
            FIRSTQ[u + 1] = len(QUANTA) + 1
            for c in range(NCH):
                QUANTA += [(u, c), (u + 1, c)]
            LASTQ[u] = len(QUANTA) - 2
            LASTQ[u + 1] = len(QUANTA) - 1
            u += 2
            continue
        else:
            QUANTA += [(u, c) for c in range(NCH)]
        LASTQ[u] = len(QUANTA) - 1
        u += 1
    SPLIT = [u for u, (k, _) in enumerate(UNITS) if k != 'ada']
    SIDX = {u: i for i, u in enumerate(SPLIT)}
    QP1 = LASTQ[N1 - 1] + 1
    NRAW, NSPL1, NSPL3 = 3, 2, 4

    def spl_slots(i):
        return NSPL1 if SPLIT[i] < N1 else NSPL3

    BANK, PREV = [], []
    last_use = {}
    for q, (u, c) in enumerate(QUANTA):
        b = q % 3 if q < QP1 else q % 7
        BANK.append(b)
        PREV.append(last_use.get(b))
        last_use[b] = q

    def evac_engine(q):
        kind = UNITS[QUANTA[q][0]][0]
        return 'dve' if kind in ('out', 'up', 'down') else 'act'

    EV = {'act': [], 'dve': []}
    for q in range(len(QUANTA)):
        EV[evac_engine(q)].append(q)
    EVN = {q: i + 1 for e in EV for i, q in enumerate(EV[e])}
    GATES = [q for q, (u, _) in enumerate(QUANTA) if UNITS[u][0] == 'gate']
    UPS = [q for q, (u, _) in enumerate(QUANTA) if UNITS[u][0] == 'up']
    STAGED = [q for q, (u, _) in enumerate(QUANTA) if UNITS[u][0] in ('xbc', 'hg')]
    TILE_IN_GROUP = [i for n in GROUPS for i in range(n)]

    ctx = ExitStack()
    with ctx:
        def sem(name):
            return ctx.enter_context(nc.semaphore(name))

        lo = nc.sbuf_base
        hi = nc.sbuf_usable_end

        class Region:

            def __init__(self, base, limit):
                self.at, self.limit = -(-base // 64) * 64, limit

            def t(self, name, shape, dtype=F32):
                n = 4
                for s in shape[1:]:
                    n *= s
                self.at = -(-self.at // 32) * 32
                out = nc.alloc_sbuf_tensor_at(name, shape, dtype, offset=self.at)
                self.at += n
                assert self.at <= self.limit, (name, self.at, self.limit)
                return out

        keep = Region(lo, hi)
        ident = keep.t("ident", [P, P])
        ones = keep.t("ones", [P, P])
        headsum = keep.t("headsum", [P, P])
        triu = keep.t("triu", [P, P])
        PAR = keep.t("PAR", [P, NR1 + NR2 + 4])
        CST = keep.t("CST", [P, 4])
        MOD = keep.t("MOD", [P, 48, 9])
        A1 = keep.t("A1", [P, KT, 9])
        CT = keep.t("CT", [P, KT, 9])
        DTZ = keep.t("DTZ", [P, 9, 8])
        HMK = keep.t("HMK", [P, 6, 32])
        CM32 = keep.t("CM32", [P, BLK])
        G4 = keep.t("G4", [P, 32])
        WDT = [keep.t("WDTH", [P, KT, 8], F32R), keep.t("WDTL", [P, KT, 8], F32R)]
        RAW = [keep.t(f"RAW{i}", [P, KT, P]) for i in range(NRAW)]
        TMP8 = keep.t("TMP8", [P, NS])
        h_at = keep.at
        hreg = Region(h_at, hi)
        HHI = hreg.t("HHI", [P, KT, T], F32R)
        HLO = hreg.t("HLO", [P, KT, T], F32R)
        h_end = hreg.at
        p1 = Region(h_end, hi)
        WHI1 = [p1.t(f"WHI1_{i}", [P, KT, P], F32R) for i in range(NSPL1)]
        WLO1 = [p1.t(f"WLO1_{i}", [P, KT, P], F32R) for i in range(NSPL1)]
        MIX = p1.t("MIX", [P, KT, T])
        mix_end = p1.at
        p0 = Region(mix_end, hi)
        XT0 = p0.t("XT0", [P, KT, T])
        XTOK = [p0.t(f"XTOK_{i}", [P, D]) for i in range(2)]
        PV = p0.t("PV", [P, 2, P])
        BIG = p0.t("BIG", [P, P])
        DHEAD = p0.t("DHEAD", [P, 8])
        WDR = p0.t("WDR", [P, KT, 8])
        p0b = Region(mix_end - 4 * KT * T, mix_end)
        H32 = p0b.t("H32", [P, KT, CH])
        SQ = p0b.t("SQ", [P, KT, CH])
        SS = p0b.t("SS", [P, CH])
        RB = p0b.t("RB", [P, CH])
        C9 = p0b.t("C9", [9, 2, D])
        mx_at = p1.at
        MX = p1.t("MX", [P, 7, BLK])
        LA = p1.t("LA", [P, BLK])
        SG = p1.t("SG", [P, 4, BLK])
        GT = p1.t("GT", [P, 2, BLK])
        KK = p1.t("KK", [P, 2, BLK])
        T2 = p1.t("T2", [P, 2, BLK])
        RS = p1.t("RS", [P, 2, BLK])
        BB = p1.t("BB", [P, 2, BLK])
        BM = p1.t("BM", [P, 2, BLK])
        EB = p1.t("EB", [P, 2, BLK])
        ENB = p1.t("ENB", [P, 2, BLK])
        KP = p1.t("KP", [P, 2, BLK])
        OS = BB
        PR = p1.t("PR", [P, 7, T + 1])
        AR = p1.t("AR", [P, 4, 2, 64])
        BK = p1.t("BK", [P, 4, 2, 64])
        vz_at = p1.at
        VZ = p1.t("VZ", [P, 4, 2, 64])
        ar_at = p1.at
        ARt = p1.t("ARt", [P, 4, P])
        BKt = p1.t("BKt", [P, 4, P])
        UV = p1.t("UV", [P, 4, P])
        AM = p1.t("AM", [P, 2, 4, P])
        X = p1.t("X", [P, 4, 64])
        Y = p1.t("Y", [P, 4, 64])
        PS = p1.t("PS", [P, 4, 64])
        W1S = p1.t("W1S", [P, 4, 64])
        ar_end = p1.at
        T1S, PTS = PS, X
        ST = p1.t("ST", [P, 2, 64])
        RWM = p1.t("RWM", [P, 2, P])
        LM = p1.t("LM", [P, 6, 2, 64], mybir.dt.int8)
        I4 = p1.t("I4", [P, 64])
        CM64 = p1.t("CM64", [P, BLK])
        WL = p1.t("WL", [P, 256])
        SHF = p1.t("SHF", [P, 7, NS])
        SCV = p1.t("SCV", [P, 6, 24])
        OMKA = p1.t("OMKA", [P, 2])
        XL = p1.t("XL", [P, 6, 11])
        STG = [p1.t(f"STG{i}", [P, 3 + CH]) for i in range(2)]
        ACC = [p1.t(f"ACC{i}", [P, CH]) for i in range(1)]
        SGC = p1.t("SGC", [P, CH])
        sreg = Region(ar_at, ar_end)
        SCT = Region(ar_at, ar_end).t("SCT", [3 * NS, CONV_DIM])
        SHT = Region(ar_at + 4 * CONV_DIM, ar_end).t("SHT", [NS, RW_DIM])
        STKW = sreg.t("STKW", [NS, 6 * 256])
        SWK = sreg.t("SWK", [P, 1024])
        SW1 = sreg.t("SW1", [P, 1024])
        SWV = Region(vz_at, ar_at).t("SWV", [P, 336])
        fin = Region(mx_at, vz_at)
        FST = fin.t("FST", [64, 2, P])
        FSH = fin.t("FSH", [9, RW_DIM])
        FCV = fin.t("FCV", [11, CONV_DIM])
        r2 = Region(h_at, h_end)
        HB = r2.t("HB", [P, 6, BLK])
        HN = r2.t("HN", [P, 2, BLK])
        HE = r2.t("HE", [P, 2, BLK])
        HL = r2.t("HL", [P, 2, BLK])
        HF = r2.t("HF", [P, 2, BLK])
        HK = r2.t("HK", [P, 2, BLK])
        HBb = r2.t("HBb", [P, 2, BLK])
        HD = r2.t("HD", [P, 6, 2, BLK])
        HX = r2.t("HX", [P, 2, BLK])
        HQ = r2.t("HQ", [P, 2, BLK])
        HVT = r2.t("HVT", [P, 2, BLK])
        HKT = r2.t("HKT", [P, 2, BLK])
        HAS = r2.t("HAS", [P, 2, 6, 2, 32])
        HAT = r2.t("HAT", [P, 4, 32])
        HAD = r2.t("HAD", [P, 4, BLK])
        HVD = r2.t("HVD", [P, 2, 4, BLK])
        HSH = r2.t("HSH", [P, 5, 2, 64])
        HO = r2.t("HO", [P, 2, BLK])
        HT = r2.t("HT", [P, 2, BLK])
        HR = r2.t("HR", [P, 2, BLK])
        XB = r2.t("XB", [P, 6, BLK])
        XD = r2.t("XD", [P, 8, 64])
        XDE = r2.t("XDE", [P, 8, 64])
        BT = r2.t("BT", [P, P])
        CBM = r2.t("CBM", [P, 2, P])
        SEG = r2.t("SEG", [P, 8, P])
        MM = r2.t("MM", [P, 8, P])
        E2 = r2.t("E2", [P, 4, P])
        CE = r2.t("CE", [P, 4, P])
        STt = r2.t("STt", [P, 4, 64])
        YS = r2.t("YS", [P, 4, BLK])
        T4 = r2.t("T4", [P, 4, BLK])
        RM = r2.t("RM", [P, 2, BLK])
        DT = r2.t("DT", [P, 9, 8])
        DTA = r2.t("DTA", [P, 9, 8])
        DTN = r2.t("DTN", [P, 9, 8])
        DTE = r2.t("DTE", [P, 9, 8])
        ACOL = r2.t("ACOL", [P, 8, 8])
        ES = r2.t("ES", [P, 8, 8])
        ED = r2.t("ED", [P, 8, 8])
        EDG = r2.t("EDG", [P, 8, 4])
        DTW = r2.t("DTW", [P, 2, 8, 2])
        DTB = r2.t("DTB", [P, 8])
        AEX = r2.t("AEX", [P, 8])
        r2b = Region(mix_end, hi)
        XT = r2b.t("XT", [P, KT, T])
        XTOK2 = [r2b.t(f"XTOK2_{i}", [P, D]) for i in range(2)]
        STK = r2b.t("STK", [NS, 1024])
        SHG = r2b.t("SHG", [P, 1024])
        SHT2 = r2b.t("SHT2", [P, 1024])
        SSM = r2b.t("SSM", [P, 2048])
        SMT = r2b.t("SMT", [P, 2048])
        SV1 = r2b.t("SV1", [P, 128])
        SV2 = r2b.t("SV2", [P, 192])
        SO = r2b.t("SO", [P, 64])
        SO2 = r2b.t("SO2", [32, 64])
        STF = r2b.t("STF", [P, 2, P])
        STOKEN = r2b.t("STOKEN", [NS, 768])
        r3 = Region(h_at, h_end)
        MHI = r3.t("MHI", [P, KT, T], F32R)
        MLO = r3.t("MLO", [P, KT, T], F32R)
        r3c = Region(h_at, h_end)
        H2I = r3c.t("H2I", [P, KT, T], F32R)
        H2L = r3c.t("H2L", [P, KT, T], F32R)
        xt_end = Region(mix_end, hi).at + 4 * KT * T
        r3b = Region(xt_end, hi)
        WHI3 = WHI1 + [r3b.t(f"WHI3_{i}", [P, KT, P], F32R) for i in range(NSPL3 - NSPL1)]
        WLO3 = WLO1 + [r3b.t(f"WLO3_{i}", [P, KT, P], F32R) for i in range(NSPL3 - NSPL1)]
        r3d = Region(h_end + 4 * 2 * NSPL1 * KT * P, xt_end - 4 * KT * T)
        GHI = r3d.t("GHI", [P, MAXG, T], F32R)
        SS2 = r3d.t("SS2", [P, CH])
        RB2 = r3d.t("RB2", [P, CH])
        SGF = [r3d.t(f"SGF{i}", [P, CH]) for i in range(2)]
        GU = [r3d.t(f"GU{i}", [P, CH]) for i in range(2)]
        GLO = r3b.t("GLO", [P, MAXG, T], F32R)
        r3e = Region(h_end + 4 * 2 * NSPL1 * KT * P, xt_end - 4 * KT * T)
        SQ2 = r3e.t("SQ2", [P, KT, CH])
        H322 = r3e.t("H322", [P, KT, CH])
        r3f = Region(h_at, h_end)
        SQ3 = r3f.t("SQ3", [P, KT, CH])
        SS3 = r3f.t("SS3", [P, CH])
        RB3 = r3f.t("RB3", [P, CH])
        OT = [r3f.t(f"OT{i}", [P, D]) for i in range(2)]
        stok = nc.dram_tensor("stok", (NS, 3328), F32, kind="Internal").ap()
        osc = nc.dram_tensor("osc", (NS, D), F32, kind="Internal").ap()
        dts = nc.dram_tensor("dts", (2, NS, 16), F32, kind="Internal").ap()
        hgd = nc.dram_tensor("hgd", (6, P, T), F32, kind="Internal").ap()
        xbd = nc.dram_tensor("xbd", (6, P, T), F32, kind="Internal").ap()
        BK8 = [ctx.enter_context(nc.psum_tensor(f"bank{i}", [P, 512], F32)) for i in range(8)]

        def par(name, j=0, n=1):
            return PAR[:, COL[name] + j:COL[name] + j + n]

        c_loaded = sem("c_loaded")
        par_loaded = sem("par_loaded")
        consts_built = sem("consts_built")
        c_act = sem("c_act")
        c_turned = sem("c_turned")
        par_turned = sem("par_turned")
        par_ready = sem("par_ready")
        raw_loaded = [sem(f"raw_loaded{i}") for i in range(NRAW)]
        w_hi = sem("w_hi")
        w_lo = sem("w_lo")
        dense_done = sem("dense_done")
        evac = {'act': sem("evac_act"), 'dve': sem("evac_dve")}
        x_loaded = [sem(f"x_loaded{i}") for i in range(2)]
        x_turned = sem("x_turned")
        x_act = sem("x_act")
        x_dve = sem("x_dve")
        n_sq = sem("n_sq")
        n_sum = sem("n_sum")
        n_tot = sem("n_tot")
        n_rs = sem("n_rs")
        n_h = sem("n_h")
        n_hi = sem("n_hi")
        n_lo = sem("n_lo")
        phase = sem("phase")
        st_loaded = sem("st_loaded")
        init_pool = sem("init_pool")
        st_turned = sem("st_turned")
        init_dve = sem("init_dve")
        dt_done = sem("dt_done")
        staged = sem("staged")
        conv_done = sem("conv_done")
        stg_out = [sem(f"stg_out{i}") for i in range(2)]
        acc_out = sem("acc_out")
        rw_dve = sem("rw_dve")
        rw_pe = sem("rw_pe")
        rw_act = sem("rw_act")
        smp_dve = sem("smp_dve")
        smp_pe = sem("smp_pe")
        smp_act = sem("smp_act")
        smp_dma = sem("smp_dma")
        out_dma = sem("out_dma")
        fin_pe = sem("fin_pe")
        fin_dve = sem("fin_dve")
        hg_dve = sem("hg_dve")
        hg_pe = sem("hg_pe")
        hg_act = sem("hg_act")
        hg_loaded = sem("hg_loaded")
        mb_dve = sem("mb_dve")
        mb_pe = sem("mb_pe")
        mb_act = sem("mb_act")
        mb_pool = sem("mb_pool")
        mb_loaded = sem("mb_loaded")
        mb_silu = sem("mb_silu")
        hs_dve = sem("hs_dve")
        hs_pe = sem("hs_pe")
        hs_act = sem("hs_act")
        hs_dma = sem("hs_dma")
        ms_dve = sem("ms_dve")
        ms_pe = sem("ms_pe")
        ms_act = sem("ms_act")
        ms_dma = sem("ms_dma")
        pre_dve = sem("pre_dve")
        pre_pe = sem("pre_pe")
        pre_act = sem("pre_act")
        pre_dma = sem("pre_dma")
        mix_hi = sem("mix_hi")
        mix_lo = sem("mix_lo")
        gu_hi = sem("gu_hi")
        gu_lo = sem("gu_lo")
        y_scaled = sem("y_scaled")
        y_turned = sem("y_turned")
        y_act = sem("y_act")
        y_dve = sem("y_dve")
        y_out = [sem(f"y_out{i}") for i in range(2)]
        wdt_loaded = sem("wdt_loaded")
        dhead_loaded = sem("dhead_loaded")
        ident_built = sem("ident_built")
        c_sig = sem("c_sig")
        wdt_hi = sem("wdt_hi")
        dt_split = sem("dt_split")
        smp_dma2 = sem("smp_dma2")
        smp_dma3 = sem("smp_dma3")
        smp_dma4 = sem("smp_dma4")
        hs_dma2 = sem("hs_dma2")
        hs_dma3 = sem("hs_dma3")
        ms_dma2 = sem("ms_dma2")
        ms_dma3 = sem("ms_dma3")
        silu_s = sem("silu_s")
        silu_m = sem("silu_m")
        mb_sig = sem("mb_sig")
        pre_pool = sem("pre_pool")
        act_own = sem("act_own")
        dve_own = sem("dve_own")
        pool_own = sem("pool_own")

        def linker(eng, own):
            count = [0]

            def link(ins):
                count[0] += 1
                ins.then_inc(own, 1)
                eng.wait_ge(own, count[0])
            return link

        def end_phase(eng, k, wait=True):
            eng.drain().then_inc(phase, 1)
            if wait:
                eng.wait_ge(phase, 4 * (k + 1))

        def smp(engine):
            counter, steps = {'dve': (smp_dve, SMP_DVE), 'pe': (smp_pe, SMP_PE), 'act': (smp_act, SMP_ACT)}[engine]

            def at(name):
                return counter, steps.index(name) + 1
            return at

        def XUSE(i):
            return i // 2 + 1

        def weight_view(u):
            kind, i = UNITS[u]
            if kind == 'down':
                g, d = i
                r0 = sum(GROUPS[:g]) * P
                src = w_down[0, r0:r0 + GROUPS[g] * P, d * P:(d + 1) * P]
            else:
                w, c0 = {'ada': (w_ada, 0), 'rw': (w_in, RW0), 'z': (w_in, MZ0), 'xbc': (w_in, MX0),
                         'hgg': (w_in, HG0 + 768), 'hg': (w_in, HG0), 'out': (w_out, 0), 'gate': (w_gate, 0),
                         'up': (w_up, 0)}[kind]
                src = w[0, :, c0 + i * P:c0 + (i + 1) * P]
            return src.rearrange("(k p) n -> p k n", p=P)

        def unit_k(u):
            kind, i = UNITS[u]
            return GROUPS[i[0]] if kind == 'down' else KT

        SLOT, SPREV = [], []
        slot_user = {}
        n1s = sum(1 for u in SPLIT if u < N1)
        for i, u in enumerate(SPLIT):
            s = i % NSPL1 if i < n1s else (i - n1s) % NSPL3
            SLOT.append(s)
            SPREV.append(slot_user.get(s))
            slot_user[s] = i

        def w_split(i):
            hi_, lo_ = (WHI1, WLO1) if i < n1s else (WHI3, WLO3)
            return hi_[SLOT[i]], lo_[SLOT[i]]

        RW_STAGES = ['mix', 'lora', 'gate', 'decay', 'turn', 'inv1', 'inv2', 'inv3', 'inv4', 'inv5', 'fold', 'seq0',
                     'seq1', 'post']
        plan0 = [('mm', q) for q in range(16)]
        PLAN1 = []
        q = 16
        pend = []
        first_rw_q = 16
        splits_at = {}
        for i, u in enumerate(SPLIT):
            if i == 0:
                continue
            j = i - 1
            if UNITS[u][0] == 'up':
                j = i - 2
            elif UNITS[u][0] == 'gate' and UNITS[SPLIT[i - 1]][0] == 'up':
                j = i - 2
            elif UNITS[u][0] == 'down' and UNITS[SPLIT[i - 1]][0] == 'up':
                j = i - 1
            splits_at.setdefault(FIRSTQ[SPLIT[j]], []).append(i)

        def dense_items(q0, q1, lag_tail=True):
            items = []
            for q in range(q0, q1):
                items += [('split', i) for i in splits_at.get(q, []) if not (SPLIT[i] >= N1 > UNITS_OF(q))]
                items.append(('mm', q))
                if q > q0:
                    items.append(('ev', q - 1))
            if lag_tail and q1 > q0:
                items.append(('ev', q1 - 1))
            return items

        def UNITS_OF(q):
            return QUANTA[q][0]

        q_rw_end = LASTQ[16 + 6] + 1
        PLAN1 += dense_items(16, q_rw_end)
        PLAN1.append(('dt', 0))
        left = list(range(q_rw_end, QP1))
        rw_list = [('rw_' + s, b) for b in range(NB) for s in RW_STAGES]
        per = len(left) / (len(rw_list) - 10)
        due, k = 0.0, 0
        prev_q = None
        for item in rw_list:
            PLAN1.append(item)
            due += per
            while k < len(left) and k < due:
                q = left[k]
                PLAN1 += [('split', i) for i in splits_at.get(q, []) if SPLIT[i] < N1]
                PLAN1.append(('mm', q))
                if prev_q is not None:
                    PLAN1.append(('ev', prev_q))
                prev_q = q
                k += 1
        assert k == len(left)
        PLAN1.append(('ev', prev_q))
        PLAN1 += [('rws', s) for s in range(4)]
        PLAN1.append(('rw_final', 0))

        HG_STAGES = ['gate', 'levels', 'att', 'state', 'post']
        MB_STAGES = ['turn', 'decay', 'prod', 'post']
        PLAN2 = [('pre', 0)]
        for b in range(NB):
            PLAN2 += [('hg_gate', b), ('mb_turn', b), ('hg_levels', b), ('mb_decay', b), ('hg_att', b), ('hg_state', b),
                      ('mb_prod', b), ('hg_post', b), ('mb_post', b)]
        PLAN2 += [('hgs', 0), ('mbs', 0), ('mix_final', 0)]

        PLAN3 = [('split', i) for i, u in enumerate(SPLIT)
                 if u >= N1 and any(i in splits_at[q] for q in splits_at if q < QP1)]
        PLAN3 += [('mixsplit', c) for c in range(NCH)]
        q_out_end = LASTQ[N1 + 7] + 1
        for q0, q1, norm0 in ((QP1, q_out_end, 3), (q_out_end, len(QUANTA), 6)):
            for item in dense_items(q0, q1):
                PLAN3.append(item)
                if item[0] == 'ev' and item[1] >= q1 - NCH:
                    PLAN3.append(('norm', norm0 + item[1] - (q1 - NCH)))

        block = ctx.enter_context(nc.Block())

        @block.sync
        def _(sp):
            sp.dma_start(C9[0:1, 0, :], c_prompt).then_inc(c_loaded, 16)
            sp.dma_start(C9[1:9, 0, :], c_sample).then_inc(c_loaded, 16)
            for name, n in ROWS1 + ROWS2:
                half = 0 if COL[name] < NR1 else 1
                r = COL[name] - half * NR1
                dst = PV[r:r + n, half, :]
                sp.dma_start(dst, param_rows[name]).then_inc(par_loaded, 16)
            sp.dma_start(DHEAD[:, :], mb_D.broadcast_to([P, 8])).then_inc(dhead_loaded, 16)
            sp.dma_start(WDR[:, :, :], w_in[0, :, DT0:DT0 + 8].rearrange("(k p) n -> p k n", p=P)).then_inc(
                wdt_loaded, 16)
            for u in range(len(UNITS)):
                if u >= NRAW:
                    if UNITS[u - NRAW][0] == 'ada':
                        sp.wait_ge(dense_done, LASTQ[u - NRAW] + 1)
                    else:
                        sp.wait_ge(w_lo, SIDX[u - NRAW] + 1)
                sp.dma_start(RAW[u % NRAW][:, 0:unit_k(u), :], weight_view(u)).then_inc(raw_loaded[u % NRAW], 16)

        @block.gpsimd
        def _(pool):
            g = nc.gpsimd
            link = linker(pool, pool_own)

            def load_x(i, bufs):
                if i >= 2:
                    pool.wait_ge(x_turned, i - 1)
                dst = bufs[i % 2]
                if i % 9 < NB:
                    pool.dma_start(dst[:, :], x_prompt[0, (i % 9) * BLK:(i % 9 + 1) * BLK, :]).then_inc(
                        x_loaded[i % 2], 16)
                else:
                    pool.dma_start(dst[0:NS, :], x_sample[:, 0, :]).then_inc(x_loaded[i % 2], 16)

            def keep_where(t, base, pattern, cm, n=P):
                link(g.affine_select(out=t, in_=t, pattern=pattern, compare_op=ALU.is_ge, fill=0.0, base=base,
                                     channel_multiplier=cm))

            load_x(0, XTOK)
            load_x(1, XTOK)
            link(g.memset(ident[:, :], 0.0))
            g.affine_select(out=ident[:, :], in_=ident[:, :], pattern=[[-1, P]], compare_op=ALU.not_equal, fill=1.0,
                            base=0, channel_multiplier=1).then_inc(ident_built, 1)
            pool.wait_ge(ident_built, 1)
            link(g.memset(ones[:, :], 1.0))
            link(g.memset(triu[:, :], 1.0))
            keep_where(triu[:, :], 0, [[1, P]], -1)
            link(g.memset(headsum[:, :], 0.0))
            link(g.memset(headsum[0:64, 0:64], 1.0))
            link(g.memset(headsum[64:P, 64:P], 1.0))
            for c, v in enumerate((GN_EPS, 15 * LN2, RMS_EPS, 1.0)):
                link(g.memset(CST[:, c:c + 1], v))
            link(g.memset(CM32[:, :], 1.0))
            link(g.memset(CM32[:, 0:BLK:32], 0.0))
            link(g.memset(G4[:, :], 1.0))
            keep_where(G4[:, :], 0, [[-4, 32]], 1)
            keep_where(G4[:, :], 3, [[4, 32]], -1)
            for lv, n in enumerate(HLEV):
                link(g.memset(BIG[:, :], 1.0))
                keep_where(BIG[:, :], 0, [[-2 * n, P // (2 * n)], [0, 2 * n]], 1)
                keep_where(BIG[:, :], n - 1, [[2 * n, P // (2 * n)], [0, 2 * n]], -1)
                link(g.memset(BIG[:, :].rearrange("p (b e r) -> p b e r", e=2, r=n)[:, :, 0, :], 0.0))
                for s in range(4):
                    link(g.tensor_copy(HMK[32 * s:32 * s + 32, lv, :], BIG[32 * s:32 * s + 32, 32 * s:32 * s + 32]))
            for s in range(3):
                link(g.tensor_copy(HMK[32 * s:32 * s + 32, 5, :], ident[32 * s:32 * s + 32, 32 * s:32 * s + 32]))
            g.tensor_copy(HMK[96:P, 5, :], ident[96:P, 96:P]).then_inc(consts_built, 1)
            for i in range(2, 9):
                load_x(i, XTOK)
            end_phase(pool, 0)

            pool.dma_start(SCT[:, :], state_conv[0].rearrange("b j c -> (b j) c")).then_inc(st_loaded, 16)
            pool.dma_start(SHT[:, :], state_shift[0]).then_inc(st_loaded, 16)
            pool.dma_start(WL[0:32, :], rw_w2[0]).then_inc(st_loaded, 16)
            pool.dma_start(WL[32:64, :], rw_a2[0]).then_inc(st_loaded, 16)
            pool.dma_start(WL[64:P, :], rw_g2[0]).then_inc(st_loaded, 16)
            link(g.memset(PR[:, :, 0:1], 0.0))
            link(g.memset(VZ[:, :, :, :], 0.0))
            link(g.memset(ST[:, :, :], 0.0))
            link(g.memset(CM64[:, :], 1.0))
            link(g.memset(CM64[:, 0:BLK:64], 0.0))
            for hp in range(2):
                r = slice(64 * hp, 64 * hp + 64)
                link(g.tensor_copy(I4[r, :], ident[r, r]))
                for own in range(2):
                    o = slice(64 * own, 64 * own + 64)
                    link(g.tensor_copy(RWM[o, hp, 64 * (1 - hp):64 * (1 - hp) + 64], triu[o, o]))
                    link(g.tensor_tensor(RWM[o, hp, 64 * hp:64 * hp + 64], triu[o, o], ident[o, o], ALU.subtract))
            MW = SGC[:, 0:P]
            for lv, n in enumerate(LEVELS):
                for turned in range(2):
                    link(g.memset(MW, 1.0))
                    keep_where(MW, 0 if turned else -n, [[-2 * n, P // (2 * n)], [0, 2 * n]], 1)
                    keep_where(MW, n - 1 if turned else 2 * n - 1, [[2 * n, P // (2 * n)], [0, 2 * n]], -1)
                    link(g.memset(MW.rearrange("p (b e r) -> p b e r", e=2, r=n)[:, :, 1 - turned, :], 0.0))
                    for hp in range(2):
                        r = slice(64 * hp, 64 * hp + 64)
                        link(g.tensor_copy(LM[r, lv, turned, :], MW[r, 64 * hp:64 * hp + 64]))
            g.memset(SGC[:, 0:1], 0.0).then_inc(init_pool, 1)

            def stage_out(q):
                u, c = QUANTA[q]
                kind, t = UNITS[u]
                if kind not in ('hg', 'xbc'):
                    return
                r = STAGED.index(q)
                cols = slice(c * CH, (c + 1) * CH)
                if kind == 'hg':
                    pool.wait_ge(evac['act'], EVN[q])
                    pool.dma_start(hgd[t, :, cols], STG[r % 2][:, 3:3 + CH]).then_inc(stg_out[r % 2], 16)
                else:
                    pool.wait_ge(conv_done, r + 1)
                    pool.dma_start(xbd[t, :, cols], ACC[0][:, :]).then_inc(acc_out, 16)

            def rws(s):
                D_, T_, A_ = smp('dve'), smp('pe'), smp('act')
                if s == 1:
                    pool.wait_ge(*A_('tok'))
                    for v in range(5):
                        pool.dma_start(
                            stok[:, RWV:RWV + 1280].rearrange("b (h v k) -> b h v k", h=4, v=5)[:, :, v, :],
                            STKW[:, v * 256:(v + 1) * 256].rearrange("b (h k) -> b h k", h=4)).then_inc(smp_dma, 16)
                    pool.dma_start(stok[:, RWV + 1280:RWV + 1536], STKW[:, 1280:1536]).then_inc(smp_dma, 16)
                    pool.dma_start(SWK[:, :], state_wkv[0].rearrange("b h (r v) k -> (b h r) (v k)", r=4)).then_inc(
                        smp_dma, 16)
                    pool.wait_ge(smp_dma, 7 * 16)
                    for b in range(NS):
                        pool.dma_start(
                            SWV[16 * b:16 * b + 16, 0:320],
                            stok[b, RWV:RWV + 1280].rearrange("(h x) -> h x", h=4).unsqueeze(1).broadcast_to(
                                [4, 4, 320])).then_inc(smp_dma2, 16)
                    pool.dma_start(SWV[:, 320:336],
                                   stok[:, RWV + 1280:RWV + 1536].rearrange("b (x v) -> b x v", v=16)).then_inc(
                                       smp_dma2, 16)
                if s == 2:
                    pool.wait_ge(*D_('state'))
                    pool.dma_start(wkv_s[0].rearrange("b h (r v) k -> (b h r) (v k)", r=4), SWK[:, :]).then_inc(
                        out_dma, 16)
                    pool.dma_start(osc[:, 768:1024].rearrange("b (x v) -> b x v", v=16), SWV[:, 0:16]).then_inc(
                        smp_dma3, 16)
                    pool.wait_ge(smp_dma3, 16)
                    pool.dma_start(STKW[:, 0:256], osc[:, 768:1024]).then_inc(smp_dma4, 16)

            def rw_final(_):
                pool.wait_ge(fin_dve, 1)
                pool.dma_start(wkv_p[0, 0].rearrange("(j h) v k -> v j h k", h=2),
                               FST[:, :, :].rearrange("v j (h k) -> v j h k", h=2)).then_inc(out_dma, 16)
                pool.dma_start(shift_p[0], FSH[0:1, :]).then_inc(out_dma, 16)
                pool.dma_start(shift_s[0], FSH[1:9, :]).then_inc(out_dma, 16)
                pool.dma_start(conv_p[0, 0], FCV[0:3, :]).then_inc(out_dma, 16)
                pool.dma_start(conv_s[0, :, 2, :], FCV[3:11, :]).then_inc(out_dma, 16)
                pool.dma_start(conv_s[0, :, 0:2, :], state_conv[0, :, 1:3, :]).then_inc(out_dma, 16)

            for what, arg in PLAN1:
                if what == 'ev':
                    stage_out(arg)
                elif what == 'rws':
                    rws(arg)
                elif what == 'rw_final':
                    rw_final(arg)
            pool.wait_ge(out_dma, 7 * 16)
            pool.wait_ge(acc_out, 16 * 18)
            for s in range(2):
                pool.wait_ge(stg_out[s], 16 * 9)
            end_phase(pool, 1)

            pool.dma_start(DTB[:, :], mb_dt_bias.broadcast_to([P, 8])).then_inc(pre_dma, 16)
            pool.dma_start(AEX[:, :], mb_A_log.broadcast_to([P, 8])).then_inc(pre_dma, 16)

            def load_hg(b):
                w = BLK if b < NB else NS
                if b:
                    pool.wait_ge(hg_dve, step(HG_DVE, 'out', b - 1))
                pool.dma_start(HB[:, :, 0:w], hgd[:, :, b * BLK:b * BLK + w].rearrange("t p c -> p t c")).then_inc(
                    hg_loaded, 16)

            def load_mb(b):
                w = BLK if b < NB else NS
                if b:
                    pool.wait_ge(mb_dve, step(MB_DVE, 'out', b - 1))
                pool.dma_start(XB[:, :, 0:w], xbd[:, :, b * BLK:b * BLK + w].rearrange("t p c -> p t c")).then_inc(
                    mb_loaded, 16)

            def mb_decay(b):
                pool.wait_ge(mb_dve, step(MB_DVE, 'xdt', b))
                g.tensor_tensor(XDE[:, :, :], XD[:, :, :], ES[:, b, :].unsqueeze(2).broadcast_to([P, 8, 64]),
                                ALU.mult).then_inc(mb_pool, 1)
                pool.wait_ge(mb_act, step(MB_ACT, 'E2', b))
                g.tensor_tensor(CE[:, :, :], E2[:, :, :], XB[:, 5, :].unsqueeze(1).broadcast_to([P, 4, P]),
                                ALU.mult).then_inc(mb_pool, 1)

            load_hg(0)
            load_mb(0)
            link(g.memset(HSH[:, :, :, :], 0.0))
            link(g.memset(HAD[:, :, :], 0.0))
            link(g.memset(HVD[:, :, :, :], 0.0))
            g.memset(STt[:, :, :], 0.0).then_inc(pre_pool, 1)
            load_x(9, XTOK2)
            load_x(10, XTOK2)
            for what, arg in PLAN2:
                if what == 'mb_decay':
                    mb_decay(arg)
                elif what == 'hg_post':
                    load_hg(arg + 1)
                    if arg >= 2:
                        load_x(9 + arg, XTOK2)
                elif what == 'mb_post':
                    load_mb(arg + 1)
                elif what == 'hgs':
                    load_x(9 + 8, XTOK2)
                    pool.dma_start(SHG[:, :], state_hgrn[0].rearrange("b h (r k) v -> (b h r) (k v)", r=4)).then_inc(
                        hs_dma, 16)
                    pool.wait_ge(hs_act, 3)
                    pool.dma_start(stok[:, 0:1024], STK[:, :]).then_inc(hs_dma, 16)
                    pool.wait_ge(hs_dma, 32)
                    for v in range(3):
                        pool.dma_start(SV1[:, v * 16:v * 16 + 16],
                                       stok[:, v * 256:v * 256 + 256].rearrange("b (x k) -> b x k", k=16)).then_inc(
                                           hs_dma2, 16)
                    for b in range(NS):
                        pool.dma_start(SV1[16 * b:16 * b + 16, 64:128],
                                       stok[b, 768:1024].rearrange("(h v) -> h v", h=4).unsqueeze(1).broadcast_to(
                                           [4, 4, 64])).then_inc(hs_dma2, 16)
                    pool.wait_ge(hs_dve, HS_DVE.index('state') + 1)
                    pool.dma_start(hg_s[0].rearrange("b h (r k) v -> (b h r) (k v)", r=4), SHG[:, :]).then_inc(
                        out_dma, 16)
                    pool.wait_ge(hs_dve, HS_DVE.index('osum') + 1)
                    pool.dma_start(osc[:, 0:256].rearrange("b (h v) -> b h v", h=4), SO2[:, :]).then_inc(hs_dma3, 16)
                    pool.wait_ge(hs_dma3, 16)
                    pool.dma_start(STK[:, 0:256], osc[:, 0:256]).then_inc(hs_dma3, 16)
                elif what == 'mbs':
                    pool.dma_start(SSM[:, :], state_ssm[0].rearrange("b h (r p) n -> (b h r) (p n)", r=2)).then_inc(
                        ms_dma, 16)
                    pool.wait_ge(ms_act, 1)
                    pool.wait_ge(pre_dve, PRE_DVE.index('twice') + 1)
                    for v in range(2):
                        pool.dma_start(dts[v], DTW[P - NS:P, v, :, :].rearrange("b h r -> b (h r)")).then_inc(ms_dma, 16)
                    pool.dma_start(stok[:, MBV:MBV + 512], STOKEN[:, 0:512]).then_inc(ms_dma, 16)
                    for v in range(2):
                        pool.dma_start(
                            stok[:, MBV + 512:MBV + 768].rearrange("b (g v n) -> b g v n", g=2, v=2)[:, :, v, :],
                            STOKEN[:, 512 + v * P:512 + (v + 1) * P].rearrange("b (g n) -> b g n", g=2)).then_inc(
                                ms_dma, 16)
                    pool.wait_ge(ms_dma, 6 * 16)
                    pool.dma_start(SV2[:, 128:160],
                                   stok[:, MBV:MBV + 512].rearrange("b (x p) -> b x p", p=32)).then_inc(ms_dma2, 16)
                    for v in range(2):
                        pool.dma_start(SV2[:, 160 + v:161 + v],
                                       dts[v].unsqueeze(2)).then_inc(ms_dma2, 16)
                    for b in range(NS):
                        pool.dma_start(SV2[16 * b:16 * b + 16, 0:128],
                                       stok[b, MBV + 512:MBV + 768].rearrange("(g x) -> g x", g=2).unsqueeze(
                                           1).broadcast_to([2, 8, 128])).then_inc(ms_dma2, 16)
                    pool.wait_ge(ms_dve, MS_DVE.index('y') + 1)
                    pool.dma_start(ssm_s[0].rearrange("b h (r p) n -> (b h r) (p n)", r=2), SSM[:, :]).then_inc(
                        out_dma, 16)
                    pool.dma_start(osc[:, 256:768].rearrange("b (x p) -> b x p", p=32), SV1[:, 0:32]).then_inc(
                        ms_dma3, 16)
                    pool.wait_ge(ms_dma3, 16)
                    pool.dma_start(STOKEN[:, 0:512], osc[:, 256:768]).then_inc(ms_dma3, 16)
                elif what == 'mix_final':
                    pool.wait_ge(hg_dve, step(HG_DVE, 'out', NB - 1))
                    for h in range(2):
                        pool.dma_start(hg_p[0, 0].rearrange("(j h) k v -> h k j v", h=2)[h],
                                       HSH[64 * h:64 * h + 64, 4, :, :]).then_inc(out_dma, 16)
                    pool.wait_ge(fin_dve, 2)
                    for r in range(2):
                        for gr in range(2):
                            pool.dma_start(ssm_p[0, 0].rearrange("(g a r) p n -> g r p a n", g=2, a=2)[gr, r],
                                           STF[64 * r:64 * r + 64, :, 64 * gr:64 * gr + 64]).then_inc(out_dma, 16)
            pool.wait_ge(out_dma, 15 * 16)
            end_phase(pool, 2)
            for i in range(9):
                pool.wait_ge(y_act, i + 1)
                pool.wait_ge(y_dve, i + 1)
                if i < NB:
                    pool.dma_start(y_p[0, i * BLK:(i + 1) * BLK, :], OT[i % 2][:, :]).then_inc(y_out[i % 2], 16)
                else:
                    pool.dma_start(y_s[:, 0, :], OT[i % 2][0:NS, :]).then_inc(y_out[i % 2], 16)
            pool.wait_ge(y_out[0], 16 * 5)
            pool.wait_ge(y_out[1], 16 * 4)

        @block.tensor
        def _(pe):
            mm = nc.tensor.matmul

            def turn(out, in_, n):
                return nc.tensor.transpose(out, in_, ident[0:n, 0:n])

            def turn_x(i, bufs):
                b0 = 3 + 2 * (i % 2) if i < 9 else 0
                pe.wait_ge(x_loaded[i % 2], 16 * XUSE(i))
                if i < 9:
                    if i >= 2:
                        pe.wait_ge(x_act, i - 1)
                        pe.wait_ge(x_dve, i - 1)
                else:
                    if i > 9:
                        pe.wait_ge(x_act, i)
                        pe.wait_ge(x_dve, i)
                n = BLK if i % 9 < NB else NS
                for k in range(KT):
                    last = turn(BK8[b0 + k // 4][:, (k % 4) * P:(k % 4) * P + n], bufs[i % 2][0:n, k * P:(k + 1) * P], n)
                last.then_inc(x_turned, 1)

            def dense(q):
                u, c = QUANTA[q]
                kind, arg = UNITS[u]
                bank = BK8[BANK[q]]
                if PREV[q] is not None:
                    pe.wait_ge(evac[evac_engine(PREV[q])], EVN[PREV[q]])
                if kind == 'ada':
                    pe.wait_ge(raw_loaded[u % NRAW], 16 * (u // NRAW + 1))
                    for k in range(KT):
                        last = mm(bank[:, 0:9], RAW[u % NRAW][:, k, :], CT[:, k, :], start=(k == 0), stop=(k == KT - 1))
                    last.then_inc(dense_done, 1)
                    return
                if c == 0:
                    pe.wait_ge(w_hi, SIDX[u] + 1)
                    pe.wait_ge(w_lo, SIDX[u] + 1)
                if kind in ('out', 'gate'):
                    ready = [mix_lo, n_lo][kind == 'gate']
                    pe.wait_ge(ready, c + 1 + (3 if kind == 'gate' else 0))
                if kind == 'rw':
                    pe.wait_ge(n_lo, c + 1)
                if kind == 'down':
                    tiles = sum(GROUPS[:arg[0] + 1])
                    pe.wait_ge(gu_lo, 3 * (tiles - 1) + c + 1)
                hi_, lo_ = {'out': (MHI, MLO), 'gate': (H2I, H2L), 'up': (H2I, H2L), 'down': (GHI, GLO)}.get(
                    kind, (HHI, HLO))
                whi, wlo = w_split(SIDX[u])
                cols = slice(c * CH, (c + 1) * CH)
                nk = unit_k(u)
                for k in range(nk):
                    mm(bank[:, 0:CH], whi[:, k, :], hi_[:, k, cols], start=(k == 0), stop=False)
                    mm(bank[:, 0:CH], whi[:, k, :], lo_[:, k, cols], start=False, stop=False)
                    last = mm(bank[:, 0:CH], wlo[:, k, :], hi_[:, k, cols], start=False, stop=(k == nk - 1))
                last.then_inc(dense_done, 1)

            def norm_sum(n):
                pe.wait_ge(n_sum, n + 1)
                if n:
                    pe.wait_ge(n_rs, n)
                mm(BK8[7][:, 0:CH], ones[:, :], (SS, SS2, SS3)[n // 3][:, :], start=True, stop=True).then_inc(n_tot, 1)

            pe.wait_ge(ident_built, 1)
            pe.wait_ge(c_act, 1)
            for k in range(KT):
                last = turn(BK8[7][:, k * 9:k * 9 + 9], C9[:, 0, k * P:(k + 1) * P], 9)
            last.then_inc(c_turned, 1)
            pe.wait_ge(par_loaded, 16 * len(ROWS1 + ROWS2))
            turn(BK8[7][:, 128:128 + NR1], PV[0:NR1, 0, :], NR1)
            turn(BK8[7][:, 256:256 + NR2], PV[0:NR2, 1, :], NR2).then_inc(par_turned, 1)
            pe.wait_ge(par_ready, 1)
            for q in range(16):
                dense(q)
                if q % 2 and q // 2 < 8:
                    turn_x(q // 2, XTOK)
            turn_x(8, XTOK)
            pe.wait_ge(consts_built, 1)
            for n in range(3):
                norm_sum(n)
            end_phase(pe, 0, wait=False)

            def rw_init():
                pe.wait_ge(st_loaded, 16 * 5)
                for t in range(6):
                    turn(BK8[3][:, 24 * t:24 * t + 24], SCT[:, t * P:(t + 1) * P], 24)
                for t in range(7):
                    last = turn(BK8[3][:, 160 + 8 * t:168 + 8 * t], SHT[:, t * P:(t + 1) * P], NS)
                last.then_inc(st_turned, 1)

            def dt_proj():
                pe.wait_ge(dt_split, 1)
                for i in range(9):
                    t0 = i * P if i < 8 else T - P
                    for k in range(KT):
                        mm(BK8[4][:, 8 * i:8 * i + 8], HHI[:, k, t0:t0 + P], WDT[0][:, k, :], start=(k == 0), stop=False)
                        mm(BK8[4][:, 8 * i:8 * i + 8], HHI[:, k, t0:t0 + P], WDT[1][:, k, :], start=False, stop=False)
                        last = mm(BK8[4][:, 8 * i:8 * i + 8], HLO[:, k, t0:t0 + P], WDT[0][:, k, :], start=False,
                                  stop=(k == KT - 1))
                last.then_inc(dt_done, 1)

            def lora(w, mx, la, waits):
                for s_, v_ in waits:
                    pe.wait_ge(s_, v_)
                for j in range(2):
                    cj = slice(j * P, (j + 1) * P)
                    oj = slice(j * BLK, j * BLK + w)
                    mm(BK8[3][:, oj], WL[0:32, cj], la[0:32, 0:w], start=True, stop=True)
                    mm(BK8[5][:, oj], WL[32:64, cj], mx[32:64, 6, 0:w], start=True, stop=True)
                    last = mm(BK8[4][:, oj], WL[64:P, cj], la[64:P, 0:w], start=True, stop=True)
                return last

            HP = [slice(0, 64), slice(64, P)]

            def rw(stage, b):
                def V(name):
                    return rw_dve, step(RW_DVE, name, b)

                def A(name):
                    return rw_act, step(RW_ACT, name, b)

                B0, B1, B2, B3, B4 = BK8[3:8]
                if stage == 'lora':
                    lora(BLK, MX, LA, [V('mixed'), A('lora_in')]).then_inc(rw_pe, 1)
                    pe.wait_ge(*V('squared'))
                    mm(B3[:, 0:2 * BLK], headsum[:, :], T2[:, :, :].rearrange("p j t -> p (j t)"), start=True,
                       stop=True).then_inc(rw_pe, 1)
                elif stage == 'turn':
                    pe.wait_ge(*V('operands'))
                    for src, bank in ((AR, B2), (BK, B3), (VZ, B4)):
                        for jc in range(4):
                            last = turn(bank[:, jc * P:(jc + 1) * P], src[:, jc, :, :].rearrange("p s t -> p (s t)"), P)
                    last.then_inc(rw_pe, 1)
                    for hp, bank in ((0, B0), (1, B1)):
                        for jc in range(4):
                            last = mm(bank[:, jc * P:(jc + 1) * P], BK[HP[hp], jc, :, :].rearrange("p s t -> p (s t)"),
                                      AR[HP[hp], jc, :, :].rearrange("p s t -> p (s t)"), start=True, stop=True)
                    last.then_inc(rw_pe, 1)
                    pe.wait_ge(*A('turned'))
                    for jc in range(4):
                        for hp in range(2):
                            last = mm(B2[HP[hp], jc * 64:jc * 64 + 64], AR[HP[hp], jc, hp, :], BK[HP[hp], jc, hp, :],
                                      start=True, stop=True)
                    last.then_inc(rw_pe, 1)
                elif stage[:3] == 'inv':
                    lv = int(stage[3])
                    pe.wait_ge(*V(f'inv{lv - 1}'))
                    if lv == 1:
                        pe.wait_ge(*V('masked'))
                    for jc in range(4):
                        for hp in range(2):
                            last = mm(B0[HP[hp], jc * 64:jc * 64 + 64], AM[HP[hp], hp, jc, 64 * hp:64 * hp + 64],
                                      X[HP[hp], jc, :], start=True, stop=True)
                    last.then_inc(rw_pe, 1)
                    pe.wait_ge(*A(f'P{lv}'))
                    for jc in range(4):
                        for hp in range(2):
                            if lv < 5:
                                mm(B1[HP[hp], jc * 64:jc * 64 + 64], Y[HP[hp], jc, :], PS[HP[hp], jc, :],
                                   start=True, stop=True)
                            last = mm(B3[HP[hp], jc * 64:jc * 64 + 64], PS[HP[hp], jc, :], Y[HP[hp], jc, :],
                                      start=True, stop=True)
                    last.then_inc(rw_pe, 1)
                elif stage == 'fold':
                    pe.wait_ge(*V('inv5'))
                    for jc in range(4):
                        for hp in range(2):
                            o = 1 - hp
                            last = mm(B4[HP[hp], jc * 64:jc * 64 + 64], AM[HP[o], hp, jc, 64 * hp:64 * hp + 64],
                                      UV[HP[o], jc, 64 * hp:64 * hp + 64], start=True, stop=True)
                    last.then_inc(rw_pe, 1)
                    for jc in range(4):
                        for hp in range(2):
                            last = mm(B2[HP[hp], jc * 64:jc * 64 + 64], ARt[HP[hp], jc, 64 * hp:64 * hp + 64],
                                      Y[HP[hp], jc, :], start=True, stop=True)
                    last.then_inc(rw_pe, 1)
                    pe.wait_ge(*A('T1'))
                    for jc in range(4):
                        for hp in range(2):
                            last = mm(B0[HP[hp], jc * 64:jc * 64 + 64], Y[HP[hp], jc, :], T1S[HP[hp], jc, :],
                                      start=True, stop=True)
                    last.then_inc(rw_pe, 1)
                elif stage[:3] == 'seq':
                    c = int(stage[3])
                    if c == 0:
                        pe.wait_ge(*A('PT'))
                        if b == 0:
                            pe.wait_ge(init_pool, 1)
                        else:
                            pe.wait_ge(rw_dve, step(RW_DVE, 'S1', b - 1))
                    else:
                        pe.wait_ge(*V('S0'))
                    for j in range(2):
                        for hp in range(2):
                            last = mm(B1[HP[hp], j * 64:j * 64 + 64], PTS[HP[hp], 2 * j + c, :], ST[HP[hp], j, :],
                                      start=True, stop=True)
                    last.then_inc(rw_pe, 1)
                    pe.wait_ge(*V(f'U{c}'))
                    for j in range(2):
                        for hp in range(2):
                            jc = 2 * j + c
                            out = B3[HP[hp], jc * 64:jc * 64 + 64]
                            mm(out, ST[HP[hp], j, :], AR[HP[hp], jc, 1 - hp, :], start=True, stop=False)
                            mm(out, UV[:, jc, 64 * hp:64 * hp + 64], AM[:, hp, jc, 64 * (1 - hp):64 * (1 - hp) + 64],
                               start=False, stop=True)
                            last = mm(B4[HP[hp], j * 64:j * 64 + 64], BKt[:, jc, 64 * hp:64 * hp + 64],
                                      UV[:, jc, 64 * hp:64 * hp + 64], start=True, stop=True)
                    last.then_inc(rw_pe, 1)
                elif stage == 'post':
                    rw_norm_sums(BLK, V, A, rw_pe)

            def rw_norm_sums(w, V, A, s):
                pe.wait_ge(*V('o'))
                mm(BK8[3][:, 0:2 * BLK], headsum[:, :], OS[:, :, :].rearrange("p j t -> p (j t)"), start=True,
                   stop=True).then_inc(s, 1)
                pe.wait_ge(*V('bonus'))
                mm(BK8[5][:, 0:2 * BLK], headsum[:, :], KK[:, :, :].rearrange("p j t -> p (j t)"), start=True,
                   stop=True).then_inc(s, 1)
                mm(BK8[4][:, 0:2 * BLK], headsum[:, :], T2[:, :, :].rearrange("p j t -> p (j t)"), start=True,
                   stop=True).then_inc(s, 1)

            def rws(s):
                V, A = smp('dve'), smp('act')
                if s == 0:
                    pe.wait_ge(rw_dve, step(RW_DVE, 'out', NB - 1))
                    lora(NS, MX, LA, [V('mixed'), A('lora_in')]).then_inc(smp_pe, 1)
                    pe.wait_ge(*V('squared'))
                    mm(BK8[6][:, 0:2 * BLK], headsum[:, :], T2[:, :, :].rearrange("p j t -> p (j t)"), start=True,
                       stop=True).then_inc(smp_pe, 1)
                elif s == 1:
                    pe.wait_ge(*V('vectors'))
                    pe.wait_ge(*A('wexp'))
                    for v, src in enumerate((MX[:, 0:2, :], KK, SG[:, 2:4, :], KP, SG[:, 0:2, :], MX[:, 4:6, :])):
                        for j in range(2):
                            i = 2 * v + j
                            last = turn(BK8[3 + i // 4][0:NS, (i % 4) * P:(i % 4) * P + P], src[:, j, 0:NS], P)
                    last.then_inc(smp_pe, 1)
                elif s == 3:
                    pe.wait_ge(smp_dma4, 16)
                    for j in range(2):
                        last = turn(BK8[6][:, 8 * j:8 * j + 8], STKW[:, j * P:(j + 1) * P], NS)
                    last.then_inc(smp_pe, 1)
                    rw_norm_sums(NS, V, A, smp_pe)

            def rw_final():
                pe.wait_ge(*smp('dve')('out'))
                for j in range(2):
                    turn(BK8[3][0:64, j * P:(j + 1) * P], ST[:, j, :], P)
                for t in range(7):
                    turn(BK8[4 + t // 4][0:9, (t % 4) * P:(t % 4) * P + P], PR[:, t, SEQ:SEQ + 9], P)
                for t in range(6):
                    last = turn(BK8[6 + t // 4][0:11, (t % 4) * P:(t % 4) * P + P], XL[:, t, :], P)
                last.then_inc(fin_pe, 1)

            for what, arg in PLAN1:
                if what == 'mm':
                    dense(arg)
                elif what == 'dt':
                    rw_init()
                    dt_proj()
                elif what[:3] == 'rw_' and what != 'rw_final':
                    rw(what[3:], arg)
                elif what == 'rws':
                    rws(arg)
                elif what == 'rw_final':
                    rw_final()
            end_phase(pe, 1)

            H0, H1, H2, H3, M0, M1, M2, M3 = BK8

            def pre():
                pe.wait_ge(pre_dve, PRE_DVE.index('dta') + 1)
                mm(M0[:, 0:64], triu[:, :], DTA[:, 0:8, :].rearrange("p b h -> p (b h)"), start=True, stop=True)
                mm(M0[:, 64:128], ones[:, :], DTA[:, 0:8, :].rearrange("p b h -> p (b h)"), start=True,
                   stop=True).then_inc(pre_pe, 1)

            def hg(stage, b):
                def V(name):
                    return hg_dve, step(HG_DVE, name, b)

                def A(name):
                    return hg_act, step(HG_ACT, name, b)

                if stage == 'att':
                    pe.wait_ge(*V('factors'))
                    if b:
                        pe.wait_ge(x_act, 9 + b)
                        pe.wait_ge(x_dve, 9 + b)
                    for j in range(2):
                        turn(H0[:, j * P:(j + 1) * P], HB[:, 4 + j, :], P)
                    for j in range(2):
                        last = turn(H0[:, (2 + j) * P:(3 + j) * P], HD[:, 5, j, :], P)
                    last.then_inc(hg_pe, 1)
                    for hp, bank in ((0, H1), (1, H2)):
                        for j in range(2):
                            for lv in range(6):
                                for s in range(4):
                                    t = slice(32 * s, 32 * s + 32)
                                    kk = HD[HP[hp], lv, j, t] if lv < 5 else HK[HP[hp], j, t]
                                    qq = HD[HP[hp], lv, j, t] if lv < 5 else HB[HP[hp], j, t]
                                    last = mm(bank[t, (lv * 2 + j) * 32:(lv * 2 + j) * 32 + 32], kk, qq, start=True,
                                              stop=True)
                    last.then_inc(hg_pe, 1)
                elif stage == 'state':
                    pe.wait_ge(*A('v'))
                    for j in range(2):
                        for hp in range(2):
                            last = mm(H0[HP[hp], j * 256:j * 256 + 256], HKT[:, j, 64 * hp:64 * hp + 64],
                                      HVD[:, j, :, 64 * hp:64 * hp + 64], start=True, stop=True)
                    last.then_inc(hg_pe, 1)
                    pe.wait_ge(*V('att'))
                    pe.wait_ge(*V('S'))
                    for hp in range(2):
                        for j in range(2):
                            mm(H3[HP[hp], j * P:(j + 1) * P], HVT[:, j, 64 * hp:64 * hp + 64], HAD[:, 2 * hp + j, :],
                               start=(j == 0), stop=False, skip_group_check=True)
                    for hp in range(2):
                        for j in range(2):
                            for s in range(4):
                                last = mm(H3[HP[hp], j * P + 32 * s:j * P + 32 * s + 32], HSH[HP[hp], s, j, :],
                                          HQ[HP[hp], j, 32 * s:32 * s + 32], start=False, stop=True,
                                          skip_group_check=True)
                    last.then_inc(hg_pe, 1)
                elif stage == 'post':
                    pe.wait_ge(*V('squared'))
                    mm(H1[:, 0:2 * BLK], headsum[:, :], HT[:, :, :].rearrange("p j t -> p (j t)"), start=True,
                       stop=True).then_inc(hg_pe, 1)
                    pe.wait_ge(*V('out'))
                    turn_x(9 + b, XTOK2)

            def mb(stage, b):
                def V(name):
                    return mb_dve, step(MB_DVE, name, b)

                def A(name):
                    return mb_act, step(MB_ACT, name, b)

                if stage == 'turn':
                    pe.wait_ge(mb_silu, b + 1)
                    if b:
                        pe.wait_ge(mb_dve, step(MB_DVE, 'out', b - 1))
                    for t in range(4):
                        turn(M0[:, t * P:(t + 1) * P], XB[:, t, :], P)
                    turn(M1[:, 0:P], XB[:, 4, :], P)
                    mm(M1[:, P:2 * P], XB[0:64, 4, :], XB[0:64, 5, :], start=True, stop=True)
                    mm(M2[:, 0:P], XB[64:P, 4, :], XB[64:P, 5, :], start=True, stop=True).then_inc(mb_pe, 1)
                elif stage == 'decay':
                    pe.wait_ge(*V('cb'))
                    for h in range(8):
                        last = mm((M2, M3)[h // 4][:, (h % 4) * P:(h % 4 + 1) * P],
                                  DTA[:, b, h:h + 1].broadcast_to([P, P]), triu[:, :], start=True, stop=True)
                    last.then_inc(mb_pe, 1)
                elif stage == 'prod':
                    pe.wait_ge(*V('m'))
                    pe.wait_ge(mb_pool, step(MB_POOL, 'ce', b))
                    if b == 0:
                        pe.wait_ge(pre_pool, 1)
                    for h in range(8):
                        j, hp, gr = h // 2, h % 2, h // 4
                        out = (M1, M2)[gr][HP[hp], (j % 2) * P:(j % 2 + 1) * P]
                        mm(out, XD[:, h, :], MM[:, h, :], start=True, stop=False)
                        last = mm(out, STt[HP[gr], h % 4, :], CE[HP[gr], h % 4, :], start=False, stop=True)
                    last.then_inc(mb_pe, 1)
                    for gr in range(2):
                        last = mm(M0[HP[gr], 0:256], BT[:, 64 * gr:64 * gr + 64],
                                  XDE[:, 4 * gr:4 * gr + 4, :].rearrange("p h x -> p (h x)"), start=True, stop=True)
                    last.then_inc(mb_pe, 1)
                elif stage == 'post':
                    mb_norm_sum(A, mb_pe)

            def mb_norm_sum(A, s):
                pe.wait_ge(*A('squared'))
                for gr in range(2):
                    for t in range(2):
                        last = mm(M3[:, gr * P:(gr + 1) * P], ones[:, :], T4[:, 2 * gr + t, :], start=(t == 0),
                                  stop=(t == 1))
                last.then_inc(s, 1)

            def hgs():
                pe.wait_ge(hs_act, 2)
                for i in range(8):
                    src = (HB[:, i, 0:NS] if i < 2 else HE[:, i - 2, 0:NS] if i < 4 else HK[:, i - 4, 0:NS] if i < 6
                           else HB[:, i - 2, 0:NS])
                    last = turn((H2, H3)[i // 4][0:NS, (i % 4) * P:(i % 4 + 1) * P], src, P)
                last.then_inc(hs_pe, 1)
                pe.wait_ge(hs_dve, HS_DVE.index('opart') + 1)
                mm(H2[0:32, 0:64], G4[:, :], SO[:, :], start=True, stop=True).then_inc(hs_pe, 1)
                pe.wait_ge(hs_dma3, 32)
                for j in range(2):
                    last = turn(H3[:, 8 * j:8 * j + 8], STK[:, j * P:(j + 1) * P], NS)
                last.then_inc(hs_pe, 1)
                pe.wait_ge(hs_dve, HS_DVE.index('squared') + 1)
                mm(H2[:, 0:2 * BLK], headsum[:, :], HT[:, :, :].rearrange("p j t -> p (j t)"), start=True,
                   stop=True).then_inc(hs_pe, 1)

            def mbs():
                pe.wait_ge(mb_silu, NB + 1)
                pe.wait_ge(mb_dve, step(MB_DVE, 'out', NB - 1))
                for t in range(6):
                    last = turn((M0, M1)[t // 4][0:NS, (t % 4) * P:(t % 4 + 1) * P], XB[:, t, 0:NS], P)
                last.then_inc(ms_pe, 1)
                pe.wait_ge(ms_dma3, 32)
                for t in range(4):
                    last = turn(M2[:, 8 * t:8 * t + 8], STOKEN[:, t * P:(t + 1) * P], NS)
                last.then_inc(ms_pe, 1)
                mb_norm_sum(lambda name: (ms_act, MS_ACT.index(name) + 1), ms_pe)

            def mix_final():
                for a in range(2):
                    last = turn(H0[:, a * P:(a + 1) * P],
                                STt[:, 2 * a:2 * a + 2, :].rearrange("p r x -> p (r x)"), P)
                last.then_inc(fin_pe, 1)

            for what, arg in PLAN2:
                if what == 'pre':
                    pre()
                elif what[:3] == 'hg_':
                    hg(what[3:], arg)
                elif what[:3] == 'mb_':
                    mb(what[3:], arg)
                elif what == 'hgs':
                    pe.wait_ge(x_act, 9 + NB)
                    pe.wait_ge(x_dve, 9 + NB)
                    turn_x(17, XTOK2)
                    hgs()
                elif what == 'mbs':
                    mbs()
                else:
                    pe.wait_ge(x_act, 10 + NB)
                    pe.wait_ge(x_dve, 10 + NB)
                    mix_final()
            end_phase(pe, 2)

            for what, arg in PLAN3:
                if what == 'mm':
                    dense(arg)
                elif what == 'norm':
                    norm_sum(arg)
            for i in range(9):
                n = BLK if i < NB else NS
                t0 = i * BLK
                pe.wait_ge(n_h, 6 + min(NCH, (t0 + n - 1) // CH + 1))
                if i >= 2:
                    pe.wait_ge(y_act, i - 1)
                    pe.wait_ge(y_dve, i - 1)
                for k in range(KT):
                    last = turn(BK8[2 * (i % 2) + k // 4][0:n, (k % 4) * P:(k % 4 + 1) * P], XT[:, k, t0:t0 + n], P)
                last.then_inc(y_turned, 1)

        @block.scalar
        def _(act):
            a = nc.scalar
            link = linker(act, act_own)
            HP = [slice(0, 64), slice(64, P)]

            def split_hi(i):
                u = SPLIT[i]
                nk = unit_k(u)
                act.wait_ge(raw_loaded[u % NRAW], 16 * (u // NRAW + 1))
                if SPREV[i] is not None:
                    act.wait_ge(dense_done, LASTQ[SPLIT[SPREV[i]]] + 1)
                a.copy(w_split(i)[0][:, 0:nk, :], RAW[u % NRAW][:, 0:nk, :]).then_inc(w_hi, 1)

            def bring_out(q):
                if evac_engine(q) != 'act':
                    return
                u, c = QUANTA[q]
                kind, t = UNITS[u]
                bank = BK8[BANK[q]]
                cols = slice(c * CH, (c + 1) * CH)
                if kind == 'gate':
                    n = GATES.index(q)
                    if n >= 2:
                        act.wait_ge(evac['dve'], EVN[UPS[n - 2]])
                    act.wait_ge(dense_done, q + 1)
                    a.activation(SGF[n % 2][:, :], bank[:, 0:CH], ACT.Silu).then_inc(evac['act'], 1)
                    return
                if kind in ('hg', 'xbc'):
                    r = STAGED.index(q)
                    if 0 < r <= 18:
                        act.wait_ge(conv_done, r)
                    if r >= 20:
                        act.wait_ge(stg_out[r % 2], 16 * ((r - 18) // 2))
                act.wait_ge(dense_done, q + 1)
                if kind == 'ada':
                    a.activation(MOD[:, t, :], bank[:, 0:9], ACT.Identity, bias=par('b_ada', t)).then_inc(
                        evac['act'], 1)
                elif kind == 'rw':
                    a.copy(PR[:, t, 1 + c * CH:1 + (c + 1) * CH], bank[:, 0:CH]).then_inc(evac['act'], 1)
                elif kind in ('hgg', 'z'):
                    a.copy(MIX[:, t + (2 if kind == 'z' else 0), cols], bank[:, 0:CH]).then_inc(evac['act'], 1)
                else:
                    a.copy(STG[STAGED.index(q) % 2][:, 3:3 + CH], bank[:, 0:CH]).then_inc(evac['act'], 1)

            def x_half(i, dst):
                act.wait_ge(x_turned, i + 1)
                n = BLK if i % 9 < NB else NS
                b0 = 3 + 2 * (i % 2) if i < 9 else 0
                t0 = (i % 9) * BLK
                a.copy(dst[:, 0:4, t0:t0 + n], BK8[b0][:, :].rearrange("p (k t) -> p k t", k=4)[:, :, 0:n]).then_inc(
                    x_act, 1)

            def norm_squares(n, src, waits):
                c = n % 3
                for s_, v_ in waits:
                    act.wait_ge(s_, v_)
                if n:
                    act.wait_ge(n_sum, n)
                a.activation((SQ, SQ2, SQ3)[n // 3][:, :, :], src[:, :, c * CH:(c + 1) * CH], ACT.Square).then_inc(
                    n_sq, 1)

            def norm_scale(n):
                act.wait_ge(n_tot, n + 1)
                if n:
                    act.wait_ge(n_h, n)
                rb = (RB, RB2, RB3)[n // 3]
                link(a.activation(rb[:, :], BK8[7][:, 0:CH], ACT.Ln, bias=CST[:, 2:3], scale=1.0 / D))
                a.activation(rb[:, :], rb[:, :], ACT.Exp, scale=-0.5).then_inc(n_rs, 1)

            def norm_head(n):
                act.wait_ge(n_h, n + 1)
                c = n % 3
                a.copy((HHI, H2I)[n // 3][:, :, c * CH:(c + 1) * CH], (H32, H322)[n // 3][:, :, :]).then_inc(n_hi, 1)

            act.wait_ge(c_loaded, 32)
            a.activation(C9[:, 1, :], C9[:, 0, :], ACT.Sigmoid).then_inc(c_sig, 1)
            act.wait_ge(wdt_loaded, 16)
            a.copy(WDT[0][:, :, :], WDR[:, :, :]).then_inc(wdt_hi, 1)
            act.wait_ge(par_ready, 1)
            for q in range(16):
                if q % 2 and q // 2 < 8:
                    x_half(q // 2, XT0)
                bring_out(q)
            x_half(8, XT0)
            split_hi(0)
            for n in range(3):
                norm_squares(n, XT0, [(x_dve, 9), (x_act, 9)])
                norm_scale(n)
                norm_head(n)
            end_phase(act, 0)

            def lora_in(w, mx, la):
                a.activation(la[0:32, 0:w], mx[0:32, 6, 0:w], ACT.Tanh)
                return a.activation(la[64:P, 0:w], mx[64:P, 6, 0:w], ACT.Sigmoid)

            def gates(w):
                for j in range(2):
                    a.activation(SG[:, j, 0:w], BK8[3][:, j * BLK:j * BLK + w], ACT.Sigmoid, bias=par('rw_w0', j))
                    a.activation(SG[:, 2 + j, 0:w], BK8[5][:, j * BLK:j * BLK + w], ACT.Sigmoid, bias=par('rw_a0', j))
                return a.copy(GT[:, :, 0:w], BK8[4][:, 0:2 * BLK].rearrange("p (j t) -> p j t", j=2)[:, :, 0:w])

            def kk_scale(w):
                link(a.activation(RS[:, :, 0:w], T2[:, :, 0:w], ACT.Ln, scale=float(2 ** 30)))
                return a.activation(RS[:, :, 0:w], RS[:, :, 0:w], ACT.Exp, scale=-0.5, bias=CST[:, 1:2])

            def var_scale(w):
                link(a.activation(RS[:, :, 0:w], BK8[4][:, 0:2 * BLK].rearrange("p (j t) -> p j t", j=2)[:, :, 0:w],
                                  ACT.Ln, scale=1.0 / 64, bias=CST[:, 0:1]))
                return a.activation(RS[:, :, 0:w], RS[:, :, 0:w], ACT.Exp, scale=-0.5)

            def rw(stage, b):
                def V(name):
                    return rw_dve, step(RW_DVE, name, b)

                def T_(name):
                    return rw_pe, step(RW_PE, name, b)

                if stage == 'lora':
                    act.wait_ge(*V('mixed'))
                    lora_in(BLK, MX, LA).then_inc(rw_act, 1)
                    act.wait_ge(*T_('lora'))
                    gates(BLK).then_inc(rw_act, 1)
                elif stage == 'gate':
                    act.wait_ge(*V('clamped'))
                    kk_scale(BLK).then_inc(rw_act, 1)
                elif stage == 'decay':
                    act.wait_ge(*V('decays'))
                    a.activation(EB[:, :, :], BB[:, :, :], ACT.Exp)
                    a.activation(ENB[:, :, :], BB[:, :, :], ACT.Exp, scale=-1.0)
                    a.activation(BM[:, :, :], BM[:, :, :], ACT.Exp).then_inc(rw_act, 1)
                elif stage == 'turn':
                    act.wait_ge(*T_('turned'))
                    for dst, bank in ((ARt, BK8[5]), (BKt, BK8[6]), (UV, BK8[7])):
                        last = a.copy(dst[:, :, :].rearrange("p c t -> p (c t)"), bank[:, :])
                    last.then_inc(rw_act, 1)
                elif stage[:3] == 'inv':
                    act.wait_ge(*T_(f'P{stage[3]}'))
                    a.copy(PS[:, :, :].rearrange("p c t -> p (c t)"), BK8[3][:, 0:256]).then_inc(rw_act, 1)
                elif stage == 'fold':
                    act.wait_ge(*T_('T1'))
                    a.copy(T1S[:, :, :].rearrange("p c t -> p (c t)"), BK8[7][:, 0:256]).then_inc(rw_act, 1)
                    act.wait_ge(*T_('PT'))
                    a.copy(PTS[:, :, :].rearrange("p c t -> p (c t)"), BK8[5][:, 0:256]).then_inc(rw_act, 1)
                elif stage == 'post':
                    act.wait_ge(*T_('var'))
                    var_scale(BLK).then_inc(rw_act, 1)

            def rws(s):
                V, T_ = smp('dve'), smp('pe')
                if s == 0:
                    act.wait_ge(*V('mixed'))
                    lora_in(NS, MX, LA).then_inc(smp_act, 1)
                    act.wait_ge(*T_('lora'))
                    gates(NS).then_inc(smp_act, 1)
                    act.wait_ge(*V('clamped'))
                    kk_scale(NS).then_inc(smp_act, 1)
                elif s == 1:
                    act.wait_ge(*V('vectors'))
                    a.activation(SG[:, 0:2, 0:NS], SG[:, 0:2, 0:NS], ACT.Exp).then_inc(smp_act, 1)
                    act.wait_ge(*T_('tok'))
                    for i in range(3):
                        last = a.copy(STKW[:, 512 * i:512 * i + 512], BK8[3 + i][0:NS, :])
                    last.then_inc(smp_act, 1)
                elif s == 3:
                    act.wait_ge(*T_('var'))
                    var_scale(NS).then_inc(smp_act, 1)

            for what, arg in PLAN1:
                if what == 'split':
                    split_hi(arg)
                elif what == 'ev':
                    bring_out(arg)
                elif what[:3] == 'rw_' and what != 'rw_final':
                    rw(what[3:], arg)
                elif what == 'rws':
                    rws(arg)
            end_phase(act, 1)

            def pre():
                for t in range(6):
                    if t >= 2:
                        act.wait_ge(silu_m, t - 1)
                    a.activation((SMT, SSM)[t % 2][:, 0:T], MIX[:, t, :], ACT.Sigmoid).then_inc(silu_s, 1)
                act.wait_ge(pre_dma, 32)
                a.activation(AEX[:, :], AEX[:, :], ACT.Exp).then_inc(pre_act, 1)
                act.wait_ge(pre_dve, PRE_DVE.index('nabs') + 1)
                link(a.activation(DTE[:, :, :], DTN[:, :, :], ACT.Exp))
                a.activation(DTE[:, :, :], DTE[:, :, :], ACT.Ln, bias=1.0).then_inc(pre_act, 1)
                act.wait_ge(pre_dve, PRE_DVE.index('dta') + 1)
                a.activation(DTE[:, :, :], DTA[:, :, :], ACT.Exp).then_inc(pre_act, 1)
                act.wait_ge(pre_dve, PRE_DVE.index('es') + 1)
                a.activation(ES[:, :, :], ES[:, :, :], ACT.Exp)
                a.activation(ED[:, :, :].rearrange("p b h -> p (b h)"), BK8[4][:, 64:128], ACT.Exp).then_inc(pre_act, 1)

            def soft(w):
                link(a.activation(HE[:, :, 0:w], HN[:, :, 0:w], ACT.Exp))
                return a.activation(HL[:, :, 0:w], HE[:, :, 0:w], ACT.Ln, bias=1.0)

            def ssq_scale(w, bank, dst, n):
                link(a.activation(dst[:, :, 0:w], bank[:, 0:2 * BLK].rearrange("p (j t) -> p j t", j=2)[:, :, 0:w],
                                  ACT.Ln, scale=1.0 / n, bias=CST[:, 2:3]))
                return a.activation(dst[:, :, 0:w], dst[:, :, 0:w], ACT.Exp, scale=-0.5)

            def hg(stage, b):
                def V(name):
                    return hg_dve, step(HG_DVE, name, b)

                def T_(name):
                    return hg_pe, step(HG_PE, name, b)

                if stage == 'gate':
                    act.wait_ge(*V('nabs'))
                    soft(BLK).then_inc(hg_act, 1)
                    act.wait_ge(*V('logf'))
                    a.activation(HK[:, :, :], HK[:, :, :], ACT.Exp).then_inc(hg_act, 1)
                elif stage == 'levels':
                    act.wait_ge(*V('diffs'))
                    a.activation(HX[:, :, :], HBb[:, :, :], ACT.Exp)
                    a.activation(HD[:, :, :, :], HD[:, :, :, :], ACT.Exp).then_inc(hg_act, 1)
                elif stage == 'att':
                    act.wait_ge(*T_('turned'))
                    a.copy(HVT[:, :, :].rearrange("p j t -> p (j t)"), BK8[0][:, 0:256])
                    a.copy(HKT[:, :, :].rearrange("p j t -> p (j t)"), BK8[0][:, 256:512]).then_inc(hg_act, 1)
                    act.wait_ge(hg_act, step(HG_ACT, 'turned', b))
                    if b == 0:
                        act.wait_ge(pre_pool, 1)
                    for s in range(4):
                        t = slice(32 * s, 32 * s + 32)
                        last = a.copy(HVD[t, :, s, :], HVT[t, :, :])
                    last.then_inc(hg_act, 1)
                elif stage == 'post':
                    act.wait_ge(*T_('ssq'))
                    ssq_scale(BLK, BK8[1], HR, 64).then_inc(hg_act, 1)
                    x_half(9 + b, XT)

            def mb_sigmoid(b):
                w = BLK if b < NB else NS
                act.wait_ge(mb_loaded, 16 * (b + 1))
                if b:
                    act.wait_ge(mb_dve, step(MB_DVE, 'out', b - 1))
                a.activation(MM[:, 0:6, 0:w], XB[:, :, 0:w], ACT.Sigmoid).then_inc(mb_sig, 1)

            def mb(stage, b):
                def V(name):
                    return mb_dve, step(MB_DVE, name, b)

                def T_(name):
                    return mb_pe, step(MB_PE, name, b)

                if stage == 'turn':
                    mb_sigmoid(b)
                elif stage == 'decay':
                    act.wait_ge(*T_('acum'))
                    for gr in range(2):
                        last = a.activation(E2[HP[gr], :, :].rearrange("p h t -> p (h t)"), BK8[6 + gr][HP[gr], :],
                                            ACT.Exp)
                    last.then_inc(mb_act, 1)
                    act.wait_ge(*V('seg'))
                    a.activation(SEG[:, :, :], SEG[:, :, :], ACT.Exp).then_inc(mb_act, 1)
                elif stage == 'post':
                    act.wait_ge(*V('z'))
                    a.activation(T4[:, :, :], YS[:, :, :], ACT.Square).then_inc(mb_act, 1)
                    act.wait_ge(*T_('ssq'))
                    ssq_scale(BLK, BK8[7], RM, 256).then_inc(mb_act, 1)

            def hgs():
                act.wait_ge(hs_dve, HS_DVE.index('nabs') + 1)
                soft(NS).then_inc(hs_act, 1)
                act.wait_ge(hs_dve, HS_DVE.index('logf') + 1)
                a.activation(HE[:, :, 0:NS], HF[:, :, 0:NS], ACT.Exp)
                a.activation(HK[:, :, 0:NS], HK[:, :, 0:NS], ACT.Exp).then_inc(hs_act, 1)
                act.wait_ge(hs_pe, 1)
                for i in range(2):
                    last = a.copy(STK[:, 512 * i:512 * i + 512], BK8[2 + i][0:NS, :])
                last.then_inc(hs_act, 1)
                act.wait_ge(hs_pe, 4)
                ssq_scale(NS, BK8[2], HR, 64).then_inc(hs_act, 1)

            def mbs():
                act.wait_ge(ms_pe, 1)
                a.copy(STOKEN[:, 0:512], BK8[4][0:NS, :])
                a.copy(STOKEN[:, 512:768], BK8[5][0:NS, 0:256]).then_inc(ms_act, 1)
                act.wait_ge(ms_dve, MS_DVE.index('z') + 1)
                a.activation(T4[:, :, 0:NS], YS[:, :, 0:NS], ACT.Square).then_inc(ms_act, 1)
                act.wait_ge(ms_pe, 3)
                ssq_scale(NS, BK8[7], RM, 256).then_inc(ms_act, 1)

            for what, arg in PLAN2:
                if what == 'pre':
                    pre()
                elif what[:3] == 'hg_':
                    hg(what[3:], arg)
                elif what[:3] == 'mb_':
                    mb(what[3:], arg)
                elif what == 'hgs':
                    x_half(17, XT)
                    hgs()
                elif what == 'mbs':
                    mb_sigmoid(NB)
                    mbs()
            end_phase(act, 2)

            def gu_head(n):
                u, c = QUANTA[UPS[n]]
                f = UNITS[u][1]
                act.wait_ge(evac['dve'], EVN[UPS[n]])
                a.copy(GHI[:, TILE_IN_GROUP[f], c * CH:(c + 1) * CH], GU[n % 2][:, :]).then_inc(gu_hi, 1)

            for what, arg in PLAN3:
                if what == 'split':
                    split_hi(arg)
                elif what == 'ev':
                    bring_out(arg)
                    if arg in UPS:
                        gu_head(UPS.index(arg))
                elif what == 'mixsplit':
                    cols = slice(arg * CH, (arg + 1) * CH)
                    a.copy(MHI[:, :, cols], MIX[:, :, cols]).then_inc(mix_hi, 1)
                elif what == 'norm':
                    if arg < 6:
                        norm_squares(arg, XT, [(evac['dve'], EVN[LASTQ[N1 + 7] - 2 + arg % 3])])
                        norm_scale(arg)
                        norm_head(arg)
                    else:
                        norm_squares(arg, XT, [(evac['dve'], EVN[len(QUANTA) - 3 + arg % 3])])
                        norm_scale(arg)
            for i in range(9):
                n = BLK if i < NB else NS
                act.wait_ge(y_turned, i + 1)
                if i >= 2:
                    act.wait_ge(y_out[i % 2], 16 * (i // 2))
                a.copy(OT[i % 2][0:n, 0:512], BK8[2 * (i % 2)][0:n, :]).then_inc(y_act, 1)

        @block.vector
        def _(dve):
            v = nc.vector
            link = linker(dve, dve_own)
            HP = [slice(0, 64), slice(64, P)]

            def split_lo(i):
                u = SPLIT[i]
                nk = unit_k(u)
                dve.wait_ge(w_hi, i + 1)
                whi, wlo = w_split(i)
                v.tensor_tensor(wlo[:, 0:nk, :], RAW[u % NRAW][:, 0:nk, :], whi[:, 0:nk, :].bitcast(F32),
                                ALU.subtract).then_inc(w_lo, 1)

            def conv(q, r):
                u, c = QUANTA[q]
                t = UNITS[u][1]
                s = STG[r % 2]
                w = [par('mb_conv_w', 6 * j + t) for j in range(4)]
                n = CH if c < 2 else CH - NS
                if c == 0:
                    link(v.memset(s[:, 0:3], 0.0))
                else:
                    link(v.tensor_copy(s[:, 0:3], STG[(r - 1) % 2][:, CH:CH + 3]))
                dve.wait_ge(evac['act'], EVN[q])
                if r:
                    dve.wait_ge(acc_out, 16 * r)
                acc = ACC[0]
                link(v.tensor_scalar(acc[:, 0:n], s[:, 0:n], w[0], par('mb_conv_b', t), ALU.mult, ALU.add))
                for j in range(1, 3):
                    link(v.scalar_tensor_tensor(acc[:, 0:n], s[:, j:j + n], w[j], acc[:, 0:n], ALU.mult, ALU.add))
                last = v.scalar_tensor_tensor(acc[:, 0:n], s[:, 3:3 + n], w[3], acc[:, 0:n], ALU.mult, ALU.add)
                if c == 2:
                    link(last)
                    old = SCV[:, t, :].rearrange("p (b j) -> p j b", j=3)
                    out = acc[:, n:CH]
                    link(v.tensor_scalar(out, old[:, 0, :], w[0], par('mb_conv_b', t), ALU.mult, ALU.add))
                    link(v.scalar_tensor_tensor(out, old[:, 1, :], w[1], out, ALU.mult, ALU.add))
                    link(v.scalar_tensor_tensor(out, old[:, 2, :], w[2], out, ALU.mult, ALU.add))
                    link(v.scalar_tensor_tensor(out, s[:, 3 + n:3 + CH], w[3], out, ALU.mult, ALU.add))
                    last = v.tensor_copy(XL[:, t, :], s[:, 3 + n - 3:3 + CH])
                last.then_inc(conv_done, 1)

            def bring_out(q):
                u, c = QUANTA[q]
                kind, arg = UNITS[u]
                if kind == 'xbc':
                    conv(q, STAGED.index(q))
                if evac_engine(q) != 'dve':
                    return
                bank = BK8[BANK[q]]
                n = CH if c < 2 else CH - NS
                dve.wait_ge(dense_done, q + 1)
                if kind == 'up':
                    i = UPS.index(q)
                    dve.wait_ge(evac['act'], EVN[GATES[i]])
                    if i >= 2:
                        dve.wait_ge(gu_hi, i - 1)
                    v.tensor_tensor(GU[i % 2][:, :], SGF[i % 2][:, :], bank[:, 0:CH], ALU.mult).then_inc(
                        evac['dve'], 1)
                    return
                t, m = (arg, 16) if kind == 'out' else (arg[1], 40)
                c0 = c * CH
                if c == 2:
                    link(v.tensor_tensor(TMP8[:, :], bank[:, n:CH], MOD[:, m + t, 1:9], ALU.mult))
                    link(v.tensor_tensor(XT[:, t, c0 + n:c0 + CH], XT[:, t, c0 + n:c0 + CH], TMP8[:, :], ALU.add))
                v.scalar_tensor_tensor(XT[:, t, c0:c0 + n], bank[:, 0:n], MOD[:, m + t, 0:1], XT[:, t, c0:c0 + n],
                                       ALU.mult, ALU.add).then_inc(evac['dve'], 1)

            def x_half(i, dst):
                dve.wait_ge(x_turned, i + 1)
                n = BLK if i % 9 < NB else NS
                b0 = 3 + 2 * (i % 2) if i < 9 else 0
                t0 = (i % 9) * BLK
                v.tensor_copy(dst[:, 4:8, t0:t0 + n],
                              BK8[b0 + 1][:, :].rearrange("p (k t) -> p k t", k=4)[:, :, 0:n]).then_inc(x_dve, 1)

            def norm_squares(n):
                dve.wait_ge(n_sq, n + 1)
                if n:
                    dve.wait_ge(n_tot, n)
                v.tensor_reduce((SS, SS2, SS3)[n // 3][:, :],
                                (SQ, SQ2, SQ3)[n // 3][:, :, :].rearrange("p k t -> p t k"), AX.X, ALU.add).then_inc(
                                    n_sum, 1)

            def modulated(n, src, sh):
                c = n % 3
                cols = slice(c * CH, (c + 1) * CH)
                h = (H32, H322)[n // 3]
                w = CH if c < 2 else CH - NS
                dve.wait_ge(n_rs, n + 1)
                if n:
                    dve.wait_ge(n_hi, n)
                link(v.tensor_tensor(h[:, :, :], src[:, :, cols],
                                     (RB, RB2)[n // 3][:, :].unsqueeze(1).broadcast_to([P, KT, CH]), ALU.mult))
                if c == 2:
                    link(v.tensor_tensor(h[:, :, w:CH], h[:, :, w:CH], A1[:, :, 1:9], ALU.mult))
                    link(v.tensor_tensor(h[:, :, w:CH], h[:, :, w:CH], MOD[:, sh:sh + 8, 1:9], ALU.add))
                for k in range(KT):
                    last = v.tensor_scalar(h[:, k, 0:w], h[:, k, 0:w], A1[:, k, 0:1], MOD[:, sh + k, 0:1], ALU.mult,
                                           ALU.add)
                last.then_inc(n_h, 1)
                dve.wait_ge(n_h, n + 1)
                dve.wait_ge(n_hi, n + 1)
                v.tensor_tensor((HLO, H2L)[n // 3][:, :, cols], h[:, :, :], (HHI, H2I)[n // 3][:, :, cols].bitcast(F32),
                                ALU.subtract).then_inc(n_lo, 1)

            def modulation(sc, g):
                link(v.scalar_tensor_tensor(A1[:, :, :], MOD[:, sc:sc + 8, :], 1.0,
                                            par(g, 0, 8).unsqueeze(2).broadcast_to([P, KT, 9]), ALU.add, ALU.mult))

            dve.wait_ge(c_sig, 1)
            v.tensor_tensor(C9[:, 0, :], C9[:, 0, :], C9[:, 1, :], ALU.mult).then_inc(c_act, 1)
            dve.wait_ge(wdt_hi, 1)
            v.tensor_tensor(WDT[1][:, :, :], WDR[:, :, :], WDT[0][:, :, :].bitcast(F32), ALU.subtract).then_inc(
                dt_split, 1)
            dve.wait_ge(par_turned, 1)
            v.tensor_copy(CT[:, :, :].rearrange("p k c -> p (k c)"), BK8[7][:, 0:72])
            v.tensor_copy(PAR[:, 0:NR1], BK8[7][:, 128:128 + NR1])
            dve.wait_ge(dhead_loaded, 16)
            for hp in range(2):
                v.tensor_copy(par('mb_D', 0, 4)[HP[hp]], DHEAD[HP[hp], hp:8:2])
            v.tensor_copy(PAR[:, NR1:NR1 + NR2], BK8[7][:, 256:256 + NR2]).then_inc(par_ready, 1)
            for i in range(9):
                x_half(i, XT0)
            split_lo(0)
            dve.wait_ge(par_ready, 1)
            dve.wait_ge(evac['act'], 16)
            modulation(8, 'g_norm1')
            for n in range(3):
                norm_squares(n)
                modulated(n, XT0, 0)
            end_phase(dve, 0)

            def three(t):
                return t[:, :, :].rearrange("p j (c t) -> p (j c) t", c=2)

            def rw_mix(w, cur, prev):
                mu = par('rw_mu', 0, 7).unsqueeze(2).broadcast_to([P, 7, w])
                mx = MX[:, :, 0:w]
                link(v.tensor_tensor(mx, prev, cur, ALU.subtract))
                link(v.tensor_tensor(mx, mx, mu, ALU.mult))
                return v.tensor_tensor(mx, mx, cur, ALU.add)

            def rw_kk(w):
                for j in range(2):
                    link(v.tensor_scalar(KK[:, j, 0:w], MX[:, 2 + j, 0:w], par('rw_k_k', j), None, ALU.mult))
                return v.tensor_tensor(T2[:, :, 0:w], KK[:, :, 0:w], KK[:, :, 0:w], ALU.mult)

            def clamp(w, bank):
                return v.tensor_scalar(T2[:, :, 0:w], bank[:, 0:2 * BLK].rearrange("p (j t) -> p j t", j=2)[:, :, 0:w],
                                       1e-24, None, ALU.max)

            def rw_keys(w):
                for j in range(2):
                    link(v.tensor_scalar(KP[:, j, 0:w], SG[:, 2 + j, 0:w], par('rw_k_a', j), OMKA[:, j:j + 1],
                                         ALU.mult, ALU.add))
                link(v.tensor_tensor(KP[:, :, 0:w], KP[:, :, 0:w], MX[:, 2:4, 0:w], ALU.mult))
                return v.tensor_tensor(SG[:, 2:4, 0:w], SG[:, 2:4, 0:w], KK[:, :, 0:w], ALU.mult)

            def rw_post(w, V, T_, A, s, cols, obank, o0):
                def two(bank):
                    return bank[:, 0:2 * BLK].rearrange("p (j t) -> p j t", j=2)[:, :, 0:w]

                o = OS[:, :, 0:w]
                v.tensor_copy(o, o0).then_inc(s, 1)
                dve.wait_ge(*V('o'))
                dve.wait_ge(*T_('mean'))
                link(v.scalar_tensor_tensor(o, two(BK8[3]), -1.0 / 64, o, ALU.mult, ALU.add))
                v.tensor_tensor(T2[:, :, 0:w], o, o, ALU.mult).then_inc(s, 1)
                kk = KK[:, :, 0:w]
                link(v.tensor_tensor(kk, MX[:, 0:2, 0:w], KP[:, :, 0:w], ALU.mult))
                for j in range(2):
                    last = v.tensor_scalar(KK[:, j, 0:w], KK[:, j, 0:w], par('rw_r_k', j), None, ALU.mult)
                last.then_inc(s, 1)
                dve.wait_ge(*T_('bonus'))
                dve.wait_ge(*V('bonus'))
                link(v.tensor_tensor(kk, two(BK8[5]), MX[:, 4:6, 0:w], ALU.mult))
                dve.wait_ge(*A('var'))
                link(v.tensor_tensor(o, o, RS[:, :, 0:w], ALU.mult))
                for j in range(2):
                    link(v.tensor_scalar(OS[:, j, 0:w], OS[:, j, 0:w], par('rw_ln_g', j), par('rw_ln_b', j), ALU.mult,
                                         ALU.add))
                link(v.tensor_tensor(o, o, kk, ALU.add))
                v.tensor_tensor(MIX[:, 6:8, cols], o, GT[:, :, 0:w], ALU.mult).then_inc(s, 1)

            def rw(stage, b):
                def V(name):
                    return rw_dve, step(RW_DVE, name, b)

                def T_(name):
                    return rw_pe, step(RW_PE, name, b)

                def A(name):
                    return rw_act, step(RW_ACT, name, b)

                B0, B1, B2, B3, B4 = BK8[3:8]
                t0 = b * BLK
                if stage == 'mix':
                    if b == 0:
                        dve.wait_ge(init_pool, 1)
                        dve.wait_ge(evac['act'], EVN[LASTQ[16 + 6]])
                    if b:
                        dve.wait_ge(rw_dve, step(RW_DVE, 'out', b - 1))
                    rw_mix(BLK, PR[:, :, 1 + t0:1 + t0 + BLK], PR[:, :, t0:t0 + BLK]).then_inc(rw_dve, 1)
                elif stage == 'lora':
                    dve.wait_ge(*V('mixed'))
                    rw_kk(BLK).then_inc(rw_dve, 1)
                    dve.wait_ge(*T_('ssq'))
                    clamp(BLK, B3).then_inc(rw_dve, 1)
                elif stage == 'gate':
                    dve.wait_ge(*A('rs'))
                    link(v.tensor_tensor(KK[:, :, :], KK[:, :, :], RS[:, :, :], ALU.mult))
                    link(v.tensor_scalar(SG[:, 0:2, :], SG[:, 0:2, :], -EXP_M05, None, ALU.mult))
                    for j in range(2):
                        link(v.tensor_tensor_scan(BB[:, j, :], CM64[:, :], SG[:, j, :], 0.0, ALU.mult, ALU.add))
                    v.tensor_tensor(BM[:, :, :], BB[:, :, :], SG[:, 0:2, :], ALU.subtract).then_inc(rw_dve, 1)
                    link(rw_keys(BLK))
                elif stage == 'decay':
                    dve.wait_ge(*A('exps'))
                    for hp in range(2):
                        r = HP[hp]
                        v.scalar_tensor_tensor(AR[r, :, hp, :], three(KK)[r], -1.0, three(BM)[r], ALU.mult, ALU.mult)
                        v.tensor_tensor(AR[r, :, 1 - hp, :], MX[r, 0:2, :].rearrange("p j (c t) -> p (j c) t", c=2),
                                        three(EB)[r], ALU.mult)
                        v.tensor_tensor(BK[r, :, hp, :], SG[r, 2:4, :].rearrange("p j (c t) -> p (j c) t", c=2),
                                        three(ENB)[r], ALU.mult)
                        v.tensor_tensor(BK[r, :, 1 - hp, :], three(KP)[r], three(ENB)[r], ALU.mult)
                        last = v.tensor_copy(VZ[r, :, 1 - hp, :],
                                             MX[r, 4:6, :].rearrange("p j (c t) -> p (j c) t", c=2))
                    last.then_inc(rw_dve, 1)
                elif stage == 'turn':
                    dve.wait_ge(*T_('A'))
                    for hp, bank in ((0, B0), (1, B1)):
                        last = v.tensor_tensor(AM[:, hp, :, :], bank[:, :].rearrange("p (c t) -> p c t", c=4),
                                               RWM[:, hp, :].unsqueeze(1).broadcast_to([P, 4, P]), ALU.mult)
                    last.then_inc(rw_dve, 1)
                    dve.wait_ge(*V('masked'))
                    eye = I4[:, :].unsqueeze(1).broadcast_to([P, 4, 64])
                    v.tensor_copy(X[:, :, :], eye)
                    link(v.tensor_copy(Y[:, :, :], eye))
                    dve.wait_ge(*T_('N'))
                    v.copy_predicated(X[:, :, :], LM[:, 0, 0, :].unsqueeze(1).broadcast_to([P, 4, 64]),
                                      B2[:, 0:256].rearrange("p (c t) -> p c t", c=4))
                    for hp in range(2):
                        last = v.copy_predicated(Y[HP[hp], :, :],
                                                 LM[HP[hp], 0, 1, :].unsqueeze(1).broadcast_to([64, 4, 64]),
                                                 AM[HP[hp], hp, :, 64 * hp:64 * hp + 64])
                    last.then_inc(rw_dve, 1)
                elif stage[:3] == 'inv':
                    lv = int(stage[3])
                    dve.wait_ge(*T_(f'XY{lv}'))
                    if lv < 5:
                        v.copy_predicated(X[:, :, :], LM[:, lv, 0, :].unsqueeze(1).broadcast_to([P, 4, 64]),
                                          B1[:, 0:256].rearrange("p (c t) -> p c t", c=4))
                    v.copy_predicated(Y[:, :, :], LM[:, lv, 1, :].unsqueeze(1).broadcast_to([P, 4, 64]),
                                      B3[:, 0:256].rearrange("p (c t) -> p c t", c=4)).then_inc(rw_dve, 1)
                elif stage == 'fold':
                    dve.wait_ge(*T_('W1'))
                    v.tensor_copy(W1S[:, :, :].rearrange("p c t -> p (c t)"), B0[:, 0:256]).then_inc(rw_dve, 1)
                elif stage[:3] == 'seq':
                    c = int(stage[3])
                    dve.wait_ge(*T_(f'U{c}'))
                    dve.wait_ge(*V('W1'))
                    for hp in range(2):
                        r = HP[hp]
                        last = v.tensor_tensor(
                            UV[r, c:4:2, 64 * hp:64 * hp + 64], B1[r, 0:P].rearrange("p (j x) -> p j x", j=2),
                            W1S[r, c:4:2, :], ALU.add)
                    last.then_inc(rw_dve, 1)
                    dve.wait_ge(*T_(f'S{c}'))
                    link(v.tensor_tensor(ST[:, :, :], ST[:, :, :], B4[:, 0:P].rearrange("p (j x) -> p j x", j=2),
                                         ALU.add))
                    e = 64 * c + 63
                    v.tensor_tensor(ST[:, :, :], ST[:, :, :], EB[:, :, e:e + 1].broadcast_to([P, 2, 64]),
                                    ALU.mult).then_inc(rw_dve, 1)
                elif stage == 'post':
                    rw_post(BLK, V, T_, A, rw_dve, slice(t0, t0 + BLK), None,
                            B3[:, 0:256].rearrange("p (j t) -> p j t", j=2))

            def rws(s):
                V, T_, A = smp('dve'), smp('pe'), smp('act')
                if s == 0:
                    dve.wait_ge(rw_dve, step(RW_DVE, 'out', NB - 1))
                    rw_mix(NS, PR[:, :, 1 + SEQ:1 + T], SHF[:, :, :]).then_inc(smp_dve, 1)
                    dve.wait_ge(*V('mixed'))
                    rw_kk(NS).then_inc(smp_dve, 1)
                    dve.wait_ge(*T_('ssq'))
                    clamp(NS, BK8[6]).then_inc(smp_dve, 1)
                elif s == 1:
                    dve.wait_ge(*A('rs'))
                    link(v.tensor_tensor(KK[:, :, 0:NS], KK[:, :, 0:NS], RS[:, :, 0:NS], ALU.mult))
                    link(v.tensor_scalar(SG[:, 0:2, 0:NS], SG[:, 0:2, 0:NS], -EXP_M05, None, ALU.mult))
                    rw_keys(NS).then_inc(smp_dve, 1)
                elif s == 2:
                    dve.wait_ge(smp_dma, 7 * 16)
                    dve.wait_ge(smp_dma2, 9 * 16)
                    S = SWK[:, :].rearrange("p (v k) -> p v k", v=16)
                    W = SW1[:, :].rearrange("p (v k) -> p v k", v=16)

                    def key(i):
                        return SWV[:, 64 * i:64 * i + 64].unsqueeze(1).broadcast_to([P, 16, 64])

                    def val(x):
                        return x.unsqueeze(2).broadcast_to([P, 16, 64])

                    sk = T2[:, 0, 0:16]
                    link(v.tensor_tensor(W, S, key(1), ALU.mult))
                    link(v.tensor_reduce(sk, W, AX.X, ALU.add))
                    link(v.tensor_tensor(S, S, key(4), ALU.mult))
                    link(v.tensor_tensor(W, val(sk), key(2), ALU.mult))
                    link(v.tensor_tensor(S, S, W, ALU.subtract))
                    link(v.tensor_tensor(W, val(SWV[:, 320:336]), key(3), ALU.mult))
                    link(v.tensor_tensor(S, S, W, ALU.add))
                    link(v.tensor_tensor(W, S, key(0), ALU.mult))
                    v.tensor_reduce(SWV[:, 0:16], W, AX.X, ALU.add).then_inc(smp_dve, 1)
                elif s == 3:
                    dve.wait_ge(*T_('oturn'))
                    rw_post(NS, V, T_, A, smp_dve, slice(SEQ, T), None,
                            BK8[6][:, 0:16].rearrange("p (j t) -> p j t", j=2))

            def rw_final():
                dve.wait_ge(fin_pe, 1)
                v.tensor_copy(FST[:, :, :].rearrange("v j k -> v (j k)"), BK8[3][0:64, 0:256])
                v.tensor_copy(FSH[:, 0:512], BK8[4][0:9, :])
                v.tensor_copy(FSH[:, 512:896], BK8[5][0:9, 0:384])
                v.tensor_copy(FCV[:, 0:512], BK8[6][0:11, :])
                v.tensor_copy(FCV[:, 512:768], BK8[7][0:11, 0:256]).then_inc(fin_dve, 1)

            for what, arg in PLAN1:
                if what == 'split':
                    split_lo(arg)
                elif what == 'ev':
                    bring_out(arg)
                elif what == 'dt':
                    dve.wait_ge(st_turned, 1)
                    v.tensor_copy(SCV[:, :, :].rearrange("p t c -> p (t c)"), BK8[3][:, 0:144])
                    v.tensor_copy(SHF[:, :, :].rearrange("p t c -> p (t c)"), BK8[3][:, 160:216])
                    link(v.tensor_scalar(OMKA[:, :], par('rw_k_a', 0, 2), -1.0, 1.0, ALU.mult, ALU.add))
                    dve.wait_ge(dt_done, 1)
                    link(v.tensor_copy(DTZ[:, :, :].rearrange("p b h -> p (b h)"), BK8[4][:, 0:72]))
                elif what[:3] == 'rw_' and what != 'rw_final':
                    rw(what[3:], arg)
                elif what == 'rws':
                    rws(arg)
                elif what == 'rw_final':
                    rw_final()
            end_phase(dve, 1)

            def pre():
                for t in range(6):
                    dve.wait_ge(silu_s, t + 1)
                    v.tensor_tensor(MIX[:, t, :], MIX[:, t, :], (SMT, SSM)[t % 2][:, 0:T], ALU.mult).then_inc(silu_m, 1)
                dve.wait_ge(pre_dma, 32)
                link(v.tensor_tensor(DTZ[:, :, :], DTZ[:, :, :], DTB[:, :].unsqueeze(1).broadcast_to([P, 9, 8]), ALU.add))
                v.scalar_tensor_tensor(DTN[:, :, :], DTZ[:, :, :], -1.0, DTZ[:, :, :], ALU.mult, ALU.min).then_inc(
                    pre_dve, 1)
                dve.wait_ge(pre_act, PRE_ACT.index('soft') + 1)
                link(v.scalar_tensor_tensor(DT[:, :, :], DTZ[:, :, :], 0.0, DTE[:, :, :], ALU.max, ALU.add))
                v.scalar_tensor_tensor(DTA[:, :, :], DT[:, :, :], -1.0, AEX[:, :].unsqueeze(1).broadcast_to([P, 9, 8]),
                                       ALU.mult, ALU.mult).then_inc(pre_dve, 1)
                dve.wait_ge(pre_pe, 1)
                link(v.tensor_copy(ACOL[:, :, :].rearrange("p b h -> p (b h)"), BK8[4][:, 0:64]))
                v.tensor_tensor(ES[:, :, :].rearrange("p b h -> p (b h)"), BK8[4][:, 64:128],
                                ACOL[:, :, :].rearrange("p b h -> p (b h)"), ALU.subtract).then_inc(pre_dve, 1)
                dve.wait_ge(pre_act, PRE_ACT.index('ed') + 1)
                for i, src in enumerate((DT, DTE)):
                    v.tensor_copy(DTW[:, i, :, :], src[:, 8, :].unsqueeze(2).broadcast_to([P, 8, 2]))
                for gr in range(2):
                    last = v.tensor_copy(EDG[HP[gr], :, :], ED[HP[gr], :, 4 * gr:4 * gr + 4])
                last.then_inc(pre_dve, 1)
                dve.wait_ge(pre_dve, PRE_DVE.index('twice') + 1)

            def hg_nabs(w):
                f = HB[:, 2:4, 0:w]
                return v.scalar_tensor_tensor(HN[:, :, 0:w], f, -1.0, f, ALU.mult, ALU.min)

            def hg_logf(w):
                f = HB[:, 2:4, 0:w]
                link(v.scalar_tensor_tensor(HF[:, :, 0:w], f, 0.0, HL[:, :, 0:w], ALU.min, ALU.subtract))
                return v.tensor_tensor(HK[:, :, 0:w], HF[:, :, 0:w], f, ALU.subtract)

            def hg_out(w, cols, s):
                link(v.tensor_tensor(HO[:, :, 0:w], HO[:, :, 0:w], HR[:, :, 0:w], ALU.mult))
                for j in range(2):
                    last = v.scalar_tensor_tensor(MIX[:, j, cols], HO[:, j, 0:w], par('hg_norm_g', j), MIX[:, j, cols],
                                                  ALU.mult, ALU.mult)
                last.then_inc(s, 1)

            def hg(stage, b):
                def V(name):
                    return hg_dve, step(HG_DVE, name, b)

                def T_(name):
                    return hg_pe, step(HG_PE, name, b)

                def A(name):
                    return hg_act, step(HG_ACT, name, b)

                H0, H1, H2, H3 = BK8[0:4]
                if stage == 'gate':
                    dve.wait_ge(hg_loaded, 16 * (b + 1))
                    hg_nabs(BLK).then_inc(hg_dve, 1)
                    dve.wait_ge(*A('soft'))
                    hg_logf(BLK).then_inc(hg_dve, 1)
                    dve.wait_ge(*V('logf'))
                    for j in range(2):
                        link(v.tensor_tensor_scan(HBb[:, j, :], CM32[:, :], HF[:, j, :], 0.0, ALU.mult, ALU.add))
                    cum = HBb[:, :, :].rearrange("p j t -> p (j t)")
                    for lv, n in enumerate(HLEV):
                        x = cum.rearrange("p (b e r) -> p b e r", e=2, r=n)
                        d = HD[:, lv, :, :].rearrange("p j t -> p (j t)").rearrange("p (b e r) -> p b e r", e=2, r=n)
                        nb = 2 * BLK // (2 * n)
                        ref = x[:, :, 0, n - 1:n].broadcast_to([P, nb, n])
                        v.tensor_tensor(d[:, :, 0, :], ref, x[:, :, 0, :], ALU.subtract)
                        v.tensor_tensor(d[:, :, 1, :], x[:, :, 1, :], ref, ALU.subtract)
                    x = cum.rearrange("p (b r) -> p b r", r=32)
                    v.tensor_tensor(HD[:, 5, :, :].rearrange("p j t -> p (j t)").rearrange("p (b r) -> p b r", r=32),
                                    x[:, :, 31:32].broadcast_to([P, 8, 32]), x, ALU.subtract).then_inc(hg_dve, 1)
                elif stage == 'levels':
                    dve.wait_ge(*A('exps'))
                    q = HB[:, 0:2, :].rearrange("p j t -> p (j t)")
                    k = HK[:, :, :].rearrange("p j t -> p (j t)")
                    for lv, n in enumerate(HLEV):
                        d = HD[:, lv, :, :].rearrange("p j t -> p (j t)").rearrange("p (b e r) -> p b e r", e=2, r=n)
                        for e, src in ((0, k), (1, q)):
                            v.tensor_tensor(d[:, :, e, :], d[:, :, e, :],
                                            src.rearrange("p (b e r) -> p b e r", e=2, r=n)[:, :, e, :], ALU.mult)
                    v.tensor_tensor(HD[:, 5, :, :], HD[:, 5, :, :], HK[:, :, :], ALU.mult)
                    v.tensor_tensor(HQ[:, :, :], HB[:, 0:2, :], HX[:, :, :], ALU.mult).then_inc(hg_dve, 1)
                elif stage == 'att':
                    dve.wait_ge(*T_('att'))
                    mask = HMK[:, :, :].unsqueeze(2).broadcast_to([P, 6, 2, 32])
                    for hp, bank in ((0, H1), (1, H2)):
                        last = v.tensor_tensor(HAS[:, hp, :, :, :],
                                               bank[:, 0:384].rearrange("p (l j t) -> p l j t", l=6, j=2), mask, ALU.mult)
                    last.then_inc(hg_dve, 1)
                    dve.wait_ge(*V('masked'))
                    for hp in range(2):
                        last = v.tensor_reduce(HAT[:, 2 * hp:2 * hp + 2, :].rearrange("p j t -> p (j t)"),
                                               HAS[:, hp, :, :, :].rearrange("p l j t -> p (j t) l"), AX.X, ALU.add)
                    link(last)
                    if b == 0:
                        dve.wait_ge(pre_pool, 1)
                    for s in range(4):
                        t = slice(32 * s, 32 * s + 32)
                        last = v.tensor_copy(HAD[t, :, t], HAT[t, :, :])
                    last.then_inc(hg_dve, 1)
                elif stage == 'state':
                    link(v.tensor_copy(HSH[:, 0, :, :], HSH[:, 4, :, :]))
                    dve.wait_ge(*T_('u'))
                    for s in range(4):
                        for j in range(2):
                            e = 32 * s + 31
                            last = v.scalar_tensor_tensor(HSH[:, s + 1, j, :], HSH[:, s, j, :], HX[:, j, e:e + 1],
                                                          H0[:, j * 256 + 64 * s:j * 256 + 64 * s + 64], ALU.mult, ALU.add)
                        if s < 3:
                            link(last)
                    last.then_inc(hg_dve, 1)
                elif stage == 'post':
                    dve.wait_ge(*T_('o'))
                    v.tensor_copy(HO[:, :, :].rearrange("p j t -> p (j t)"), H3[:, 0:256]).then_inc(hg_dve, 1)
                    dve.wait_ge(*V('o'))
                    v.tensor_tensor(HT[:, :, :], HO[:, :, :], HO[:, :, :], ALU.mult).then_inc(hg_dve, 1)
                    dve.wait_ge(*A('rs'))
                    hg_out(BLK, slice(b * BLK, (b + 1) * BLK), hg_dve)
                    dve.wait_ge(*V('out'))
                    x_half(9 + b, XT)

            def mb_silu_(b):
                w = BLK if b < NB else NS
                dve.wait_ge(mb_sig, b + 1)
                v.tensor_tensor(XB[:, :, 0:w], XB[:, :, 0:w], MM[:, 0:6, 0:w], ALU.mult).then_inc(mb_silu, 1)

            def mb_skip(w, ybank):
                for t in range(4):
                    last = v.scalar_tensor_tensor(YS[:, t, 0:w], XB[:, t, 0:w], par('mb_D', t), ybank(t), ALU.mult,
                                                  ALU.add)
                return last

            def mb_out(w, cols, s):
                for t in range(4):
                    last = v.scalar_tensor_tensor(MIX[:, 2 + t, cols], YS[:, t, 0:w], par('mb_norm_g', t),
                                                  RM[:, t // 2, 0:w], ALU.mult, ALU.mult)
                last.then_inc(s, 1)

            def mb(stage, b):
                def V(name):
                    return mb_dve, step(MB_DVE, name, b)

                def T_(name):
                    return mb_pe, step(MB_PE, name, b)

                def A(name):
                    return mb_act, step(MB_ACT, name, b)

                M0, M1, M2, M3 = BK8[4:8]
                cols = slice(b * BLK, (b + 1) * BLK)
                if stage == 'turn':
                    mb_silu_(b)
                    dve.wait_ge(*T_('turned'))
                    v.tensor_tensor(XD[:, :, :], M0[:, :].rearrange("p (h x) -> p h x", h=8),
                                    DT[:, b, :].unsqueeze(2).broadcast_to([P, 8, 64]), ALU.mult).then_inc(mb_dve, 1)
                    v.tensor_copy(BT[:, :], M1[:, 0:P])
                    v.tensor_tensor(CBM[:, 0, :], M1[:, P:2 * P], triu[:, :], ALU.mult)
                    v.tensor_tensor(CBM[:, 1, :], M2[:, 0:P], triu[:, :], ALU.mult).then_inc(mb_dve, 1)
                elif stage == 'decay':
                    dve.wait_ge(*A('E2'))
                    for h in range(8):
                        last = v.tensor_scalar(SEG[:, h, :], (M2, M3)[h // 4][:, (h % 4) * P:(h % 4 + 1) * P],
                                               ACOL[:, b, h:h + 1], 0.0, ALU.subtract, ALU.min)
                    last.then_inc(mb_dve, 1)
                    dve.wait_ge(*A('L'))
                    for gr in range(2):
                        last = v.tensor_tensor(MM[:, 4 * gr:4 * gr + 4, :], SEG[:, 4 * gr:4 * gr + 4, :],
                                               CBM[:, gr, :].unsqueeze(1).broadcast_to([P, 4, P]), ALU.mult)
                    last.then_inc(mb_dve, 1)
                elif stage == 'prod':
                    dve.wait_ge(*T_('y'))
                    mb_skip(BLK, lambda t: (M1, M2)[t // 2][:, (t % 2) * P:(t % 2 + 1) * P]).then_inc(mb_dve, 1)
                    dve.wait_ge(*T_('S'))
                    link(v.tensor_tensor(STt[:, :, :], STt[:, :, :], EDG[:, b, :].unsqueeze(2).broadcast_to([P, 4, 64]),
                                         ALU.mult))
                    v.tensor_tensor(STt[:, :, :], STt[:, :, :], M0[:, 0:256].rearrange("p (h x) -> p h x", h=4),
                                    ALU.add).then_inc(mb_dve, 1)
                    dve.wait_ge(*V('y'))
                    v.tensor_tensor(YS[:, :, :], YS[:, :, :], MIX[:, 2:6, cols], ALU.mult).then_inc(mb_dve, 1)
                elif stage == 'post':
                    dve.wait_ge(*A('rs'))
                    mb_out(BLK, cols, mb_dve)

            def hgs():
                dve.wait_ge(hg_loaded, 16 * (NB + 1))
                hg_nabs(NS).then_inc(hs_dve, 1)
                dve.wait_ge(hs_act, HS_ACT.index('soft') + 1)
                hg_logf(NS).then_inc(hs_dve, 1)
                dve.wait_ge(hs_dma, 32)
                dve.wait_ge(hs_dma2, 11 * 16)
                S = SHG[:, :].rearrange("p (k v) -> p k v", k=16)
                W = SHT2[:, :].rearrange("p (k v) -> p k v", k=16)

                def key(i):
                    return SV1[:, 16 * i:16 * i + 16].unsqueeze(2).broadcast_to([P, 16, 64])

                link(v.tensor_tensor(S, S, key(1), ALU.mult))
                link(v.tensor_tensor(W, SV1[:, 64:128].unsqueeze(1).broadcast_to([P, 16, 64]), key(2), ALU.mult))
                v.tensor_tensor(S, S, W, ALU.add).then_inc(hs_dve, 1)
                dve.wait_ge(hs_dve, HS_DVE.index('state') + 1)
                link(v.tensor_tensor(W, S, key(0), ALU.mult))
                v.tensor_reduce(SO[:, :], W.rearrange("p k v -> p v k"), AX.X, ALU.add).then_inc(hs_dve, 1)
                dve.wait_ge(hs_pe, 2)
                v.tensor_copy(SO2[:, :], BK8[2][0:32, 0:64]).then_inc(hs_dve, 1)
                dve.wait_ge(hs_pe, 3)
                link(v.tensor_copy(HO[:, :, 0:NS], BK8[3][:, 0:16].rearrange("p (j t) -> p j t", j=2)))
                v.tensor_tensor(HT[:, :, 0:NS], HO[:, :, 0:NS], HO[:, :, 0:NS], ALU.mult).then_inc(hs_dve, 1)
                dve.wait_ge(hs_act, HS_ACT.index('rs') + 1)
                hg_out(NS, slice(SEQ, T), hs_dve)

            def mbs():
                dve.wait_ge(ms_dma, 16 * 6)
                dve.wait_ge(ms_dma2, 11 * 16)
                S = SSM[:, :].rearrange("p (x n) -> p x n", x=32)
                W = SMT[:, :].rearrange("p (x n) -> p x n", x=32)
                link(v.tensor_scalar(SV2[:, 128:160], SV2[:, 128:160], SV2[:, 160:161], None, ALU.mult))
                link(v.tensor_scalar(SSM[:, :], SSM[:, :], SV2[:, 161:162], None, ALU.mult))
                link(v.tensor_tensor(W, SV2[:, 128:160].unsqueeze(2).broadcast_to([P, 32, 64]),
                                     SV2[:, 0:64].unsqueeze(1).broadcast_to([P, 32, 64]), ALU.mult))
                link(v.tensor_tensor(S, S, W, ALU.add))
                link(v.tensor_tensor(W, S, SV2[:, 64:128].unsqueeze(1).broadcast_to([P, 32, 64]), ALU.mult))
                v.tensor_reduce(SV1[:, 0:32], W, AX.X, ALU.add).then_inc(ms_dve, 1)
                dve.wait_ge(ms_pe, 2)
                link(mb_skip(NS, lambda t: BK8[6][:, 8 * t:8 * t + 8]))
                v.tensor_tensor(YS[:, :, 0:NS], YS[:, :, 0:NS], MIX[:, 2:6, SEQ:T], ALU.mult).then_inc(ms_dve, 1)
                dve.wait_ge(ms_act, MS_ACT.index('rs') + 1)
                mb_out(NS, slice(SEQ, T), ms_dve)

            for what, arg in PLAN2:
                if what == 'pre':
                    pre()
                elif what[:3] == 'hg_':
                    hg(what[3:], arg)
                elif what[:3] == 'mb_':
                    mb(what[3:], arg)
                elif what == 'hgs':
                    x_half(17, XT)
                    hgs()
                elif what == 'mbs':
                    mb_silu_(NB)
                    mbs()
                else:
                    dve.wait_ge(fin_pe, 2)
                    v.tensor_copy(STF[:, :, :].rearrange("p a x -> p (a x)"), BK8[0][:, 0:256]).then_inc(fin_dve, 1)
            end_phase(dve, 2)

            def gu_rest(n):
                u, c = QUANTA[UPS[n]]
                f = UNITS[u][1]
                cols = slice(c * CH, (c + 1) * CH)
                t = TILE_IN_GROUP[f]
                dve.wait_ge(gu_hi, n + 1)
                v.tensor_tensor(GLO[:, t, cols], GU[n % 2][:, :], GHI[:, t, cols].bitcast(F32), ALU.subtract).then_inc(
                    gu_lo, 1)

            for what, arg in PLAN3:
                if what == 'split':
                    split_lo(arg)
                elif what == 'ev':
                    bring_out(arg)
                    if arg in UPS:
                        gu_rest(UPS.index(arg))
                elif what == 'mixsplit':
                    cols = slice(arg * CH, (arg + 1) * CH)
                    dve.wait_ge(mix_hi, arg + 1)
                    v.tensor_tensor(MLO[:, :, cols], MIX[:, :, cols], MHI[:, :, cols].bitcast(F32),
                                    ALU.subtract).then_inc(mix_lo, 1)
                elif what == 'norm':
                    norm_squares(arg)
                    if arg < 6:
                        if arg == 3:
                            modulation(32, 'g_norm2')
                        modulated(arg, XT, 24)
                    else:
                        cols = slice((arg - 6) * CH, (arg - 5) * CH)
                        dve.wait_ge(n_rs, arg + 1)
                        for k in range(KT):
                            last = v.scalar_tensor_tensor(XT[:, k, cols], XT[:, k, cols], par('g_final', k), RB3[:, :],
                                                          ALU.mult, ALU.mult)
                        last.then_inc(n_h, 1)
            for i in range(9):
                n = BLK if i < NB else NS
                dve.wait_ge(y_turned, i + 1)
                if i >= 2:
                    dve.wait_ge(y_out[i % 2], 16 * (i // 2))
                v.tensor_copy(OT[i % 2][0:n, 512:D], BK8[2 * (i % 2) + 1][0:n, :]).then_inc(y_dve, 1)


def kernel(**inputs):
    import numpy as np
    import concourse.bacc as bacc
    from concourse.bass_utils import run_bass_kernel_spmd

    nc = bacc.Bacc("TRN2", target_bir_lowering=False, num_devices=1)
    arrays, args = {}, []
    for name in IN_NAMES:
        arr = np.ascontiguousarray(inputs[name])
        arrays[f"in_{name}"] = arr
        args.append(nc.dram_tensor(f"in_{name}", arr.shape, mybir.dt.from_np(arr.dtype), kind="ExternalInput").ap())
    outs = [nc.dram_tensor(f"out_{i}", s, F32, kind="ExternalOutput").ap() for i, s in enumerate(OUT_SHAPES)]
    kernel_program(nc, args, outs)
    res = run_bass_kernel_spmd(nc, [arrays], core_ids=[0]).results[0]
    return tuple(res[f"out_{i}"] for i in range(len(OUT_SHAPES)))
```

```python
from contextlib import ExitStack

import concourse.bass as bass
from concourse import mybir

F32 = mybir.dt.float32
F32R = mybir.dt.float32r
ALU = mybir.AluOpType
ACT = mybir.ActivationFunctionType
AX = mybir.AxisListType

P = 128
D = 1024
KT = D // P
SEQ = 1024
NS = 8
T = SEQ + NS
NCH = 3
CH = T // NCH
BLK = 128
NB = SEQ // BLK
HG0, MZ0, MX0, DT0, RW0 = 0, 1024, 1536, 2304, 2312
RW_DIM = 896
CONV_DIM = 768
FF = 2816
GROUPS = [6, 6, 5, 5]
MAXG = max(GROUPS)
RMS_EPS = 1e-6
GN_EPS = 64e-5
EXP_M05 = 0.6065306597126334
LN2 = 0.6931471805599453
LEVELS = [1, 2, 4, 8, 16, 32]
HLEV = [1, 2, 4, 8, 16]

IN_NAMES = ['x_prompt', 'x_sample', 'state_hgrn', 'state_ssm', 'state_conv', 'state_wkv', 'state_shift', 'c_prompt',
            'c_sample', 'w_ada', 'b_ada', 'g_norm1', 'w_in', 'hg_norm_g', 'mb_conv_w', 'mb_conv_b',
            'mb_dt_bias', 'mb_A_log', 'mb_D', 'mb_norm_g', 'rw_mu', 'rw_w0', 'rw_w2', 'rw_a0', 'rw_a2', 'rw_g2',
            'rw_k_k', 'rw_k_a', 'rw_r_k', 'rw_ln_g', 'rw_ln_b', 'w_out', 'g_norm2', 'w_gate', 'w_up', 'w_down',
            'g_final']
OUT_SHAPES = [(1, SEQ, D), (NS, 1, D), (1, 1, 4, 64, 64), (1, NS, 4, 64, 64), (1, 1, 8, 64, 64), (1, NS, 8, 64, 64),
              (1, 1, 3, CONV_DIM), (1, NS, 3, CONV_DIM), (1, 1, 4, 64, 64), (1, NS, 4, 64, 64), (1, 1, RW_DIM),
              (1, NS, RW_DIM)]

ROWS1 = [('b_ada', 48), ('g_norm1', 8), ('g_norm2', 8), ('g_final', 8), ('mb_conv_w', 24), ('mb_conv_b', 6)]
ROWS2 = [('rw_mu', 7), ('rw_w0', 2), ('rw_a0', 2), ('rw_k_k', 2), ('rw_k_a', 2), ('rw_r_k', 2), ('rw_ln_g', 2),
         ('rw_ln_b', 2), ('hg_norm_g', 2), ('mb_norm_g', 4)]
COL = {}
for _name, _n in ROWS1 + ROWS2:
    COL[_name] = sum(n for _, n in (ROWS1 + ROWS2)[:len(COL)])
NR1 = sum(n for _, n in ROWS1)
NR2 = sum(n for _, n in ROWS2)
COL['mb_D'] = NR1 + NR2

RWF_DVE = ['mixed', 'squared', 'clamped', 'decays', 'operands', 'bonus']
RWF_PE = ['lora', 'bonus']
RWF_ACT = ['lora_in', 'gates', 'rs', 'exps']
RW_DVE = ['masked', 'inv0', 'inv1', 'inv2', 'inv3', 'inv4', 'inv5', 'W1', 'U0', 'S0', 'U1', 'S1', 'o', 'centred', 'out']
RW_PE = ['turned', 'A', 'N', 'vturned', 'P1', 'XY1', 'P2', 'XY2', 'P3', 'XY3', 'P4', 'XY4', 'P5', 'XY5', 'T1',
         'PT', 'W1', 'U0', 'S0', 'U1', 'S1', 'mean', 'var']
RW_ACT = ['turned', 'vturned', 'P1', 'P2', 'P3', 'P4', 'P5', 'T1', 'PT', 'var']
HGF_DVE = ['nabs', 'logf', 'diffs', 'factors']
HGF_ACT = ['soft', 'k', 'exps']
HG_DVE = ['masked', 'att', 'S', 'o', 'squared', 'out']
HG_PE = ['turned', 'att', 'u', 'o', 'ssq']
HG_ACT = ['turned', 'v', 'rs']
MBF_DVE = ['xdt', 'cb']
MB_DVE = ['seg', 'm', 'y', 'S', 'z', 'out']
MB_PE = ['acum', 'y', 'S', 'ssq']
MB_ACT = ['E2', 'L', 'squared', 'rs']
MB_POOL = ['xdte', 'ce']
PRE_DVE = ['nabs', 'dta', 'es', 'twice']
PRE_ACT = ['aexp', 'soft', 'dtexp', 'ed']
SMP_DVE = ['mixed', 'squared', 'clamped', 'vectors', 'bonus', 'state', 'o', 'centred', 'out']
SMP_PE = ['lora', 'tok', 'bonus', 'oturn', 'mean', 'var']
SMP_ACT = ['lora_in', 'gates', 'rs', 'wexp', 'tok', 'var']
HS_DVE = ['nabs', 'logf', 'state', 'opart', 'osum', 'squared', 'out']
HS_ACT = ['soft', 'vectors', 'tok', 'rs']
MS_DVE = ['y', 'z', 'out']
MS_ACT = ['tok', 'squared', 'rs']


def step(steps, name, b=0):
    return b * len(steps) + steps.index(name) + 1



def dense_plan():
    ada = [('ada', (a, s)) for a in range(12) for s in range(4)]
    rw = [('rw', t) for t in range(7)] + [('dt', 0)]
    mb = [('z', t) for t in range(4)] + [('xbc', t) for t in range(6)]
    hg = [('hgg', t) for t in range(2)] + [('hg', t) for t in range(6)]
    units = ada[:16] + rw + mb + hg + ada[16:]
    n1 = len(units)
    units += [('out', t) for t in range(8)]
    f = 0
    for g, n in enumerate(GROUPS):
        for i in range(n):
            units += [('gate', f), ('up', f)]
            f += 1
        units += [('down', (g, d)) for d in range(KT)]
    return units, n1


def kernel_program(nc, ins, outs):
    (y_p, y_s, hg_p, hg_s, ssm_p, ssm_s, conv_p, conv_s, wkv_p, wkv_s, shift_p, shift_s) = outs
    (x_prompt, x_sample, state_hgrn, state_ssm, state_conv, state_wkv, state_shift, c_prompt, c_sample, w_ada, b_ada,
     g_norm1, w_in, hg_norm_g, mb_conv_w, mb_conv_b, mb_dt_bias, mb_A_log, mb_D, mb_norm_g, rw_mu, rw_w0, rw_w2, rw_a0,
     rw_a2, rw_g2, rw_k_k, rw_k_a, rw_r_k, rw_ln_g, rw_ln_b, w_out, g_norm2, w_gate, w_up, w_down, g_final) = ins

    def rows(x):
        return x.rearrange("o (a p) -> (o a) p", p=P)

    param_rows = {
        'b_ada': rows(b_ada), 'g_norm1': rows(g_norm1), 'g_norm2': rows(g_norm2),
        'g_final': g_final.rearrange("(a p) -> a p", p=P),
        'mb_conv_w': mb_conv_w.rearrange("o j (a p) -> (o j a) p", p=P), 'mb_conv_b': rows(mb_conv_b),
        'rw_mu': rows(rw_mu), 'rw_w0': rows(rw_w0), 'rw_a0': rows(rw_a0), 'rw_k_k': rows(rw_k_k),
        'rw_k_a': rows(rw_k_a), 'rw_r_k': rw_r_k.rearrange("o (a h) k -> (o a) (h k)", h=2), 'rw_ln_g': rows(rw_ln_g),
        'rw_ln_b': rows(rw_ln_b), 'hg_norm_g': rows(hg_norm_g), 'mb_norm_g': rows(mb_norm_g)}
    UNITS, N1 = dense_plan()
    QUANTA, FIRSTQ, LASTQ = [], {}, {}
    u = 0
    while u < len(UNITS):
        kind = UNITS[u][0]
        FIRSTQ[u] = len(QUANTA)
        if kind == 'ada':
            QUANTA.append((u, 0))
        elif kind == 'gate' or UNITS[u] in (('out', KT - 2), ('down', (len(GROUPS) - 1, KT - 2))):
            FIRSTQ[u + 1] = len(QUANTA) + 1
            for c in range(NCH):
                QUANTA += [(u, c), (u + 1, c)]
            LASTQ[u] = len(QUANTA) - 2
            LASTQ[u + 1] = len(QUANTA) - 1
            u += 2
            continue
        else:
            QUANTA += [(u, c) for c in range(NCH)]
        LASTQ[u] = len(QUANTA) - 1
        u += 1
    SPLIT = [u for u, (k, _) in enumerate(UNITS) if k != 'ada']
    SIDX = {u: i for i, u in enumerate(SPLIT)}
    QP1 = LASTQ[SPLIT[sum(u < N1 for u in SPLIT) - 1]] + 1
    QP2 = LASTQ[N1 - 1] + 1
    NRAW, NSPL1, NSPL3 = 3, 2, 4

    BANK, PREV = [], []
    last_use = {}
    for q, (u, c) in enumerate(QUANTA):
        kind, arg = UNITS[u]
        if q < QP1:
            b = arg[0] % 2 if kind == 'ada' else q % 2
        else:
            b = 3 if q < QP2 else q % 7
        BANK.append(b)
        PREV.append(last_use.get(b) if kind != 'ada' or arg[1] == 0 else None)
        last_use[b] = q

    def evac_engine(q):
        kind = UNITS[QUANTA[q][0]][0]
        return 'dve' if kind in ('out', 'up', 'down') else 'ada' if kind == 'ada' else 'act'

    EV = {'act': [], 'dve': [], 'ada': []}
    for q, (u, _) in enumerate(QUANTA):
        if UNITS[u][0] != 'ada' or UNITS[u][1][1] == 3:
            EV[evac_engine(q)].append(q)
    EVN = {q: i + 1 for e in EV for i, q in enumerate(EV[e])}
    GATES = [q for q, (u, _) in enumerate(QUANTA) if UNITS[u][0] == 'gate']
    UPS = [q for q, (u, _) in enumerate(QUANTA) if UNITS[u][0] == 'up']
    STAGED = [q for q, (u, _) in enumerate(QUANTA) if UNITS[u][0] in ('xbc', 'hg')]
    SQUARED = [q for q, (u, _) in enumerate(QUANTA)
               if UNITS[u][0] == 'out' or (UNITS[u][0] == 'down' and UNITS[u][1][0] == len(GROUPS) - 1)]
    TILE_IN_GROUP = [i for n in GROUPS for i in range(n)]

    ctx = ExitStack()
    with ctx:
        def sem(name):
            return ctx.enter_context(nc.semaphore(name))

        lo = nc.sbuf_base
        hi = nc.sbuf_usable_end

        class Region:

            def __init__(self, base, limit):
                self.at, self.limit = -(-base // 64) * 64, limit

            def t(self, name, shape, dtype=F32):
                n = 4
                for s in shape[1:]:
                    n *= s
                self.at = -(-self.at // 32) * 32
                out = nc.alloc_sbuf_tensor_at(name, shape, dtype, offset=self.at)
                self.at += n
                assert self.at <= self.limit, (name, self.at, self.limit)
                return out

        keep = Region(lo, hi)
        ident = keep.t("ident", [P, P])
        ones = keep.t("ones", [P, P])
        headsum = keep.t("headsum", [P, P])
        triu = keep.t("triu", [P, P])
        PAR = keep.t("PAR", [P, NR1 + NR2 + 4])
        CST = keep.t("CST", [P, 4])
        MOD = keep.t("MOD", [P, 48, 9])
        A1 = keep.t("A1", [P, KT, 9])
        CT = keep.t("CT", [P, KT, 9])
        DTZ = keep.t("DTZ", [P, 9, 8])
        HMK = keep.t("HMK", [P, 6, 32])
        CM32 = keep.t("CM32", [P, BLK])
        G4 = keep.t("G4", [P, 32])
        RAW = [keep.t(f"RAW{i}", [P, KT, P]) for i in range(NRAW)]
        TMP8 = keep.t("TMP8", [P, NS])
        h_at = keep.at
        hreg = Region(h_at, hi)
        HHI = hreg.t("HHI", [P, KT, T], F32R)
        HLO = hreg.t("HLO", [P, KT, T], F32R)
        h_end = hreg.at
        p1 = Region(h_end, hi)
        WHI1 = [p1.t(f"WHI1_{i}", [P, KT, P], F32R) for i in range(NSPL1)]
        WLO1 = [p1.t(f"WLO1_{i}", [P, KT, P], F32R) for i in range(NSPL1)]
        MIX = p1.t("MIX", [P, KT, T])
        mix_end = p1.at
        p0 = Region(mix_end, hi)
        XT0 = p0.t("XT0", [P, KT, T])
        XTOK = [p0.t(f"XTOK_{i}", [P, D]) for i in range(2)]
        PV = p0.t("PV", [P, 2, P])
        BIG = p0.t("BIG", [P, P])
        DHEAD = p0.t("DHEAD", [P, 8])
        ADT0 = p0.t("ADT0", [9, 512])
        p0b = Region(mix_end - 4 * KT * T, mix_end)
        H1 = [p0b.t(f"H1_{i}", [P, KT, CH]) for i in range(2)]
        SS1 = [p0b.t(f"SS1_{i}", [P, CH]) for i in range(NCH)]
        RB1 = [p0b.t(f"RB1_{i}", [P, CH]) for i in range(NCH)]
        SQ = p0.t("SQ", [P, KT, CH])
        C9 = p0.t("C9", [9, 2, D])
        MX = p1.t("MX", [P, 7, BLK])
        LA = p1.t("LA", [P, 3, BLK])
        SG = p1.t("SG", [P, 4, BLK])
        GT2 = [p1.t(f"GT{i}", [P, 2, BLK]) for i in range(2)]
        KK = p1.t("KK", [P, 2, BLK])
        T2 = p1.t("T2", [P, 2, BLK])
        RS = p1.t("RS", [P, 2, BLK])
        BB = p1.t("BB", [P, 2, BLK])
        BM = p1.t("BM", [P, 2, BLK])
        EB = p1.t("EB", [P, 2, BLK])
        ENB = p1.t("ENB", [P, 2, BLK])
        KP = p1.t("KP", [P, 2, BLK])
        pr_at = -(-p1.at // 32) * 32
        PR = p1.t("PR", [P, 7, T + 1])
        arr_at = p1.at
        AR = p1.t("AR", [P, 4, 2, 64])
        bk_at = p1.at
        BK = p1.t("BK", [P, 4, 2, 64])
        OS = Region(bk_at, p1.at).t("OS", [P, 2, BLK])
        OSQ = Region(bk_at + 8 * BLK, p1.at).t("OSQ", [P, 2, BLK])
        BON, RSV = ENB, EB
        vz_at = p1.at
        VZ = p1.t("VZ", [P, 4, 2, 64])
        ar_at = p1.at
        ARt = p1.t("ARt", [P, 4, P])
        BKt = p1.t("BKt", [P, 4, P])
        UV = p1.t("UV", [P, 4, P])
        AM = p1.t("AM", [P, 2, 4, P])
        X = p1.t("X", [P, 4, 64])
        Y = p1.t("Y", [P, 4, 64])
        PS = p1.t("PS", [P, 4, 64])
        ar_end = p1.at
        T1S, PTS, W1S = PS, X, PS
        sgt = Region(ar_at + 4 * (6 * 256 + 1024), ar_end)
        SGT = [sgt.t(f"SGT{i}", [P, CH]) for i in range(2)]
        ST = p1.t("ST", [P, 2, 64])
        RWM = p1.t("RWM", [P, 2, P])
        LM = p1.t("LM", [P, 6, 2, 64], mybir.dt.int8)
        I4 = p1.t("I4", [P, 64])
        CM64 = p1.t("CM64", [P, BLK])
        WL = p1.t("WL", [P, 256])
        SHF = p1.t("SHF", [P, 7, NS])
        SCV = p1.t("SCV", [P, 6, 24])
        OMKA = p1.t("OMKA", [P, 2])
        XL = p1.t("XL", [P, 6, 11])
        STG = [p1.t(f"STG{i}", [P, 3 + CH]) for i in range(2)]
        ACC = [p1.t(f"ACC{i}", [P, CH]) for i in range(1)]
        sreg = Region(ar_at, ar_end)
        SCT = Region(ar_at, ar_end).t("SCT", [3 * NS, CONV_DIM])
        SHT = Region(ar_at + 4 * CONV_DIM, ar_end).t("SHT", [NS, RW_DIM])
        DTF = Region(ar_at + 4 * (CONV_DIM + RW_DIM), ar_end).t("DTF", [8, T])
        STKW = sreg.t("STKW", [NS, 6 * 256])
        SWK = sreg.t("SWK", [P, 1024])
        SW1 = Region(arr_at, vz_at).t("SW1", [P, 1024])
        SWV = Region(vz_at, ar_at).t("SWV", [P, 336])
        FST, FSH, FCV = [nc.alloc_sbuf_tensor_at(n, shape, F32, offset=-(-(pr_at + 4 * t * (T + 1)) // 32) * 32)
                         for t, (n, shape) in enumerate((("FST", [64, 2, P]), ("FSH", [9, RW_DIM]),
                                                         ("FCV", [11, CONV_DIM])))]
        r2 = Region(h_at, h_end)
        HB2 = [r2.t(f"HB{i}", [P, 6, BLK]) for i in range(2)]
        HN = r2.t("HN", [P, 2, BLK])
        HE = r2.t("HE", [P, 2, BLK])
        HL = r2.t("HL", [P, 2, BLK])
        HF = r2.t("HF", [P, 2, BLK])
        HK = r2.t("HK", [P, 2, BLK])
        HBb = r2.t("HBb", [P, 2, BLK])
        HD = r2.t("HD", [P, 6, 2, BLK])
        HX2 = [r2.t(f"HX{i}", [P, 2, BLK]) for i in range(2)]
        HQ = r2.t("HQ", [P, 2, BLK])
        HVT = r2.t("HVT", [P, 2, BLK])
        HKT = r2.t("HKT", [P, 2, BLK])
        HAS = r2.t("HAS", [P, 2, 6, 2, 32])
        HAT = r2.t("HAT", [P, 4, 32])
        HAD = r2.t("HAD", [P, 4, BLK])
        HVD = r2.t("HVD", [P, 2, 4, BLK])
        HSH = r2.t("HSH", [P, 5, 2, 64])
        HO = r2.t("HO", [P, 2, BLK])
        HT = r2.t("HT", [P, 2, BLK])
        HR = r2.t("HR", [P, 2, BLK])
        XD = r2.t("XD", [P, 8, 64])
        XDE = r2.t("XDE", [P, 8, 64])
        BT = r2.t("BT", [P, P])
        CBM = r2.t("CBM", [P, 2, P])
        SEG = r2.t("SEG", [P, 8, P])
        MM = r2.t("MM", [P, 8, P])
        E2 = r2.t("E2", [P, 4, P])
        CE = r2.t("CE", [P, 4, P])
        STt = r2.t("STt", [P, 4, 64])
        YS = r2.t("YS", [P, 4, BLK])
        T4 = r2.t("T4", [P, 4, BLK])
        RM = r2.t("RM", [P, 2, BLK])
        DT = r2.t("DT", [P, 9, 8])
        DTA = r2.t("DTA", [P, 9, 8])
        DTN = r2.t("DTN", [P, 9, 8])
        DTE = r2.t("DTE", [P, 9, 8])
        ACOL = r2.t("ACOL", [P, 8, 8])
        ES = r2.t("ES", [P, 8, 8])
        ED = r2.t("ED", [P, 8, 8])
        EDG = r2.t("EDG", [P, 8, 4])
        DTW = r2.t("DTW", [P, 2, 8, 2])
        DTB = r2.t("DTB", [P, 8])
        AEX = r2.t("AEX", [P, 8])
        r2b = Region(mix_end, hi)
        XT = r2b.t("XT", [P, KT, T])
        XTOK2 = [r2b.t(f"XTOK2_{i}", [P, D]) for i in range(2)]
        SHG = r2b.t("SHG", [P, 1024])
        SHT2 = r2b.t("SHT2", [P, 1024])
        STMP = Region(r2b.at - 4 * 2048, r2b.at).t("STMP", [P, 2048])
        SMT = r2b.t("SMT", [P, 2048])
        xb_at = r2b.at
        SSM = r2b.t("SSM", [P, 2048])
        STK = r2b.t("STK", [NS, 1024])
        r2b.t("XPAD", [P, 3 * T - 3072])
        xr1, xr2 = Region(h_end, mix_end - 4 * KT * T), Region(xb_at, r2b.at)
        XB = [(xr1 if t < 3 else xr2).t(f"XB{t}", [P, T]) for t in range(6)]
        XBS = r2b.t("XBS", [P, 6, NS])
        SV1 = r2b.t("SV1", [P, 128])
        SV2 = r2b.t("SV2", [P, 192])
        SO = r2b.t("SO", [P, 64])
        SO2 = r2b.t("SO2", [32, 64])
        SY = r2b.t("SY", [P, 32])
        STF = r2b.t("STF", [P, 2, P])
        stoken_at = r2b.at
        STOKEN = r2b.t("STOKEN", [NS, 768])
        ADT2 = Region(stoken_at, r2b.at).t("ADT2", [9, 512])
        r3 = Region(h_at, h_end)
        MHI = r3.t("MHI", [P, KT, T], F32R)
        MLO = r3.t("MLO", [P, KT, T], F32R)
        r3c = Region(h_at, h_end)
        H2I = r3c.t("H2I", [P, KT, T], F32R)
        H2L = r3c.t("H2L", [P, KT, T], F32R)
        xt_end = Region(mix_end, hi).at + 4 * KT * T
        r3b = Region(xt_end, hi)
        WHI3 = WHI1 + [r3b.t(f"WHI3_{i}", [P, KT, P], F32R) for i in range(NSPL3 - NSPL1)]
        WLO3 = WLO1 + [r3b.t(f"WLO3_{i}", [P, KT, P], F32R) for i in range(NSPL3 - NSPL1)]
        r3d = Region(h_end + 4 * 2 * NSPL1 * KT * P, xt_end - 4 * KT * T)
        GHI = r3d.t("GHI", [P, MAXG, T], F32R)
        SGF = [r3d.t(f"SGF{i}", [P, CH]) for i in range(2)]
        GU = [r3d.t(f"GU{i}", [P, CH]) for i in range(2)]
        GLO = r3b.t("GLO", [P, MAXG, T], F32R)
        SQT = [r3b.t(f"SQT{i}", [P, CH]) for i in range(2)]
        r3e = Region(h_end + 4 * 2 * NSPL1 * KT * P, xt_end - 4 * KT * T)
        H3 = [r3e.t(f"H3_{i}", [P, KT, CH]) for i in range(2)]
        SS2 = [r3e.t(f"SS2_{i}", [P, CH]) for i in range(NCH)]
        RB2 = [r3e.t(f"RB2_{i}", [P, CH]) for i in range(NCH)]
        r3f = Region(h_at, h_end)
        SS3 = [r3f.t(f"SS3_{i}", [P, CH]) for i in range(NCH)]
        RB3 = [r3f.t(f"RB3_{i}", [P, CH]) for i in range(NCH)]
        OT = [r3f.t(f"OT{i}", [P, D]) for i in range(2)]
        hg_vec = nc.dram_tensor("hg_vec", (4, NS, 256), F32, kind="Internal").ap()
        mb_x = nc.dram_tensor("mb_x", (NS, 512), F32, kind="Internal").ap()
        mb_bc = nc.dram_tensor("mb_bc", (NS, 256), F32, kind="Internal").ap()
        rw_key = nc.dram_tensor("rw_key", (NS, 1280), F32, kind="Internal").ap()
        rw_val = nc.dram_tensor("rw_val", (NS, 256), F32, kind="Internal").ap()
        osc = nc.dram_tensor("osc", (NS, D), F32, kind="Internal").ap()
        dts = nc.dram_tensor("dts", (2, NS, 16), F32, kind="Internal").ap()
        hgd = nc.dram_tensor("hgd", (6, P, T), F32, kind="Internal").ap()
        xbd = nc.dram_tensor("xbd", (6, P, T), F32, kind="Internal").ap()
        BK8 = [ctx.enter_context(nc.psum_tensor(f"bank{i}", [P, 512], F32)) for i in range(8)]

        def par(name, j=0, n=1):
            return PAR[:, COL[name] + j:COL[name] + j + n]

        c_loaded = sem("c_loaded")
        par_loaded = sem("par_loaded")
        consts_built = sem("consts_built")
        c_act = sem("c_act")
        c_turned = sem("c_turned")
        par_turned = sem("par_turned")
        par_ready = sem("par_ready")
        raw_loaded = [sem(f"raw_loaded{i}") for i in range(NRAW)]
        w_hi = sem("w_hi")
        w_lo = sem("w_lo")
        dense_done = sem("dense_done")
        evac = {'act': sem("evac_act"), 'dve': sem("evac_dve"), 'ada': sem("evac_ada")}
        ada_out = sem("ada_out")
        ada_turned = sem("ada_turned")
        x_loaded = [sem(f"x_loaded{i}") for i in range(2)]
        x_turned = sem("x_turned")
        x_act = sem("x_act")
        x_dve = sem("x_dve")
        t_sq = sem("t_sq")
        t_sum = sem("t_sum")
        n_sq = sem("n_sq")
        n_sum = sem("n_sum")
        n_tot = sem("n_tot")
        n_rs = sem("n_rs")
        n_h = sem("n_h")
        n_hi = sem("n_hi")
        n_lo = sem("n_lo")
        phase = sem("phase")
        st_loaded = sem("st_loaded")
        init_pool = sem("init_pool")
        st_turned = sem("st_turned")
        dt_done = sem("dt_done")
        dt_read = sem("dt_read")
        conv_done = sem("conv_done")
        stg_out = [sem(f"stg_out{i}") for i in range(2)]
        acc_out = sem("acc_out")
        rwf_dve = sem("rwf_dve")
        rwf_pe = sem("rwf_pe")
        rwf_act = sem("rwf_act")
        rw_dve = sem("rw_dve")
        rw_pe = sem("rw_pe")
        rw_act = sem("rw_act")
        smp_dve = sem("smp_dve")
        smp_pe = sem("smp_pe")
        smp_act = sem("smp_act")
        smp_dma = sem("smp_dma")
        out_dma = sem("out_dma")
        fin_pe = sem("fin_pe")
        fin_dve = sem("fin_dve")
        hgf_dve = sem("hgf_dve")
        hgf_act = sem("hgf_act")
        mbf_dve = sem("mbf_dve")
        mbf_pe = sem("mbf_pe")
        hg_dve = sem("hg_dve")
        hg_pe = sem("hg_pe")
        hg_act = sem("hg_act")
        hg_loaded = [sem(f"hg_loaded{i}") for i in range(2)]
        mb_dve = sem("mb_dve")
        mb_pe = sem("mb_pe")
        mb_act = sem("mb_act")
        mb_pool = sem("mb_pool")
        mb_loaded = [sem(f"mb_loaded{i}") for i in range(6)]
        hs_dve = sem("hs_dve")
        hs_pe = sem("hs_pe")
        hs_act = sem("hs_act")
        hs_dma = sem("hs_dma")
        ms_dve = sem("ms_dve")
        ms_pe = sem("ms_pe")
        ms_act = sem("ms_act")
        ms_dma = sem("ms_dma")
        pre_dve = sem("pre_dve")
        pre_pe = sem("pre_pe")
        pre_act = sem("pre_act")
        pre_dma = sem("pre_dma")
        mix_hi = sem("mix_hi")
        mix_lo = sem("mix_lo")
        gu_hi = sem("gu_hi")
        gu_lo = sem("gu_lo")
        y_turned = sem("y_turned")
        y_act = sem("y_act")
        y_dve = sem("y_dve")
        y_out = [sem(f"y_out{i}") for i in range(2)]
        dhead_loaded = sem("dhead_loaded")
        ident_built = sem("ident_built")
        c_sig = sem("c_sig")
        smp_dma2 = sem("smp_dma2")
        smp_dma3 = sem("smp_dma3")
        smp_dma4 = sem("smp_dma4")
        hs_dma2 = sem("hs_dma2")
        hs_dma3 = sem("hs_dma3")
        ms_dma2 = sem("ms_dma2")
        ms_dma3 = sem("ms_dma3")
        silu_s = sem("silu_s")
        silu_m = sem("silu_m")
        pre_pool = sem("pre_pool")
        act_own = sem("act_own")
        dve_own = sem("dve_own")
        pool_own = sem("pool_own")

        def linker(eng, own):
            count = [0]

            def link(ins):
                count[0] += 1
                ins.then_inc(own, 1)
                eng.wait_ge(own, count[0])
            return link

        def end_phase(eng, k, wait=True):
            eng.drain().then_inc(phase, 1)
            if wait:
                eng.wait_ge(phase, 4 * (k + 1))

        def smp(engine):
            counter, steps = {'dve': (smp_dve, SMP_DVE), 'pe': (smp_pe, SMP_PE), 'act': (smp_act, SMP_ACT)}[engine]

            def at(name):
                return counter, steps.index(name) + 1
            return at

        def XUSE(i):
            return i // 2 + 1

        def weight_view(u):
            kind, i = UNITS[u]
            if kind == 'down':
                g, d = i
                r0 = sum(GROUPS[:g]) * P
                src = w_down[0, r0:r0 + GROUPS[g] * P, d * P:(d + 1) * P]
            elif kind == 'ada':
                src = w_ada[0, 2 * i[1] * P:2 * (i[1] + 1) * P, i[0] * 512:(i[0] + 1) * 512]
            else:
                w, c0 = {'rw': (w_in, RW0), 'dt': (w_in, DT0), 'z': (w_in, MZ0), 'xbc': (w_in, MX0),
                         'hgg': (w_in, HG0 + 768), 'hg': (w_in, HG0), 'out': (w_out, 0), 'gate': (w_gate, 0),
                         'up': (w_up, 0)}[kind]
                src = w[0, :, c0 + i * P:c0 + (i + 1) * P]
            return src.rearrange("(k p) n -> p k n", p=P)

        def raw_ada(u):
            return RAW[u % NRAW][:, :, :].rearrange("p (k x) n -> p k (x n)", k=2)

        def unit_k(u):
            kind, i = UNITS[u]
            return GROUPS[i[0]] if kind == 'down' else KT

        SLOT, SPREV = [], []
        slot_user = {}
        n1s = sum(1 for u in SPLIT if u < N1)
        for i, u in enumerate(SPLIT):
            s = i % NSPL1 if i < n1s else (i - n1s) % NSPL3
            SLOT.append(s)
            SPREV.append(slot_user.get(s))
            slot_user[s] = i

        def w_split(i):
            hi_, lo_ = (WHI1, WLO1) if i < n1s else (WHI3, WLO3)
            return hi_[SLOT[i]], lo_[SLOT[i]]

        PLAN1 = []
        splits_at = {}
        for i, u in enumerate(SPLIT):
            if i == 0:
                continue
            j = i - 1
            if UNITS[u][0] == 'up':
                j = i - 2
            elif UNITS[u][0] == 'gate' and UNITS[SPLIT[i - 1]][0] == 'up':
                j = i - 2
            elif UNITS[u][0] == 'down' and UNITS[SPLIT[i - 1]][0] == 'up':
                j = i - 1
            splits_at.setdefault(FIRSTQ[SPLIT[j]], []).append(i)

        def dense_items(q0, q1, lag_tail=True):
            items = []
            for q in range(q0, q1):
                items += [('split', i) for i in splits_at.get(q, []) if not (SPLIT[i] >= N1 > UNITS_OF(q))]
                items.append(('mm', q))
                if q > q0:
                    items.append(('ev', q - 1))
            if lag_tail and q1 > q0:
                items.append(('ev', q1 - 1))
            return items

        def UNITS_OF(q):
            return QUANTA[q][0]

        q_rw_end = LASTQ[16 + 7] + 1
        PLAN1 += dense_items(16, q_rw_end)
        PLAN1.append(('dt', 0))
        left = list(range(q_rw_end, QP1))
        rw_list = [('rw_' + n, 0) for n in ('mix', 'lin', 'lora', 'gates', 'rs', 'decays', 'decay')]
        for b in range(NB):
            for n, front in (('turn', 'mix'), ('inv1', 'lin'), ('inv2', 'lora'), ('inv3', 'gates'), ('inv4', 'rs'),
                             ('inv5', 'decays'), ('fold', None), ('seq0', None), ('seq1', None), ('post', 'decay')):
                rw_list.append(('rw_' + n, b))
                if front and b + 1 < NB:
                    rw_list.append(('rw_' + front, b + 1))
        BEHIND = {'turn': 1, 'lin': 1, 'gates': 1, 'inv4': 1, 'post': 1, 'decay': 2}
        TAIL = [1, 8, 1, 0]
        left_in_tail = sum(TAIL)

        def fill(n):
            for _ in range(n):
                if left:
                    q = left.pop(0)
                    PLAN1.extend([('split', i) for i in splits_at.get(q, []) if SPLIT[i] < N1])
                    PLAN1.append(('mm', q))
                    if q > q_rw_end:
                        PLAN1.append(('ev', q - 1))

        for item in rw_list:
            PLAN1.append(item)
            fill(min(BEHIND.get(item[0][3:], 0), len(left) - left_in_tail))
        for st in range(4):
            PLAN1.append(('rws', st))
            if st == 0:
                PLAN1.append(('rw_final', 0))
            if st == 1:
                fill(3)
                PLAN1 += [('silu', i) for i in range(3 * 6)]
                fill(TAIL[1] - 3)
            else:
                fill(TAIL[st])
        assert not left
        PLAN1.append(('ev', QP1 - 1))

        PLAN2 = [('pre', 0), ('hg_logits', 0), ('mb_turn', 0), ('hg_gate', 0), ('hg_levels', 0)]
        late = list(range(QP1, QP2))
        for b in range(NB):
            items = [('hg_att', b), ('hg_state', b), ('mb_decay', b), ('hg_o', b), ('hg_logits', b + 1), ('mb_prod', b),
                     ('hg_sq', b), ('hg_gate', b + 1), ('mb_turn', b + 1), ('mb_sq', b), ('hg_out', b),
                     ('hg_levels', b + 1), ('mb_out', b), ('hg_x', b)]
            for item in items:
                if item[1] == NB:
                    continue
                PLAN2.append(item)
                if item[0] in ('mb_decay', 'hg_o', 'mb_prod', 'hg_sq', 'mb_turn', 'hg_x') and late:
                    group, part = UNITS[QUANTA[late[0]][0]][1]
                    if part == 0 and group > 4:
                        PLAN2.append(('adt', group - 1))
                    PLAN2.append(('mm', late.pop(0)))
        assert not late
        PLAN2 += [('adt', 11), ('smp_tok', 0), ('hg_x', NB), ('mix_final', 0), ('smp_state', 0), ('smp_out', 0)]

        PLAN3 = [('mixsplit', 0)]
        PLAN3 += [('split', i) for i, u in enumerate(SPLIT)
                  if u >= N1 and any(i in splits_at[q] for q in splits_at if q < QP2)]
        PLAN3 += [('mixsplit', c) for c in range(1, NCH)]
        q_out_end = LASTQ[N1 + 7] + 1
        after_out = [[('sum', 3), ('scaled', 3)], [('sum', 4), ('rest', 3), ('scaled', 4)],
                     [('sum', 5), ('rest', 4), ('scaled', 5), ('rest', 5)]]
        after_down = [[('sum', 6), ('normed', 6)], [('sum', 7), ('normed', 7), ('y', 0), ('y', 1)],
                      [('sum', 8), ('normed', 8)] + [('y', i) for i in range(2, 9)]]
        for q0, q1, after in ((QP2, q_out_end, after_out), (q_out_end, len(QUANTA), after_down)):
            for item in dense_items(q0, q1):
                PLAN3.append(item)
                if item[0] == 'ev' and item[1] in (q1 - 5, q1 - 3, q1 - 1):
                    PLAN3 += after[(item[1] - (q1 - 5)) // 2]

        YB = [b for b in range(7) if b not in BANK[-2:]]

        ADB = [BANK[q] for q in EV['ada']]
        block = ctx.enter_context(nc.Block())

        @block.sync
        def _(sp):
            sp.dma_start(C9[0:1, 0, :], c_prompt).then_inc(c_loaded, 16)
            sp.dma_start(C9[1:9, 0, :], c_sample).then_inc(c_loaded, 16)
            for name, n in ROWS1 + ROWS2:
                half = 0 if COL[name] < NR1 else 1
                r = COL[name] - half * NR1
                dst = PV[r:r + n, half, :]
                sp.dma_start(dst, param_rows[name]).then_inc(par_loaded, 16)
            sp.dma_start(DHEAD[:, :], mb_D.broadcast_to([P, 8])).then_inc(dhead_loaded, 16)
            for u in range(len(UNITS)):
                if u >= NRAW:
                    if UNITS[u - NRAW][0] == 'ada':
                        sp.wait_ge(dense_done, LASTQ[u - NRAW] + 1)
                    else:
                        sp.wait_ge(w_lo, SIDX[u - NRAW] + 1)
                sp.dma_start(raw_ada(u) if UNITS[u][0] == 'ada' else RAW[u % NRAW][:, 0:unit_k(u), :], weight_view(u)).then_inc(raw_loaded[u % NRAW], 16)

        @block.gpsimd
        def _(pool):
            g = nc.gpsimd
            link = linker(pool, pool_own)

            def load_x(i, bufs):
                if i >= 2:
                    pool.wait_ge(x_turned, i - 1)
                dst = bufs[i % 2]
                if i % 9 < NB:
                    pool.dma_start(dst[:, :], x_prompt[0, (i % 9) * BLK:(i % 9 + 1) * BLK, :]).then_inc(
                        x_loaded[i % 2], 16)
                else:
                    pool.dma_start(dst[0:NS, :], x_sample[:, 0, :]).then_inc(x_loaded[i % 2], 16)

            def keep_where(t, base, pattern, cm, n=P):
                link(g.affine_select(out=t, in_=t, pattern=pattern, compare_op=ALU.is_ge, fill=0.0, base=base,
                                     channel_multiplier=cm))

            load_x(0, XTOK)
            load_x(1, XTOK)
            link(g.memset(ident[:, :], 0.0))
            g.affine_select(out=ident[:, :], in_=ident[:, :], pattern=[[-1, P]], compare_op=ALU.not_equal, fill=1.0,
                            base=0, channel_multiplier=1).then_inc(ident_built, 1)
            pool.wait_ge(ident_built, 1)
            link(g.memset(ones[:, :], 1.0))
            link(g.memset(triu[:, :], 1.0))
            keep_where(triu[:, :], 0, [[1, P]], -1)
            link(g.memset(headsum[:, :], 0.0))
            link(g.memset(headsum[0:64, 0:64], 1.0))
            link(g.memset(headsum[64:P, 64:P], 1.0))
            for c, v in enumerate((GN_EPS, 9 * LN2, RMS_EPS, 1.0)):
                link(g.memset(CST[:, c:c + 1], v))
            link(g.memset(CM32[:, :], 1.0))
            link(g.memset(CM32[:, 0:BLK:32], 0.0))
            link(g.memset(G4[:, :], 1.0))
            keep_where(G4[:, :], 0, [[-4, 32]], 1)
            keep_where(G4[:, :], 3, [[4, 32]], -1)
            for lv, n in enumerate(HLEV):
                link(g.memset(BIG[:, :], 1.0))
                keep_where(BIG[:, :], 0, [[-2 * n, P // (2 * n)], [0, 2 * n]], 1)
                keep_where(BIG[:, :], n - 1, [[2 * n, P // (2 * n)], [0, 2 * n]], -1)
                link(g.memset(BIG[:, :].rearrange("p (b e r) -> p b e r", e=2, r=n)[:, :, 0, :], 0.0))
                for s in range(4):
                    link(g.tensor_copy(HMK[32 * s:32 * s + 32, lv, :], BIG[32 * s:32 * s + 32, 32 * s:32 * s + 32]))
            for s in range(3):
                link(g.tensor_copy(HMK[32 * s:32 * s + 32, 5, :], ident[32 * s:32 * s + 32, 32 * s:32 * s + 32]))
            g.tensor_copy(HMK[96:P, 5, :], ident[96:P, 96:P]).then_inc(consts_built, 1)
            for i in range(2, 9):
                load_x(i, XTOK)
            end_phase(pool, 0)

            pool.dma_start(SCT[:, :], state_conv[0].rearrange("b j c -> (b j) c")).then_inc(st_loaded, 16)
            pool.dma_start(SHT[:, :], state_shift[0]).then_inc(st_loaded, 16)
            pool.dma_start(WL[0:32, :], rw_w2[0]).then_inc(st_loaded, 16)
            pool.dma_start(WL[32:64, :], rw_a2[0]).then_inc(st_loaded, 16)
            pool.dma_start(WL[64:P, :], rw_g2[0]).then_inc(st_loaded, 16)
            link(g.memset(PR[:, :, 0:1], 0.0))
            link(g.memset(VZ[:, :, :, :], 0.0))
            link(g.memset(ST[:, :, :], 0.0))
            link(g.memset(CM64[:, :], 1.0))
            link(g.memset(CM64[:, 0:BLK:64], 0.0))
            for hp in range(2):
                r = slice(64 * hp, 64 * hp + 64)
                link(g.tensor_copy(I4[r, :], ident[r, r]))
                for own in range(2):
                    o = slice(64 * own, 64 * own + 64)
                    link(g.tensor_copy(RWM[o, hp, 64 * (1 - hp):64 * (1 - hp) + 64], triu[o, o]))
                    link(g.tensor_tensor(RWM[o, hp, 64 * hp:64 * hp + 64], triu[o, o], ident[o, o], ALU.subtract))
            MW = MX[:, 0, :]
            for lv, n in enumerate(LEVELS):
                for turned in range(2):
                    link(g.memset(MW, 1.0))
                    keep_where(MW, 0 if turned else -n, [[-2 * n, P // (2 * n)], [0, 2 * n]], 1)
                    keep_where(MW, n - 1 if turned else 2 * n - 1, [[2 * n, P // (2 * n)], [0, 2 * n]], -1)
                    link(g.memset(MW.rearrange("p (b e r) -> p b e r", e=2, r=n)[:, :, 1 - turned, :], 0.0))
                    for hp in range(2):
                        r = slice(64 * hp, 64 * hp + 64)
                        link(g.tensor_copy(LM[r, lv, turned, :], MW[r, 64 * hp:64 * hp + 64]))
            g.memset(LA[:, :, :], 0.0).then_inc(init_pool, 1)

            def split_rest(i):
                u = SPLIT[i]
                pool.wait_ge(w_hi, i + 1)
                whi, wlo = w_split(i)
                g.tensor_tensor(wlo[:, :, :], RAW[u % NRAW][:, :, :], whi[:, :, :].bitcast(F32),
                                ALU.subtract).then_inc(w_lo, 1)

            def stage_out(q):
                u, c = QUANTA[q]
                kind, t = UNITS[u]
                if kind not in ('hg', 'xbc'):
                    return
                r = STAGED.index(q)
                cols = slice(c * CH, (c + 1) * CH)
                if kind == 'xbc':
                    pool.wait_ge(conv_done, r + 1)
                    pool.dma_start(xbd[t, :, cols], ACC[0][:, :]).then_inc(acc_out, 16)

            def rws(s):
                D_, T_, A_ = smp('dve'), smp('pe'), smp('act')
                if s == 1:
                    pool.wait_ge(*A_('tok'))
                    pool.dma_start(rw_key, STKW[:, 0:1280]).then_inc(smp_dma, 16)
                    pool.dma_start(rw_val, STKW[:, 1280:1536]).then_inc(smp_dma, 16)
                    pool.dma_start(SWK[:, :], state_wkv[0].rearrange("b h (r v) k -> (b h r) (v k)", r=4)).then_inc(
                        smp_dma, 16)
                    pool.wait_ge(smp_dma, 3 * 16)
                    pool.dma_start(SWV[:, 0:320], rw_key.rearrange("b (h x) -> (b h) x", h=4).unsqueeze(
                        1).broadcast_to([4 * NS, 4, 320])).then_inc(smp_dma2, 16)
                    pool.dma_start(SWV[:, 320:336], rw_val.rearrange("b (x v) -> (b x) v", v=16)).then_inc(smp_dma2, 16)
                if s == 2:
                    pool.wait_ge(*D_('state'))
                    pool.dma_start(wkv_s[0].rearrange("b h (r v) k -> (b h r) (v k)", r=4), SWK[:, :]).then_inc(
                        out_dma, 16)
                    pool.dma_start(osc[:, 768:1024].rearrange("b (x v) -> b x v", v=16), SWV[:, 0:16]).then_inc(
                        smp_dma3, 16)
                    pool.wait_ge(smp_dma3, 16)
                    pool.dma_start(STKW[:, 0:256], osc[:, 768:1024]).then_inc(smp_dma4, 16)

            def rw_final(_):
                pool.wait_ge(fin_dve, 1)
                pool.dma_start(wkv_p[0, 0].rearrange("(j h) v k -> v j h k", h=2),
                               FST[:, :, :].rearrange("v j (h k) -> v j h k", h=2)).then_inc(out_dma, 16)
                pool.dma_start(shift_p[0], FSH[0:1, :]).then_inc(out_dma, 16)
                pool.dma_start(shift_s[0], FSH[1:9, :]).then_inc(out_dma, 16)
                pool.dma_start(conv_p[0, 0], FCV[0:3, :]).then_inc(out_dma, 16)
                pool.dma_start(conv_s[0, :, 2, :], FCV[3:11, :]).then_inc(out_dma, 16)
                pool.dma_start(conv_s[0, :, 0:2, :], state_conv[0, :, 1:3, :]).then_inc(out_dma, 16)

            for what, arg in PLAN1:
                if what == 'ev':
                    stage_out(arg)
                elif what == 'dt':
                    pool.wait_ge(dt_read, 1)
                elif what == 'split' and FIRSTQ[SPLIT[arg - 1]] >= q_rw_end:
                    split_rest(arg)
                elif what == 'rws':
                    rws(arg)
                elif what == 'rw_final':
                    rw_final(arg)
            pool.wait_ge(acc_out, 16 * 18)
            for s in range(2):
                pool.wait_ge(stg_out[s], 16 * 9)
            end_phase(pool, 1)

            pool.dma_start(DTB[:, :], mb_dt_bias.broadcast_to([P, 8])).then_inc(pre_dma, 16)
            pool.dma_start(AEX[:, :], mb_A_log.broadcast_to([P, 8])).then_inc(pre_dma, 16)

            def load_hg(b):
                w = BLK if b < NB else NS
                if b >= 2:
                    pool.wait_ge(hg_pe, step(HG_PE, 'att', b - 2))
                pool.dma_start(HB2[b % 2][:, :, 0:w], hgd[:, :, b * BLK:b * BLK + w].rearrange(
                    "t p c -> p t c")).then_inc(hg_loaded[b % 2], 16)

            def mb_decay(b):
                pool.wait_ge(mbf_dve, step(MBF_DVE, 'xdt', b))
                g.tensor_tensor(XDE[:, :, :], XD[:, :, :], ES[:, b, :].unsqueeze(2).broadcast_to([P, 8, 64]),
                                ALU.mult).then_inc(mb_pool, 1)
                pool.wait_ge(mb_act, step(MB_ACT, 'E2', b))
                g.tensor_tensor(CE[:, :, :], E2[:, :, :], XB[5][:, b * BLK:(b + 1) * BLK].unsqueeze(1).broadcast_to([P, 4, P]),
                                ALU.mult).then_inc(mb_pool, 1)

            for t in range(6):
                pool.dma_start(XB[t][:, :], xbd[t]).then_inc(mb_loaded[t], 16)
            load_hg(0)
            load_hg(1)
            link(g.memset(HSH[:, :, :, :], 0.0))
            link(g.memset(HAD[:, :, :], 0.0))
            link(g.memset(HVD[:, :, :, :], 0.0))
            g.memset(STt[:, :, :], 0.0).then_inc(pre_pool, 1)
            pool.wait_ge(out_dma, 7 * 16)
            load_x(9, XTOK2)
            load_x(10, XTOK2)
            for what, arg in PLAN2:
                if what == 'mb_decay':
                    mb_decay(arg)
                elif what == 'hg_x' and arg + 2 <= NB:
                    load_x(11 + arg, XTOK2)
                elif what == 'hg_att' and arg + 2 <= NB:
                    load_hg(arg + 2)
                elif what == 'smp_tok':
                    pool.dma_start(SHG[:, :], state_hgrn[0].rearrange("b h (r k) v -> (b h r) (k v)", r=4)).then_inc(
                        hs_dma, 16)
                    pool.wait_ge(mb_dve, step(MB_DVE, 'out', NB - 1))
                    pool.dma_start(SSM[:, :], state_ssm[0].rearrange("b h (r p) n -> (b h r) (p n)", r=2)).then_inc(
                        ms_dma, 16)
                    pool.wait_ge(pre_dve, PRE_DVE.index('twice') + 1)
                    pool.dma_start(dts.rearrange("v b x -> b v x"), DTW[P - NS:P, :, :, :].rearrange(
                        "b v h r -> b v (h r)")).then_inc(ms_dma, 16)
                    pool.wait_ge(hs_act, 3)
                    pool.dma_start(hg_vec.rearrange("v b x -> b v x"), STK[:, :].rearrange("b (v x) -> b v x",
                                                                                        v=4)).then_inc(hs_dma, 16)
                    pool.wait_ge(ms_act, 1)
                    pool.dma_start(mb_x, STOKEN[:, 0:512]).then_inc(ms_dma, 16)
                    pool.dma_start(mb_bc, STOKEN[:, 512:768]).then_inc(ms_dma, 16)
                    pool.wait_ge(hs_dma, 32)
                    pool.dma_start(SV1[:, 0:48].rearrange("p (v k) -> p v k", v=3),
                                   hg_vec[0:3].rearrange("v b (x k) -> (b x) v k", k=16)).then_inc(hs_dma2, 16)
                    pool.dma_start(SV1[:, 64:128], hg_vec[3].rearrange("b (h v) -> (b h) v", h=4).unsqueeze(
                        1).broadcast_to([4 * NS, 4, 64])).then_inc(hs_dma2, 16)
                    pool.wait_ge(ms_dma, 4 * 16)
                    pool.dma_start(SV2[:, 128:160], mb_x.rearrange("b (x p) -> (b x) p", p=32)).then_inc(ms_dma2, 16)
                    for v in range(2):
                        pool.dma_start(SV2[:, 160 + v:161 + v], dts[v].rearrange("b x -> (b x)").unsqueeze(1)).then_inc(
                            ms_dma2, 16)
                    pool.dma_start(SV2[:, 0:128], mb_bc.rearrange("b (g x) -> (b g) x", g=2).unsqueeze(1).broadcast_to(
                        [2 * NS, 8, P])).then_inc(ms_dma2, 16)
                elif what == 'mix_final':
                    for h in range(2):
                        pool.dma_start(hg_p[0, 0].rearrange("(j h) k v -> h k j v", h=2)[h],
                                       HSH[64 * h:64 * h + 64, 4, :, :]).then_inc(out_dma, 16)
                    pool.wait_ge(fin_dve, 2)
                    for r in range(2):
                        for gr in range(2):
                            pool.dma_start(ssm_p[0, 0].rearrange("(g a r) p n -> g r p a n", g=2, a=2)[gr, r],
                                           STF[64 * r:64 * r + 64, :, 64 * gr:64 * gr + 64]).then_inc(out_dma, 16)
                elif what == 'smp_state':
                    pool.wait_ge(hs_dve, HS_DVE.index('osum') + 1)
                    pool.dma_start(osc[:, 0:256].rearrange("b (h v) -> b h v", h=4), SO2[:, :]).then_inc(hs_dma3, 16)
                    pool.dma_start(hg_s[0].rearrange("b h (r k) v -> (b h r) (k v)", r=4), SHG[:, :]).then_inc(
                        out_dma, 16)
                    pool.wait_ge(hs_dma3, 16)
                    pool.dma_start(STK[:, 0:256], osc[:, 0:256]).then_inc(hs_dma3, 16)
                    pool.wait_ge(ms_dve, MS_DVE.index('y') + 1)
                    pool.dma_start(osc[:, 256:768].rearrange("b (x p) -> b x p", p=32), SY[:, :]).then_inc(ms_dma3, 16)
                    pool.dma_start(ssm_s[0].rearrange("b h (r p) n -> (b h r) (p n)", r=2), SSM[:, :]).then_inc(
                        out_dma, 16)
                    pool.wait_ge(ms_dma3, 16)
                    pool.dma_start(STOKEN[:, 0:512], osc[:, 256:768]).then_inc(ms_dma3, 16)
            pool.wait_ge(out_dma, 15 * 16)
            end_phase(pool, 2)
            for i in range(9):
                pool.wait_ge(y_act, i + 1)
                pool.wait_ge(y_dve, i + 1)
                if i < NB:
                    pool.dma_start(y_p[0, i * BLK:(i + 1) * BLK, :], OT[i % 2][:, :]).then_inc(y_out[i % 2], 16)
                else:
                    pool.dma_start(y_s[:, 0, :], OT[i % 2][0:NS, :]).then_inc(y_out[i % 2], 16)
            pool.wait_ge(y_out[0], 16 * 5)
            pool.wait_ge(y_out[1], 16 * 4)

        @block.tensor
        def _(pe):
            mm = nc.tensor.matmul

            def turn(out, in_, n):
                return nc.tensor.transpose(out, in_, ident[0:n, 0:n])

            def turn_x(i, bufs):
                b0 = 3 + 2 * (i % 2) if i < 9 else 0
                pe.wait_ge(x_loaded[i % 2], 16 * XUSE(i))
                if i < 9:
                    if i >= 2:
                        pe.wait_ge(x_act, i - 1)
                        pe.wait_ge(x_dve, i - 1)
                else:
                    if i > 9:
                        pe.wait_ge(x_act, i)
                        pe.wait_ge(x_dve, i)
                n = BLK if i % 9 < NB else NS
                for k in range(KT):
                    last = turn(BK8[b0 + k // 4][:, (k % 4) * P:(k % 4) * P + n], bufs[i % 2][0:n, k * P:(k + 1) * P], n)
                last.then_inc(x_turned, 1)

            def dense(q):
                u, c = QUANTA[q]
                kind, arg = UNITS[u]
                bank = BK8[BANK[q]]
                if PREV[q] is not None:
                    pe.wait_ge(evac[evac_engine(PREV[q])], EVN[PREV[q]])
                if kind == 'ada':
                    pe.wait_ge(raw_loaded[u % NRAW], 16 * (u // NRAW + 1))
                    for x in range(2):
                        k = 2 * arg[1] + x
                        last = mm(bank[0:9, :], CT[:, k, :], raw_ada(u)[:, x, :], start=(k == 0), stop=(k == KT - 1))
                    last.then_inc(dense_done, 1)
                    return
                if c == 0:
                    pe.wait_ge(w_hi, SIDX[u] + 1)
                    pe.wait_ge(w_lo, SIDX[u] + 1)
                if kind in ('out', 'gate'):
                    ready = [mix_lo, n_lo][kind == 'gate']
                    pe.wait_ge(ready, c + 1 + (3 if kind == 'gate' else 0))
                if kind == 'rw' and u == 16:
                    pe.wait_ge(n_lo, c + 1)
                if kind == 'down':
                    tiles = sum(GROUPS[:arg[0] + 1])
                    pe.wait_ge(gu_lo, 3 * (tiles - 1) + c + 1)
                hi_, lo_ = {'out': (MHI, MLO), 'gate': (H2I, H2L), 'up': (H2I, H2L), 'down': (GHI, GLO)}.get(
                    kind, (HHI, HLO))
                whi, wlo = w_split(SIDX[u])
                cols = slice(c * CH, (c + 1) * CH)
                nk = unit_k(u)
                for k in range(nk):
                    mm(bank[:, 0:CH], whi[:, k, :], hi_[:, k, cols], start=(k == 0), stop=False)
                    mm(bank[:, 0:CH], whi[:, k, :], lo_[:, k, cols], start=False, stop=False)
                    last = mm(bank[:, 0:CH], wlo[:, k, :], hi_[:, k, cols], start=False, stop=(k == nk - 1))
                last.then_inc(dense_done, 1)

            def norm_sum(n):
                pe.wait_ge(n_sum, n + 1)
                if n:
                    pe.wait_ge(n_rs, n)
                mm(BK8[7][:, 0:CH], ones[:, :], SS1[n][:, :], start=True, stop=True).then_inc(n_tot, 1)

            def ada_turn(a_):
                pe.wait_ge(ada_out, a_ + 1)
                for t in range(4):
                    last = turn(BK8[ADB[a_]][:, 9 * t:9 * t + 9], (ADT0 if a_ < 4 else ADT2)[:, t * P:(t + 1) * P], 9)
                last.then_inc(ada_turned, 1)

            def chunk_sum(n):
                c = n % 3
                pe.wait_ge(t_sum, (24 if n >= 6 else 0) + 18 + 2 * (c + 1))
                pe.wait_ge(n_rs, n)
                mm(BK8[7][:, 0:CH], ones[:, :], (SS2, SS3)[n // 6][c][:, :], start=True, stop=True).then_inc(n_tot, 1)

            pe.wait_ge(ident_built, 1)
            pe.wait_ge(c_act, 1)
            for k in range(KT):
                last = turn(BK8[7][:, k * 9:k * 9 + 9], C9[:, 0, k * P:(k + 1) * P], 9)
            last.then_inc(c_turned, 1)
            pe.wait_ge(par_loaded, 16 * len(ROWS1 + ROWS2))
            turn(BK8[7][:, 128:128 + NR1], PV[0:NR1, 0, :], NR1)
            turn(BK8[7][:, 256:256 + NR2], PV[0:NR2, 1, :], NR2).then_inc(par_turned, 1)
            pe.wait_ge(par_ready, 1)
            for q in range(16):
                dense(q)
                if q % 4 == 0 and q:
                    ada_turn(q // 4 - 1)
                if q < 9:
                    turn_x(q, XTOK)
            pe.wait_ge(consts_built, 1)
            for n in range(3):
                norm_sum(n)
            ada_turn(3)
            end_phase(pe, 0, wait=False)

            def rw_init():
                pe.wait_ge(st_loaded, 16 * 5)
                for t in range(6):
                    turn(BK8[3][:, 24 * t:24 * t + 24], SCT[:, t * P:(t + 1) * P], 24)
                for t in range(7):
                    last = turn(BK8[3][:, 160 + 8 * t:168 + 8 * t], SHT[:, t * P:(t + 1) * P], NS)
                last.then_inc(st_turned, 1)

            def dt_proj():
                pe.wait_ge(evac['act'], EVN[LASTQ[16 + 7]])
                for i in range(9):
                    t0 = i * P if i < 8 else T - P
                    last = turn(BK8[4][:, 8 * i:8 * i + 8], DTF[:, t0:t0 + P], 8)
                last.then_inc(dt_done, 1)

            def lora(w):
                for v in range(3):
                    for j in range(2):
                        o = (v % 2) * 2 * BLK + j * BLK
                        mm(BK8[2 + v // 2][:, o:o + w], WL[:, j * P:(j + 1) * P], LA[:, v, 0:w], start=True, stop=True)
                return mm(BK8[3][:, 2 * BLK:4 * BLK], headsum[:, :], T2[:, :, :].rearrange("p j t -> p (j t)"),
                          start=True, stop=True)

            HP = [slice(0, 64), slice(64, P)]

            def rw(stage, b):
                def V(name):
                    return rw_dve, step(RW_DVE, name, b)

                def A(name):
                    return rw_act, step(RW_ACT, name, b)

                B0, B1, B2, B3 = BK8[4:8]
                if stage == 'lora':
                    pe.wait_ge(rwf_dve, step(RWF_DVE, 'squared', b))
                    pe.wait_ge(rwf_act, step(RWF_ACT, 'lora_in', b))
                    lora(BLK).then_inc(rwf_pe, 1)
                elif stage == 'turn':
                    pe.wait_ge(rwf_dve, step(RWF_DVE, 'operands', b))
                    if b:
                        pe.wait_ge(rw_dve, step(RW_DVE, 'out', b - 1))
                    for src, bank in ((AR, B2), (BK, B3)):
                        for jc in range(4):
                            last = turn(bank[:, jc * P:(jc + 1) * P], src[:, jc, :, :].rearrange("p s t -> p (s t)"), P)
                    last.then_inc(rw_pe, 1)
                    for hp, bank in ((0, B0), (1, B1)):
                        for jc in range(4):
                            last = mm(bank[:, jc * P:(jc + 1) * P], BK[HP[hp], jc, :, :].rearrange("p s t -> p (s t)"),
                                      AR[HP[hp], jc, :, :].rearrange("p s t -> p (s t)"), start=True, stop=True)
                    last.then_inc(rw_pe, 1)
                    pe.wait_ge(*A('turned'))
                    for jc in range(4):
                        for hp in range(2):
                            last = mm(B3[HP[hp], jc * 64:jc * 64 + 64], AR[HP[hp], jc, hp, :], BK[HP[hp], jc, hp, :],
                                      start=True, stop=True)
                    last.then_inc(rw_pe, 1)
                    for jc in range(4):
                        last = turn(B2[:, jc * P:(jc + 1) * P], VZ[:, jc, :, :].rearrange("p s t -> p (s t)"), P)
                    last.then_inc(rw_pe, 1)
                    pe.wait_ge(rwf_dve, step(RWF_DVE, 'bonus', b))
                    mm(BK8[2][:, 0:2 * BLK], headsum[:, :], KK[:, :, :].rearrange("p j t -> p (j t)"), start=True,
                       stop=True).then_inc(rwf_pe, 1)
                elif stage[:3] == 'inv':
                    lv = int(stage[3])
                    pe.wait_ge(*V(f'inv{lv - 1}'))
                    if lv == 1:
                        pe.wait_ge(*V('masked'))
                    for jc in range(4):
                        for hp in range(2):
                            last = mm(B0[HP[hp], jc * 64:jc * 64 + 64], AM[HP[hp], hp, jc, 64 * hp:64 * hp + 64],
                                      X[HP[hp], jc, :], start=True, stop=True)
                    last.then_inc(rw_pe, 1)
                    pe.wait_ge(*A(f'P{lv}'))
                    for jc in range(4):
                        for hp in range(2):
                            if lv < 5:
                                mm(B1[HP[hp], jc * 64:jc * 64 + 64], Y[HP[hp], jc, :], PS[HP[hp], jc, :],
                                   start=True, stop=True)
                            last = mm(B3[HP[hp], jc * 64:jc * 64 + 64], PS[HP[hp], jc, :], Y[HP[hp], jc, :],
                                      start=True, stop=True)
                    last.then_inc(rw_pe, 1)
                elif stage == 'fold':
                    pe.wait_ge(*V('inv5'))
                    for jc in range(4):
                        for hp in range(2):
                            o = 1 - hp
                            last = mm(B1[HP[hp], jc * 64:jc * 64 + 64], AM[HP[o], hp, jc, 64 * hp:64 * hp + 64],
                                      UV[HP[o], jc, 64 * hp:64 * hp + 64], start=True, stop=True)
                    last.then_inc(rw_pe, 1)
                    for jc in range(4):
                        for hp in range(2):
                            last = mm(B2[HP[hp], jc * 64:jc * 64 + 64], ARt[HP[hp], jc, 64 * hp:64 * hp + 64],
                                      Y[HP[hp], jc, :], start=True, stop=True)
                    last.then_inc(rw_pe, 1)
                    pe.wait_ge(*A('T1'))
                    for jc in range(4):
                        for hp in range(2):
                            last = mm(B0[HP[hp], jc * 64:jc * 64 + 64], Y[HP[hp], jc, :], T1S[HP[hp], jc, :],
                                      start=True, stop=True)
                    last.then_inc(rw_pe, 1)
                elif stage[:3] == 'seq':
                    c = int(stage[3])
                    if c == 0:
                        pe.wait_ge(*A('PT'))
                        if b == 0:
                            pe.wait_ge(init_pool, 1)
                        else:
                            pe.wait_ge(rw_dve, step(RW_DVE, 'S1', b - 1))
                    else:
                        pe.wait_ge(*V('S0'))
                    for j in range(2):
                        for hp in range(2):
                            last = mm(B1[HP[hp], j * 64:j * 64 + 64], PTS[HP[hp], 2 * j + c, :], ST[HP[hp], j, :],
                                      start=True, stop=True)
                    last.then_inc(rw_pe, 1)
                    pe.wait_ge(*V(f'U{c}'))
                    for j in range(2):
                        for hp in range(2):
                            jc = 2 * j + c
                            out = B3[HP[hp], jc * 64:jc * 64 + 64]
                            mm(out, ST[HP[hp], j, :], AR[HP[hp], jc, 1 - hp, :], start=True, stop=False)
                            mm(out, UV[:, jc, 64 * hp:64 * hp + 64], AM[:, hp, jc, 64 * (1 - hp):64 * (1 - hp) + 64],
                               start=False, stop=True)
                            last = mm(B2[HP[hp], j * 64:j * 64 + 64], BKt[:, jc, 64 * hp:64 * hp + 64],
                                      UV[:, jc, 64 * hp:64 * hp + 64], start=True, stop=True)
                    last.then_inc(rw_pe, 1)
                elif stage == 'post':
                    rw_norm_sums(BLK, V, rw_pe)

            def head_sums(bank, src, w):
                return mm(bank[:, 0:2 * BLK].rearrange("p (j t) -> p j t", j=2)[:, :, 0:w], headsum[:, :],
                          src[:, :, 0:w], start=True, stop=True)

            def rw_norm_sums(w, V, s):
                pe.wait_ge(*V('o'))
                head_sums(BK8[4], OS, w).then_inc(s, 1)
                pe.wait_ge(*V('centred'))
                head_sums(BK8[5], OSQ, w).then_inc(s, 1)

            def rws(s):
                V, A = smp('dve'), smp('act')
                if s == 0:
                    pe.wait_ge(rw_dve, step(RW_DVE, 'out', NB - 1))
                    pe.wait_ge(*V('squared'))
                    pe.wait_ge(*A('lora_in'))
                    lora(NS).then_inc(smp_pe, 1)
                elif s == 1:
                    pe.wait_ge(*V('vectors'))
                    pe.wait_ge(*A('wexp'))
                    for v, src in enumerate((MX[:, 0:2, :], KK, SG[:, 2:4, :], KP, SG[:, 0:2, :], MX[:, 4:6, :])):
                        for j in range(2):
                            i = 2 * v + j
                            last = turn(BK8[3 + i // 4][0:NS, (i % 4) * P:(i % 4) * P + P], src[:, j, 0:NS], P)
                    last.then_inc(smp_pe, 1)
                    pe.wait_ge(*V('bonus'))
                    mm(BK8[2][:, 0:2 * BLK], headsum[:, :], T2[:, :, :].rearrange("p j t -> p (j t)"), start=True,
                       stop=True).then_inc(smp_pe, 1)
                elif s == 3:
                    pe.wait_ge(smp_dma4, 16)
                    for j in range(2):
                        last = turn(BK8[6][:, 8 * j:8 * j + 8], STKW[:, j * P:(j + 1) * P], NS)
                    last.then_inc(smp_pe, 1)
                    rw_norm_sums(NS, V, smp_pe)

            def rw_final():
                pe.wait_ge(*smp('dve')('clamped'))
                for j in range(2):
                    turn(BK8[3][0:64, j * P:(j + 1) * P], ST[:, j, :], P)
                for t in range(7):
                    turn(BK8[4 + t // 4][0:9, (t % 4) * P:(t % 4) * P + P], PR[:, t, SEQ:SEQ + 9], P)
                for t in range(6):
                    last = turn(BK8[6 + t // 4][0:11, (t % 4) * P:(t % 4) * P + P], XL[:, t, :], P)
                last.then_inc(fin_pe, 1)

            for what, arg in PLAN1:
                if what == 'mm':
                    dense(arg)
                elif what == 'dt':
                    rw_init()
                    dt_proj()
                elif what[:3] == 'rw_' and what != 'rw_final':
                    rw(what[3:], arg)
                elif what == 'rws':
                    rws(arg)
                elif what == 'rw_final':
                    rw_final()
            end_phase(pe, 1)

            H0, H1, H2, H3, M0, M1, M2, M3 = BK8

            def pre():
                pe.wait_ge(pre_dve, PRE_DVE.index('dta') + 1)
                mm(M0[:, 0:64], triu[:, :], DTA[:, 0:8, :].rearrange("p b h -> p (b h)"), start=True, stop=True)
                mm(M0[:, 64:128], ones[:, :], DTA[:, 0:8, :].rearrange("p b h -> p (b h)"), start=True,
                   stop=True).then_inc(pre_pe, 1)

            def hg(stage, b):
                def V(name):
                    return hg_dve, step(HG_DVE, name, b)

                def A(name):
                    return hg_act, step(HG_ACT, name, b)

                HB = HB2[b % 2]
                if stage == 'att':
                    pe.wait_ge(hgf_dve, step(HGF_DVE, 'factors', b))
                    if b:
                        pe.wait_ge(x_act, 9 + b)
                        pe.wait_ge(x_dve, 9 + b)
                    for j in range(2):
                        turn(H0[:, j * P:(j + 1) * P], HB[:, 4 + j, :], P)
                    for j in range(2):
                        last = turn(H0[:, (2 + j) * P:(3 + j) * P], HD[:, 5, j, :], P)
                    last.then_inc(hg_pe, 1)
                    for hp, bank in ((0, H1), (1, H2)):
                        for j in range(2):
                            for lv in range(6):
                                for s in range(4):
                                    t = slice(32 * s, 32 * s + 32)
                                    kk = HD[HP[hp], lv, j, t] if lv < 5 else HK[HP[hp], j, t]
                                    qq = HD[HP[hp], lv, j, t] if lv < 5 else HB[HP[hp], j, t]
                                    last = mm(bank[t, (lv * 2 + j) * 32:(lv * 2 + j) * 32 + 32], kk, qq, start=True,
                                              stop=True)
                    last.then_inc(hg_pe, 1)
                elif stage == 'state':
                    pe.wait_ge(*A('v'))
                    for j in range(2):
                        for hp in range(2):
                            last = mm(H0[HP[hp], j * 256:j * 256 + 256], HKT[:, j, 64 * hp:64 * hp + 64],
                                      HVD[:, j, :, 64 * hp:64 * hp + 64], start=True, stop=True)
                    last.then_inc(hg_pe, 1)
                elif stage == 'o':
                    pe.wait_ge(*V('att'))
                    pe.wait_ge(*V('S'))
                    for hp in range(2):
                        for j in range(2):
                            mm(H2[HP[hp], j * P:(j + 1) * P], HVT[:, j, 64 * hp:64 * hp + 64], HAD[:, 2 * hp + j, :],
                               start=(j == 0), stop=False, skip_group_check=True)
                    for hp in range(2):
                        for j in range(2):
                            for s in range(4):
                                last = mm(H2[HP[hp], j * P + 32 * s:j * P + 32 * s + 32], HSH[HP[hp], s, j, :],
                                          HQ[HP[hp], j, 32 * s:32 * s + 32], start=False, stop=True,
                                          skip_group_check=True)
                    last.then_inc(hg_pe, 1)
                elif stage == 'sq':
                    pe.wait_ge(*V('squared'))
                    mm(H1[:, 0:2 * BLK], headsum[:, :], HT[:, :, :].rearrange("p j t -> p (j t)"), start=True,
                       stop=True).then_inc(hg_pe, 1)
                elif stage == 'x':
                    if b < NB:
                        pe.wait_ge(*V('out'))
                    turn_x(9 + b, XTOK2)

            def mb(stage, b):
                def V(name):
                    return mb_dve, step(MB_DVE, name, b)

                def A(name):
                    return mb_act, step(MB_ACT, name, b)

                if stage == 'turn':
                    if b:
                        pe.wait_ge(mb_dve, step(MB_DVE, 'S', b - 1))
                    else:
                        pe.wait_ge(silu_m, 24)
                        pe.wait_ge(pre_dve, PRE_DVE.index('es') + 1)
                        pe.wait_ge(pre_act, PRE_ACT.index('ed') + 1)
                    t_ = slice(b * BLK, (b + 1) * BLK)
                    for t in range(4):
                        turn(M0[:, t * P:(t + 1) * P], XB[t][:, t_], P)
                    turn(M1[:, 0:P], XB[4][:, t_], P)
                    mm(M1[:, P:2 * P], XB[4][0:64, t_], XB[5][0:64, t_], start=True, stop=True)
                    mm(M2[:, 0:P], XB[4][64:P, t_], XB[5][64:P, t_], start=True, stop=True).then_inc(mbf_pe, 1)
                elif stage == 'decay':
                    pe.wait_ge(mbf_dve, step(MBF_DVE, 'cb', b))
                    if b:
                        pe.wait_ge(mb_act, step(MB_ACT, 'rs', b - 1))
                    for h in range(8):
                        last = mm((M2, M3)[h // 4][:, (h % 4) * P:(h % 4 + 1) * P],
                                  DTA[:, b, h:h + 1].broadcast_to([P, P]), triu[:, :], start=True, stop=True)
                    last.then_inc(mb_pe, 1)
                elif stage == 'prod':
                    pe.wait_ge(*V('m'))
                    pe.wait_ge(mb_pool, step(MB_POOL, 'ce', b))
                    if b == 0:
                        pe.wait_ge(pre_pool, 1)
                    for h in range(8):
                        j, hp, gr = h // 2, h % 2, h // 4
                        out = (M1, M2)[gr][HP[hp], (j % 2) * P:(j % 2 + 1) * P]
                        mm(out, XD[:, h, :], MM[:, h, :], start=True, stop=False)
                        last = mm(out, STt[HP[gr], h % 4, :], CE[HP[gr], h % 4, :], start=False, stop=True)
                    last.then_inc(mb_pe, 1)
                    for gr in range(2):
                        last = mm(M0[HP[gr], 0:256], BT[:, 64 * gr:64 * gr + 64],
                                  XDE[:, 4 * gr:4 * gr + 4, :].rearrange("p h x -> p (h x)"), start=True, stop=True)
                    last.then_inc(mb_pe, 1)
                elif stage == 'sq':
                    mb_norm_sum(A, mb_pe)

            def mb_norm_sum(A, s):
                pe.wait_ge(*A('squared'))
                for gr in range(2):
                    for t in range(2):
                        last = mm(M3[:, gr * P:(gr + 1) * P], ones[:, :], T4[:, 2 * gr + t, :], start=(t == 0),
                                  stop=(t == 1))
                last.then_inc(s, 1)

            def smp_tok():
                pe.wait_ge(evac['ada'], EVN[QP2 - 1])
                pe.wait_ge(hs_act, 2)
                HB = HB2[NB % 2]
                for i in range(8):
                    src = (HB[:, i, 0:NS] if i < 2 else HE[:, i - 2, 0:NS] if i < 4 else HK[:, i - 4, 0:NS] if i < 6
                           else HB[:, i - 2, 0:NS])
                    last = turn((H2, H3)[i // 4][0:NS, (i % 4) * P:(i % 4 + 1) * P], src, P)
                last.then_inc(hs_pe, 1)
                pe.wait_ge(mb_dve, step(MB_DVE, 'out', NB - 1))
                for t in range(6):
                    last = turn((M0, M1)[t // 4][0:NS, (t % 4) * P:(t % 4 + 1) * P], XBS[:, t, :], P)
                last.then_inc(ms_pe, 1)

            def smp_state():
                pe.wait_ge(hs_dve, HS_DVE.index('opart') + 1)
                mm(H2[0:32, 0:64], G4[:, :], SO[:, :], start=True, stop=True).then_inc(hs_pe, 1)

            def smp_out():
                pe.wait_ge(hs_dma3, 32)
                for j in range(2):
                    last = turn(H3[:, 8 * j:8 * j + 8], STK[:, j * P:(j + 1) * P], NS)
                last.then_inc(hs_pe, 1)
                pe.wait_ge(hs_dve, HS_DVE.index('squared') + 1)
                mm(H2[:, 0:2 * BLK], headsum[:, :], HT[:, :, :].rearrange("p j t -> p (j t)"), start=True,
                   stop=True).then_inc(hs_pe, 1)
                pe.wait_ge(ms_dma3, 32)
                for t in range(4):
                    last = turn(M2[:, 8 * t:8 * t + 8], STOKEN[:, t * P:(t + 1) * P], NS)
                last.then_inc(ms_pe, 1)
                mb_norm_sum(lambda name: (ms_act, MS_ACT.index(name) + 1), ms_pe)

            def mix_final():
                for a in range(2):
                    last = turn(H0[:, a * P:(a + 1) * P],
                                STt[:, 2 * a:2 * a + 2, :].rearrange("p r x -> p (r x)"), P)
                last.then_inc(fin_pe, 1)

            for what, arg in PLAN2:
                if what == 'pre':
                    pre()
                elif what == 'mm':
                    dense(arg)
                elif what == 'adt':
                    ada_turn(arg)
                elif what == 'ev':
                    pass
                elif what[:3] == 'hg_':
                    hg(what[3:], arg)
                elif what[:3] == 'mb_':
                    mb(what[3:], arg)
                elif what == 'smp_tok':
                    smp_tok()
                elif what == 'smp_state':
                    smp_state()
                elif what == 'smp_out':
                    smp_out()
                else:
                    pe.wait_ge(x_act, 10 + NB)
                    pe.wait_ge(x_dve, 10 + NB)
                    mix_final()
            end_phase(pe, 2)

            for what, arg in PLAN3:
                if what == 'mm':
                    dense(arg)
                elif what == 'sum':
                    chunk_sum(arg)
                elif what == 'y':
                    i = arg
                    n = BLK if i < NB else NS
                    t0 = i * BLK
                    pe.wait_ge(n_h, 6 + min(NCH, (t0 + n - 1) // CH + 1))
                    if i < 2:
                        for e in EV:
                            pe.wait_ge(evac[e], sum(q <= len(QUANTA) - 3 for q in EV[e]))
                    else:
                        pe.wait_ge(y_act, i - 1)
                        pe.wait_ge(y_dve, i - 1)
                    for k in range(KT):
                        last = turn(BK8[YB[2 * (i % 2) + k // 4]][0:n, (k % 4) * P:(k % 4 + 1) * P], XT[:, k, t0:t0 + n], P)
                    last.then_inc(y_turned, 1)

        @block.scalar
        def _(act):
            a = nc.scalar
            link = linker(act, act_own)
            loaded = [None]

            def tables(name):
                if loaded[0] != name:
                    loaded[0] = name
                    a.preload_act_table_set(name)

            LN_EXP, LN_SET = 'natural_log_exp_and_others', 'natural_log'
            GATES_SET, SILU_SET = 'sigmoid_and_others', 'silu_and_others'
            HP = [slice(0, 64), slice(64, P)]

            def split_hi(i):
                u = SPLIT[i]
                nk = unit_k(u)
                act.wait_ge(raw_loaded[u % NRAW], 16 * (u // NRAW + 1))
                if SPREV[i] is not None:
                    act.wait_ge(dense_done, LASTQ[SPLIT[SPREV[i]]] + 1)
                a.copy(w_split(i)[0][:, 0:nk, :], RAW[u % NRAW][:, 0:nk, :]).then_inc(w_hi, 1)

            def bring_out(q):
                if evac_engine(q) != 'act':
                    return
                u, c = QUANTA[q]
                kind, t = UNITS[u]
                bank = BK8[BANK[q]]
                cols = slice(c * CH, (c + 1) * CH)
                if kind == 'gate':
                    n = GATES.index(q)
                    if n >= 2:
                        act.wait_ge(evac['dve'], EVN[UPS[n - 2]])
                    act.wait_ge(dense_done, q + 1)
                    a.activation(SGF[n % 2][:, :], bank[:, 0:CH], ACT.Silu).then_inc(evac['act'], 1)
                    return
                if kind in ('hg', 'xbc'):
                    r = STAGED.index(q)
                    if 0 < r <= 18:
                        act.wait_ge(conv_done, r)
                    if r >= 20:
                        act.wait_ge(stg_out[r % 2], 16 * ((r - 18) // 2))
                act.wait_ge(dense_done, q + 1)
                if kind == 'rw':
                    a.copy(PR[:, t, 1 + c * CH:1 + (c + 1) * CH], bank[:, 0:CH]).then_inc(evac['act'], 1)
                elif kind == 'dt':
                    a.copy(DTF[:, cols], bank[0:8, 0:CH]).then_inc(evac['act'], 1)
                elif kind in ('hgg', 'z'):
                    a.copy(MIX[:, t + (2 if kind == 'z' else 0), cols], bank[:, 0:CH]).then_inc(evac['act'], 1)
                else:
                    r = STAGED.index(q)
                    a.copy(STG[r % 2][:, 3:3 + CH], bank[:, 0:CH]).then_inc(evac['act'], 1)
                    if kind == 'hg':
                        act.wait_ge(evac['act'], EVN[q])
                        act.dma_start(hgd[t, :, cols], STG[r % 2][:, 3:3 + CH]).then_inc(stg_out[r % 2], 16)

            def ada_act(g):
                q = EV['ada'][g]
                act.wait_ge(dense_done, q + 1)
                a.copy((ADT0 if g < 4 else ADT2)[:, :], BK8[ADB[g]][0:9, :]).then_inc(ada_out, 1)
                act.wait_ge(ada_turned, g + 1)
                for t in range(4):
                    last = a.activation(MOD[:, 4 * g + t, :], BK8[ADB[g]][:, 9 * t:9 * t + 9], ACT.Identity,
                                        bias=par('b_ada', 4 * g + t))
                last.then_inc(evac['ada'], 1)

            def x_half(i, dst):
                act.wait_ge(x_turned, i + 1)
                n = BLK if i % 9 < NB else NS
                b0 = 3 + 2 * (i % 2) if i < 9 else 0
                t0 = (i % 9) * BLK
                a.copy(dst[:, 0:4, t0:t0 + n], BK8[b0][:, :].rearrange("p (k t) -> p k t", k=4)[:, :, 0:n]).then_inc(
                    x_act, 1)

            def norm_squares(n, src, waits):
                c = n % 3
                tables(LN_EXP)
                for s_, v_ in waits:
                    act.wait_ge(s_, v_)
                if n:
                    act.wait_ge(n_sum, n)
                a.activation(SQ[:, :, :], src[:, :, c * CH:(c + 1) * CH], ACT.Square).then_inc(n_sq, 1)

            def tile_squares(q):
                i = SQUARED.index(q)
                u, c = QUANTA[q]
                t = UNITS[u][1] if UNITS[u][0] == 'out' else UNITS[u][1][1]
                act.wait_ge(evac['dve'], EVN[q])
                if i >= 2:
                    act.wait_ge(t_sum, i - 1)
                a.activation(SQT[i % 2][:, :], XT[:, t, c * CH:(c + 1) * CH], ACT.Square).then_inc(t_sq, 1)

            def norm_scale(n):
                act.wait_ge(n_tot, n + 1)
                rb = (RB1, RB2, RB3)[n // 3][n % 3]
                tables(LN_EXP)
                link(a.activation(rb[:, :], BK8[7][:, 0:CH], ACT.Ln, bias=CST[:, 2:3], scale=1.0 / D))
                a.activation(rb[:, :], rb[:, :], ACT.Exp, scale=-0.5).then_inc(n_rs, 1)

            def head(n):
                act.wait_ge(n_h, n + 1)
                c = n % 3
                w = CH if c < 2 else CH - NS
                h = (H1, H3)[n // 3][c % 2]
                dst = (HHI, H2I)[n // 3]
                for k in range(KT):
                    last = a.activation(dst[:, k, c * CH:c * CH + w], h[:, k, 0:w], ACT.Identity,
                                        bias=MOD[:, (0, 24)[n // 3] + k, 0:1])
                if c == 2:
                    last = a.copy(dst[:, :, c * CH + w:(c + 1) * CH], h[:, :, w:CH])
                last.then_inc(n_hi, 1)

            tables(GATES_SET)
            act.wait_ge(c_loaded, 32)
            a.activation(C9[:, 1, :], C9[:, 0, :], ACT.Sigmoid).then_inc(c_sig, 1)
            act.wait_ge(par_ready, 1)
            for q in range(16):
                if q % 4 == 0 and q:
                    ada_act(q // 4 - 1)
                if q < 9:
                    x_half(q, XT0)
            norm_squares(0, XT0, [(x_dve, 9), (x_act, 9)])
            for n in range(3):
                if n < 2:
                    norm_squares(n + 1, XT0, [])
                norm_scale(n)
            ada_act(3)
            split_hi(0)
            for n in range(3):
                head(n)
            end_phase(act, 0)

            def lora_in(w):
                a.activation(LA[0:32, 0, 0:w], MX[0:32, 6, 0:w], ACT.Tanh)
                a.copy(LA[32:64, 1, 0:w], MX[32:64, 6, 0:w])
                return a.activation(LA[64:P, 2, 0:w], MX[64:P, 6, 0:w], ACT.Sigmoid)

            def gates(w, gt):
                for j in range(2):
                    a.activation(SG[:, j, 0:w], BK8[2][:, j * BLK:j * BLK + w], ACT.Sigmoid, bias=par('rw_w0', j))
                    a.activation(SG[:, 2 + j, 0:w], BK8[2][:, (2 + j) * BLK:(2 + j) * BLK + w], ACT.Sigmoid,
                                 bias=par('rw_a0', j))
                return a.copy(gt[:, :, 0:w], BK8[3][:, 0:2 * BLK].rearrange("p (j t) -> p j t", j=2)[:, :, 0:w])

            def kk_scale(w):
                link(a.activation(RS[:, :, 0:w], T2[:, :, 0:w], ACT.Ln, scale=float(2 ** 18)))
                tables(LN_EXP)
                return a.activation(RS[:, :, 0:w], RS[:, :, 0:w], ACT.Exp, scale=-0.5, bias=CST[:, 1:2])

            def var_scale(w):
                link(a.activation(RSV[:, :, 0:w], BK8[5][:, 0:2 * BLK].rearrange("p (j t) -> p j t", j=2)[:, :, 0:w],
                                  ACT.Ln, scale=1.0 / 64, bias=CST[:, 0:1]))
                return a.activation(RSV[:, :, 0:w], RSV[:, :, 0:w], ACT.Exp, scale=-0.5)

            def rw(stage, b):
                def V(name):
                    return rw_dve, step(RW_DVE, name, b)

                def T_(name):
                    return rw_pe, step(RW_PE, name, b)

                def F(name):
                    return rwf_dve, step(RWF_DVE, name, b)

                if stage == 'lin':
                    tables(GATES_SET)
                    act.wait_ge(*F('mixed'))
                    if b:
                        act.wait_ge(rwf_pe, step(RWF_PE, 'bonus', b - 1))
                    lora_in(BLK).then_inc(rwf_act, 1)
                elif stage == 'gates':
                    act.wait_ge(rwf_pe, step(RWF_PE, 'lora', b))
                    gates(BLK, GT2[b % 2]).then_inc(rwf_act, 1)
                    tables(LN_SET)
                elif stage == 'rs':
                    act.wait_ge(*F('clamped'))
                    kk_scale(BLK).then_inc(rwf_act, 1)
                elif stage == 'decay':
                    act.wait_ge(*F('decays'))
                    if b:
                        act.wait_ge(rw_dve, step(RW_DVE, 'out', b - 1))
                    a.activation(EB[:, :, :], BB[:, :, :], ACT.Exp)
                    a.activation(ENB[:, :, :], BB[:, :, :], ACT.Exp, scale=-1.0)
                    a.activation(BM[:, :, :], BM[:, :, :], ACT.Exp).then_inc(rwf_act, 1)
                elif stage == 'turn':
                    act.wait_ge(*T_('turned'))
                    for dst, bank in ((ARt, BK8[6]), (BKt, BK8[7])):
                        last = a.copy(dst[:, :, :].rearrange("p c t -> p (c t)"), bank[:, :])
                    last.then_inc(rw_act, 1)
                    act.wait_ge(*T_('vturned'))
                    a.copy(UV[:, :, :].rearrange("p c t -> p (c t)"), BK8[6][:, :]).then_inc(rw_act, 1)
                elif stage[:3] == 'inv':
                    act.wait_ge(*T_(f'P{stage[3]}'))
                    a.copy(PS[:, :, :].rearrange("p c t -> p (c t)"), BK8[4][:, 0:256]).then_inc(rw_act, 1)
                elif stage == 'fold':
                    act.wait_ge(*T_('T1'))
                    a.copy(T1S[:, :, :].rearrange("p c t -> p (c t)"), BK8[5][:, 0:256]).then_inc(rw_act, 1)
                    act.wait_ge(*T_('PT'))
                    a.copy(PTS[:, :, :].rearrange("p c t -> p (c t)"), BK8[6][:, 0:256]).then_inc(rw_act, 1)
                elif stage == 'post':
                    act.wait_ge(*T_('var'))
                    var_scale(BLK).then_inc(rw_act, 1)

            def rws(s):
                V, T_ = smp('dve'), smp('pe')
                if s == 0:
                    tables(GATES_SET)
                    act.wait_ge(*V('mixed'))
                    lora_in(NS).then_inc(smp_act, 1)
                    act.wait_ge(*T_('lora'))
                    gates(NS, GT2[0]).then_inc(smp_act, 1)
                    tables(LN_SET)
                    act.wait_ge(*V('clamped'))
                    kk_scale(NS).then_inc(smp_act, 1)
                elif s == 1:
                    act.wait_ge(*V('vectors'))
                    a.activation(SG[:, 0:2, 0:NS], SG[:, 0:2, 0:NS], ACT.Exp).then_inc(smp_act, 1)
                    act.wait_ge(*T_('tok'))
                    for v_ in range(5):
                        a.copy(STKW[:, 0:1280].rearrange("b (h v k) -> b h v k", h=4, v=5)[:, :, v_, :],
                               BK8[3 + v_ // 2][0:NS, (v_ % 2) * 256:(v_ % 2) * 256 + 256].rearrange(
                                   "b (h k) -> b h k", h=4))
                    last = a.copy(STKW[:, 1280:1536], BK8[5][0:NS, 256:512])
                    last.then_inc(smp_act, 1)
                elif s == 3:
                    tables(LN_EXP)
                    act.wait_ge(*T_('var'))
                    var_scale(NS).then_inc(smp_act, 1)

            for what, arg in PLAN1:
                if what == 'split':
                    split_hi(arg)
                elif what == 'ev':
                    bring_out(arg)
                elif what == 'silu':
                    tables(GATES_SET)
                    if arg == 0:
                        act.wait_ge(smp_dve, SMP_DVE.index('bonus') + 1)
                    if arg >= 2:
                        act.wait_ge(silu_m, arg - 1)
                    a.activation(SGT[arg % 2][:, :], MIX[:, arg // 3, (arg % 3) * CH:(arg % 3 + 1) * CH],
                                 ACT.Sigmoid).then_inc(silu_s, 1)
                elif what[:3] == 'rw_' and what != 'rw_final':
                    rw(what[3:], arg)
                elif what == 'rws':
                    rws(arg)
            end_phase(act, 1)

            def pre():
                tables(GATES_SET)
                for t in range(6):
                    act.wait_ge(mb_loaded[t], 16)
                    if t >= 2:
                        act.wait_ge(silu_m, 18 + t - 1)
                    a.activation((SMT, STMP)[t % 2][:, 0:T], XB[t][:, :], ACT.Sigmoid).then_inc(silu_s, 1)
                tables(LN_EXP)
                act.wait_ge(pre_dma, 32)
                a.activation(AEX[:, :], AEX[:, :], ACT.Exp).then_inc(pre_act, 1)
                act.wait_ge(pre_dve, PRE_DVE.index('nabs') + 1)
                link(a.activation(DTE[:, :, :], DTN[:, :, :], ACT.Exp))
                a.activation(DTE[:, :, :], DTE[:, :, :], ACT.Ln, bias=1.0).then_inc(pre_act, 1)
                act.wait_ge(pre_dve, PRE_DVE.index('dta') + 1)
                a.activation(DTE[:, :, :], DTA[:, :, :], ACT.Exp).then_inc(pre_act, 1)
                act.wait_ge(pre_dve, PRE_DVE.index('es') + 1)
                a.activation(ES[:, :, :], ES[:, :, :], ACT.Exp)
                a.activation(ED[:, :, :].rearrange("p b h -> p (b h)"), BK8[4][:, 64:128], ACT.Exp).then_inc(pre_act, 1)

            def soft(w):
                link(a.activation(HE[:, :, 0:w], HN[:, :, 0:w], ACT.Exp))
                return a.activation(HL[:, :, 0:w], HE[:, :, 0:w], ACT.Ln, bias=1.0)

            def ssq_scale(w, bank, dst, n):
                link(a.activation(dst[:, :, 0:w], bank[:, 0:2 * BLK].rearrange("p (j t) -> p j t", j=2)[:, :, 0:w],
                                  ACT.Ln, scale=1.0 / n, bias=CST[:, 2:3]))
                return a.activation(dst[:, :, 0:w], dst[:, :, 0:w], ACT.Exp, scale=-0.5)

            def hg(stage, b):
                def V(name):
                    return hg_dve, step(HG_DVE, name, b)

                def T_(name):
                    return hg_pe, step(HG_PE, name, b)

                if stage == 'logits':
                    act.wait_ge(hgf_dve, step(HGF_DVE, 'nabs', b))
                    soft(BLK).then_inc(hgf_act, 1)
                elif stage == 'gate':
                    act.wait_ge(hgf_dve, step(HGF_DVE, 'logf', b))
                    a.activation(HK[:, :, :], HK[:, :, :], ACT.Exp).then_inc(hgf_act, 1)
                    act.wait_ge(hgf_dve, step(HGF_DVE, 'diffs', b))
                    a.activation(HX2[b % 2][:, :, :], HBb[:, :, :], ACT.Exp)
                    a.activation(HD[:, :, :, :], HD[:, :, :, :], ACT.Exp).then_inc(hgf_act, 1)
                elif stage == 'att':
                    act.wait_ge(*T_('turned'))
                    a.copy(HVT[:, :, :].rearrange("p j t -> p (j t)"), BK8[0][:, 0:256])
                    a.copy(HKT[:, :, :].rearrange("p j t -> p (j t)"), BK8[0][:, 256:512]).then_inc(hg_act, 1)
                    act.wait_ge(hg_act, step(HG_ACT, 'turned', b))
                    if b == 0:
                        act.wait_ge(pre_pool, 1)
                    for s in range(4):
                        t = slice(32 * s, 32 * s + 32)
                        last = a.copy(HVD[t, :, s, :], HVT[t, :, :])
                    last.then_inc(hg_act, 1)
                elif stage == 'sq':
                    act.wait_ge(*T_('ssq'))
                    ssq_scale(BLK, BK8[1], HR, 64).then_inc(hg_act, 1)
                elif stage == 'x':
                    x_half(9 + b, XT)

            def mb(stage, b):
                def V(name):
                    return mb_dve, step(MB_DVE, name, b)

                def T_(name):
                    return mb_pe, step(MB_PE, name, b)

                if stage == 'decay':
                    act.wait_ge(*T_('acum'))
                    for gr in range(2):
                        last = a.activation(E2[HP[gr], :, :].rearrange("p h t -> p (h t)"), BK8[6 + gr][HP[gr], :],
                                            ACT.Exp)
                    last.then_inc(mb_act, 1)
                    act.wait_ge(*V('seg'))
                    a.activation(SEG[:, :, :], SEG[:, :, :], ACT.Exp).then_inc(mb_act, 1)
                elif stage == 'sq':
                    act.wait_ge(*V('z'))
                    a.activation(T4[:, :, :], YS[:, :, :], ACT.Square).then_inc(mb_act, 1)
                    act.wait_ge(*T_('ssq'))
                    ssq_scale(BLK, BK8[7], RM, 256).then_inc(mb_act, 1)

            def smp_tok():
                act.wait_ge(hs_dve, HS_DVE.index('nabs') + 1)
                soft(NS).then_inc(hs_act, 1)
                act.wait_ge(hs_dve, HS_DVE.index('logf') + 1)
                a.activation(HE[:, :, 0:NS], HF[:, :, 0:NS], ACT.Exp)
                a.activation(HK[:, :, 0:NS], HK[:, :, 0:NS], ACT.Exp).then_inc(hs_act, 1)
                act.wait_ge(hs_pe, 1)
                for i in range(2):
                    last = a.copy(STK[:, 512 * i:512 * i + 512], BK8[2 + i][0:NS, :])
                last.then_inc(hs_act, 1)
                act.wait_ge(ms_pe, 1)
                a.copy(STOKEN[:, 0:512], BK8[4][0:NS, :])
                for v_ in range(2):
                    last = a.copy(STOKEN[:, 512:768].rearrange("b (g v n) -> b g v n", g=2, v=2)[:, :, v_, :],
                                  BK8[5][0:NS, v_ * P:(v_ + 1) * P].rearrange("b (g n) -> b g n", g=2))
                last.then_inc(ms_act, 1)

            def smp_out():
                act.wait_ge(hs_pe, 4)
                ssq_scale(NS, BK8[2], HR, 64).then_inc(hs_act, 1)
                act.wait_ge(ms_dve, MS_DVE.index('z') + 1)
                a.activation(T4[:, :, 0:NS], YS[:, :, 0:NS], ACT.Square).then_inc(ms_act, 1)
                act.wait_ge(ms_pe, 3)
                ssq_scale(NS, BK8[7], RM, 256).then_inc(ms_act, 1)

            for what, arg in PLAN2:
                if what == 'pre':
                    pre()
                elif what == 'adt':
                    ada_act(arg)
                elif what[:3] == 'hg_':
                    hg(what[3:], arg)
                elif what[:3] == 'mb_':
                    mb(what[3:], arg)
                elif what == 'smp_tok':
                    smp_tok()
                elif what == 'smp_out':
                    smp_out()
            end_phase(act, 2)

            def gu_head(n):
                u, c = QUANTA[UPS[n]]
                f = UNITS[u][1]
                act.wait_ge(evac['dve'], EVN[UPS[n]])
                a.copy(GHI[:, TILE_IN_GROUP[f], c * CH:(c + 1) * CH], GU[n % 2][:, :]).then_inc(gu_hi, 1)

            for what, arg in PLAN3:
                if what == 'split':
                    split_hi(arg)
                elif what == 'ev':
                    bring_out(arg)
                    if arg in UPS:
                        gu_head(UPS.index(arg))
                    if arg in SQUARED:
                        tile_squares(arg)
                elif what == 'mixsplit':
                    cols = slice(arg * CH, (arg + 1) * CH)
                    a.copy(MHI[:, :, cols], MIX[:, :, cols]).then_inc(mix_hi, 1)
                elif what == 'sum':
                    norm_scale(arg)
                    if arg == 5:
                        tables(SILU_SET)
                elif what == 'rest':
                    head(arg)
                elif what == 'y':
                    n = BLK if arg < NB else NS
                    act.wait_ge(y_turned, arg + 1)
                    if arg >= 2:
                        act.wait_ge(y_out[arg % 2], 16 * (arg // 2))
                    a.copy(OT[arg % 2][0:n, 0:512], BK8[YB[2 * (arg % 2)]][0:n, :]).then_inc(y_act, 1)

        @block.vector
        def _(dve):
            v = nc.vector
            link = linker(dve, dve_own)
            HP = [slice(0, 64), slice(64, P)]

            def split_lo(i):
                u = SPLIT[i]
                nk = unit_k(u)
                dve.wait_ge(w_hi, i + 1)
                whi, wlo = w_split(i)
                v.tensor_tensor(wlo[:, 0:nk, :], RAW[u % NRAW][:, 0:nk, :], whi[:, 0:nk, :].bitcast(F32),
                                ALU.subtract).then_inc(w_lo, 1)

            def conv(q, r):
                u, c = QUANTA[q]
                t = UNITS[u][1]
                s = STG[r % 2]
                w = [par('mb_conv_w', 6 * j + t) for j in range(4)]
                n = CH if c < 2 else CH - NS
                if c == 0:
                    link(v.memset(s[:, 0:3], 0.0))
                else:
                    link(v.tensor_copy(s[:, 0:3], STG[(r - 1) % 2][:, CH:CH + 3]))
                dve.wait_ge(evac['act'], EVN[q])
                if r:
                    dve.wait_ge(acc_out, 16 * r)
                acc = ACC[0]
                link(v.tensor_scalar(acc[:, 0:n], s[:, 0:n], w[0], par('mb_conv_b', t), ALU.mult, ALU.add))
                for j in range(1, 3):
                    link(v.scalar_tensor_tensor(acc[:, 0:n], s[:, j:j + n], w[j], acc[:, 0:n], ALU.mult, ALU.add))
                last = v.scalar_tensor_tensor(acc[:, 0:n], s[:, 3:3 + n], w[3], acc[:, 0:n], ALU.mult, ALU.add)
                if c == 2:
                    link(last)
                    old = SCV[:, t, :].rearrange("p (b j) -> p j b", j=3)
                    out = acc[:, n:CH]
                    link(v.tensor_scalar(out, old[:, 0, :], w[0], par('mb_conv_b', t), ALU.mult, ALU.add))
                    link(v.scalar_tensor_tensor(out, old[:, 1, :], w[1], out, ALU.mult, ALU.add))
                    link(v.scalar_tensor_tensor(out, old[:, 2, :], w[2], out, ALU.mult, ALU.add))
                    link(v.scalar_tensor_tensor(out, s[:, 3 + n:3 + CH], w[3], out, ALU.mult, ALU.add))
                    last = v.tensor_copy(XL[:, t, :], s[:, 3 + n - 3:3 + CH])
                last.then_inc(conv_done, 1)

            def bring_out(q):
                u, c = QUANTA[q]
                kind, arg = UNITS[u]
                if kind == 'xbc':
                    conv(q, STAGED.index(q))
                if evac_engine(q) != 'dve':
                    return
                bank = BK8[BANK[q]]
                n = CH if c < 2 else CH - NS
                dve.wait_ge(dense_done, q + 1)
                if kind == 'up':
                    i = UPS.index(q)
                    dve.wait_ge(evac['act'], EVN[GATES[i]])
                    if i >= 2:
                        dve.wait_ge(gu_hi, i - 1)
                    v.tensor_tensor(GU[i % 2][:, :], SGF[i % 2][:, :], bank[:, 0:CH], ALU.mult).then_inc(
                        evac['dve'], 1)
                    return
                t, m = (arg, 16) if kind == 'out' else (arg[1], 40)
                c0 = c * CH
                if c == 2:
                    link(v.tensor_tensor(TMP8[:, :], bank[:, n:CH], MOD[:, m + t, 1:9], ALU.mult))
                    link(v.tensor_tensor(XT[:, t, c0 + n:c0 + CH], XT[:, t, c0 + n:c0 + CH], TMP8[:, :], ALU.add))
                v.scalar_tensor_tensor(XT[:, t, c0:c0 + n], bank[:, 0:n], MOD[:, m + t, 0:1], XT[:, t, c0:c0 + n],
                                       ALU.mult, ALU.add).then_inc(evac['dve'], 1)

            def x_half(i, dst):
                dve.wait_ge(x_turned, i + 1)
                n = BLK if i % 9 < NB else NS
                b0 = 3 + 2 * (i % 2) if i < 9 else 0
                t0 = (i % 9) * BLK
                v.tensor_copy(dst[:, 4:8, t0:t0 + n],
                              BK8[b0 + 1][:, :].rearrange("p (k t) -> p k t", k=4)[:, :, 0:n]).then_inc(x_dve, 1)

            def norm_squares(n):
                dve.wait_ge(n_sq, n + 1)
                v.tensor_reduce(SS1[n][:, :], SQ[:, :, :].rearrange("p k t -> p t k"), AX.X, ALU.add).then_inc(n_sum, 1)

            def modulation(sc, g):
                link(v.scalar_tensor_tensor(A1[:, :, :], MOD[:, sc:sc + 8, :], 1.0,
                                            par(g, 0, 8).unsqueeze(2).broadcast_to([P, KT, 9]), ALU.add, ALU.mult))

            def scaled(n):
                c = n % 3
                cols = slice(c * CH, (c + 1) * CH)
                w = CH if c < 2 else CH - NS
                h = (H1, H3)[n // 3][c % 2]
                sh = (0, 24)[n // 3]
                src, rb = (XT0, XT)[n // 3], (RB1, RB2)[n // 3][c]
                if c == 0:
                    modulation(sh + 8, ('g_norm1', 'g_norm2')[n // 3])
                if c == 2:
                    dve.wait_ge(n_lo, n - 1)
                dve.wait_ge(n_rs, n + 1)
                if c == 2:
                    rs = rb[:, w:CH].unsqueeze(1).broadcast_to([P, KT, NS])
                    link(v.tensor_tensor(h[:, :, w:CH], src[:, :, cols.stop - NS:cols.stop], A1[:, :, 1:9], ALU.mult))
                    link(v.tensor_tensor(h[:, :, w:CH], h[:, :, w:CH], rs, ALU.mult))
                    v.tensor_tensor(h[:, :, w:CH], h[:, :, w:CH], MOD[:, sh:sh + 8, 1:9], ALU.add)
                for k in range(KT):
                    last = v.scalar_tensor_tensor(h[:, k, 0:w], src[:, k, cols.start:cols.start + w], A1[:, k, 0:1],
                                                  rb[:, 0:w], ALU.mult, ALU.mult)
                last.then_inc(n_h, 1)

            def rest(n):
                c = n % 3
                t0 = c * CH
                w = CH if c < 2 else CH - NS
                h = (H1, H3)[n // 3][c % 2]
                hi_, lo_, sh = ((HHI, HLO, 0), (H2I, H2L, 24))[n // 3]
                dve.wait_ge(n_hi, n + 1)
                for k in range(KT):
                    last = v.scalar_tensor_tensor(lo_[:, k, t0:t0 + w], h[:, k, 0:w], MOD[:, sh + k, 0:1],
                                                  hi_[:, k, t0:t0 + w].bitcast(F32), ALU.add, ALU.subtract)
                if c == 2:
                    last = v.tensor_tensor(lo_[:, :, t0 + w:t0 + CH], h[:, :, w:CH],
                                           hi_[:, :, t0 + w:t0 + CH].bitcast(F32), ALU.subtract)
                last.then_inc(n_lo, 1)

            dve.wait_ge(c_sig, 1)
            v.tensor_tensor(C9[:, 0, :], C9[:, 0, :], C9[:, 1, :], ALU.mult).then_inc(c_act, 1)
            dve.wait_ge(par_turned, 1)
            v.tensor_copy(CT[:, :, :].rearrange("p k c -> p (k c)"), BK8[7][:, 0:72])
            v.tensor_copy(PAR[:, 0:NR1], BK8[7][:, 128:128 + NR1])
            dve.wait_ge(dhead_loaded, 16)
            for hp in range(2):
                v.tensor_copy(par('mb_D', 0, 4)[HP[hp]], DHEAD[HP[hp], hp:8:2])
            v.tensor_copy(PAR[:, NR1:NR1 + NR2], BK8[7][:, 256:256 + NR2]).then_inc(par_ready, 1)
            for i in range(9):
                x_half(i, XT0)
            for n in range(3):
                norm_squares(n)
            split_lo(0)
            dve.wait_ge(par_ready, 1)
            dve.wait_ge(evac['ada'], 4)
            for stage, n in ((scaled, 0), (scaled, 1), (rest, 0), (scaled, 2), (rest, 1), (rest, 2)):
                stage(n)
            end_phase(dve, 0)

            def three(t):
                return t[:, :, :].rearrange("p j (c t) -> p (j c) t", c=2)

            def rw_mix(w, cur, prev):
                mu = par('rw_mu', 0, 7).unsqueeze(2).broadcast_to([P, 7, w])
                mx = MX[:, :, 0:w]
                link(v.tensor_tensor(mx, prev, cur, ALU.subtract))
                link(v.tensor_tensor(mx, mx, mu, ALU.mult))
                return v.tensor_tensor(mx, mx, cur, ALU.add)

            def rw_kk(w):
                for j in range(2):
                    link(v.tensor_scalar(KK[:, j, 0:w], MX[:, 2 + j, 0:w], par('rw_k_k', j), None, ALU.mult))
                return v.tensor_tensor(T2[:, :, 0:w], KK[:, :, 0:w], KK[:, :, 0:w], ALU.mult)

            def clamp(w, bank):
                return v.tensor_scalar(T2[:, :, 0:w], bank[:, 2 * BLK:4 * BLK].rearrange("p (j t) -> p j t", j=2)[:, :, 0:w],
                                       1e-24, None, ALU.max)

            def rw_keys(w):
                for j in range(2):
                    link(v.tensor_scalar(KP[:, j, 0:w], SG[:, 2 + j, 0:w], par('rw_k_a', j), OMKA[:, j:j + 1],
                                         ALU.mult, ALU.add))
                link(v.tensor_tensor(KP[:, :, 0:w], KP[:, :, 0:w], MX[:, 2:4, 0:w], ALU.mult))
                return v.tensor_tensor(SG[:, 2:4, 0:w], SG[:, 2:4, 0:w], KK[:, :, 0:w], ALU.mult)

            def rw_bonus_in(w, dst):
                link(v.tensor_tensor(dst[:, :, 0:w], MX[:, 0:2, 0:w], KP[:, :, 0:w], ALU.mult))
                for j in range(2):
                    last = v.tensor_scalar(dst[:, j, 0:w], dst[:, j, 0:w], par('rw_r_k', j), None, ALU.mult)
                return last

            def two(bank, w):
                return bank[:, 0:2 * BLK].rearrange("p (j t) -> p j t", j=2)[:, :, 0:w]

            def rw_post(w, V, T_, A, s, cols, o0, gt):
                o = OS[:, :, 0:w]
                v.tensor_copy(o, o0).then_inc(s, 1)
                dve.wait_ge(*V('o'))
                dve.wait_ge(*T_('mean'))
                link(v.scalar_tensor_tensor(o, two(BK8[4], w), -1.0 / 64, o, ALU.mult, ALU.add))
                v.tensor_tensor(OSQ[:, :, 0:w], o, o, ALU.mult).then_inc(s, 1)
                dve.wait_ge(*A('var'))
                link(v.tensor_tensor(o, o, RSV[:, :, 0:w], ALU.mult))
                for j in range(2):
                    last = v.tensor_scalar(OS[:, j, 0:w], OS[:, j, 0:w], par('rw_ln_g', j), par('rw_ln_b', j), ALU.mult,
                                           ALU.add)
                link(last)
                link(v.tensor_tensor(o, o, BON[:, :, 0:w], ALU.add))
                v.tensor_tensor(MIX[:, 6:8, cols], o, gt[:, :, 0:w], ALU.mult).then_inc(s, 1)

            def rw(stage, b):
                def V(name):
                    return rw_dve, step(RW_DVE, name, b)

                def T_(name):
                    return rw_pe, step(RW_PE, name, b)

                def A(name):
                    return rw_act, step(RW_ACT, name, b)

                def F(name):
                    return rwf_dve, step(RWF_DVE, name, b)

                def FA(name):
                    return rwf_act, step(RWF_ACT, name, b)

                B0, B1, B2, B3 = BK8[4:8]
                t0 = b * BLK
                if stage == 'mix':
                    if b == 0:
                        dve.wait_ge(init_pool, 1)
                        dve.wait_ge(evac['act'], EVN[LASTQ[16 + 7]])
                    rw_mix(BLK, PR[:, :, 1 + t0:1 + t0 + BLK], PR[:, :, t0:t0 + BLK]).then_inc(rwf_dve, 1)
                    dve.wait_ge(*F('mixed'))
                    rw_kk(BLK).then_inc(rwf_dve, 1)
                elif stage == 'gates':
                    dve.wait_ge(*FA('gates'))
                    clamp(BLK, BK8[3]).then_inc(rwf_dve, 1)
                elif stage == 'decays':
                    dve.wait_ge(*FA('rs'))
                    v.tensor_tensor(KK[:, :, :], KK[:, :, :], RS[:, :, :], ALU.mult)
                    link(v.tensor_scalar(SG[:, 0:2, :], SG[:, 0:2, :], -EXP_M05, None, ALU.mult))
                    for j in range(2):
                        last = v.tensor_tensor_scan(BB[:, j, :], CM64[:, :], SG[:, j, :], 0.0, ALU.mult, ALU.add)
                    link(last)
                    v.tensor_tensor(BM[:, :, :], BB[:, :, :], SG[:, 0:2, :], ALU.subtract).then_inc(rwf_dve, 1)
                    link(rw_keys(BLK))
                elif stage == 'decay':
                    dve.wait_ge(*FA('exps'))
                    for hp in range(2):
                        r = HP[hp]
                        v.scalar_tensor_tensor(AR[r, :, hp, :], three(KK)[r], -1.0, three(BM)[r], ALU.mult, ALU.mult)
                        v.tensor_tensor(AR[r, :, 1 - hp, :], MX[r, 0:2, :].rearrange("p j (c t) -> p (j c) t", c=2),
                                        three(EB)[r], ALU.mult)
                        v.tensor_tensor(BK[r, :, hp, :], SG[r, 2:4, :].rearrange("p j (c t) -> p (j c) t", c=2),
                                        three(ENB)[r], ALU.mult)
                        v.tensor_tensor(BK[r, :, 1 - hp, :], three(KP)[r], three(ENB)[r], ALU.mult)
                        last = v.tensor_copy(VZ[r, :, 1 - hp, :],
                                             MX[r, 4:6, :].rearrange("p j (c t) -> p (j c) t", c=2))
                    last.then_inc(rwf_dve, 1)
                    dve.wait_ge(*F('operands'))
                    rw_bonus_in(BLK, KK).then_inc(rwf_dve, 1)
                elif stage == 'turn':
                    dve.wait_ge(*T_('A'))
                    for hp, bank in ((0, B0), (1, B1)):
                        last = v.tensor_tensor(AM[:, hp, :, :], bank[:, :].rearrange("p (c t) -> p c t", c=4),
                                               RWM[:, hp, :].unsqueeze(1).broadcast_to([P, 4, P]), ALU.mult)
                    last.then_inc(rw_dve, 1)
                    dve.wait_ge(*V('masked'))
                    eye = I4[:, :].unsqueeze(1).broadcast_to([P, 4, 64])
                    v.tensor_copy(X[:, :, :], eye)
                    link(v.tensor_copy(Y[:, :, :], eye))
                    dve.wait_ge(*T_('N'))
                    v.copy_predicated(X[:, :, :], LM[:, 0, 0, :].unsqueeze(1).broadcast_to([P, 4, 64]),
                                      B3[:, 0:256].rearrange("p (c t) -> p c t", c=4))
                    for hp in range(2):
                        last = v.copy_predicated(Y[HP[hp], :, :],
                                                 LM[HP[hp], 0, 1, :].unsqueeze(1).broadcast_to([64, 4, 64]),
                                                 AM[HP[hp], hp, :, 64 * hp:64 * hp + 64])
                    last.then_inc(rw_dve, 1)
                    dve.wait_ge(rwf_pe, step(RWF_PE, 'bonus', b))
                    link(v.tensor_tensor(BON[:, :, :], two(BK8[2], BLK), MX[:, 4:6, :], ALU.mult))
                elif stage[:3] == 'inv':
                    lv = int(stage[3])
                    dve.wait_ge(*T_(f'XY{lv}'))
                    if lv < 5:
                        v.copy_predicated(X[:, :, :], LM[:, lv, 0, :].unsqueeze(1).broadcast_to([P, 4, 64]),
                                          B1[:, 0:256].rearrange("p (c t) -> p c t", c=4))
                    v.copy_predicated(Y[:, :, :], LM[:, lv, 1, :].unsqueeze(1).broadcast_to([P, 4, 64]),
                                      B3[:, 0:256].rearrange("p (c t) -> p c t", c=4)).then_inc(rw_dve, 1)
                elif stage == 'fold':
                    dve.wait_ge(*T_('W1'))
                    v.tensor_copy(W1S[:, :, :].rearrange("p c t -> p (c t)"), B0[:, 0:256]).then_inc(rw_dve, 1)
                elif stage[:3] == 'seq':
                    c = int(stage[3])
                    dve.wait_ge(*T_(f'U{c}'))
                    dve.wait_ge(*V('W1'))
                    for hp in range(2):
                        r = HP[hp]
                        last = v.tensor_tensor(
                            UV[r, c:4:2, 64 * hp:64 * hp + 64], B1[r, 0:P].rearrange("p (j x) -> p j x", j=2),
                            W1S[r, c:4:2, :], ALU.add)
                    last.then_inc(rw_dve, 1)
                    dve.wait_ge(*T_(f'S{c}'))
                    link(v.tensor_tensor(ST[:, :, :], ST[:, :, :], B2[:, 0:P].rearrange("p (j x) -> p j x", j=2),
                                         ALU.add))
                    e = 64 * c + 63
                    v.tensor_tensor(ST[:, :, :], ST[:, :, :], EB[:, :, e:e + 1].broadcast_to([P, 2, 64]),
                                    ALU.mult).then_inc(rw_dve, 1)
                elif stage == 'post':
                    rw_post(BLK, V, T_, A, rw_dve, slice(t0, t0 + BLK), two(B3, BLK), GT2[b % 2])

            def rws(s):
                V, T_, A = smp('dve'), smp('pe'), smp('act')
                if s == 0:
                    dve.wait_ge(rw_dve, step(RW_DVE, 'out', NB - 1))
                    rw_mix(NS, PR[:, :, 1 + SEQ:1 + T], SHF[:, :, :]).then_inc(smp_dve, 1)
                    dve.wait_ge(*V('mixed'))
                    rw_kk(NS).then_inc(smp_dve, 1)
                    dve.wait_ge(*A('gates'))
                    clamp(NS, BK8[3]).then_inc(smp_dve, 1)
                elif s == 1:
                    dve.wait_ge(*A('rs'))
                    link(v.tensor_tensor(KK[:, :, 0:NS], KK[:, :, 0:NS], RS[:, :, 0:NS], ALU.mult))
                    link(v.tensor_scalar(SG[:, 0:2, 0:NS], SG[:, 0:2, 0:NS], -EXP_M05, None, ALU.mult))
                    rw_keys(NS).then_inc(smp_dve, 1)
                    dve.wait_ge(*V('vectors'))
                    rw_bonus_in(NS, T2).then_inc(smp_dve, 1)
                elif s == 2:
                    dve.wait_ge(smp_dma, 3 * 16)
                    dve.wait_ge(smp_dma2, 2 * 16)
                    S = SWK[:, :].rearrange("p (v k) -> p v k", v=16)
                    W = SW1[:, :].rearrange("p (v k) -> p v k", v=16)

                    def key(i):
                        return SWV[:, 64 * i:64 * i + 64].unsqueeze(1).broadcast_to([P, 16, 64])

                    def val(x):
                        return x.unsqueeze(2).broadcast_to([P, 16, 64])

                    sk = RS[:, 0, 0:16]
                    link(v.tensor_tensor(W, S, key(1), ALU.mult))
                    link(v.tensor_reduce(sk, W, AX.X, ALU.add))
                    link(v.tensor_tensor(S, S, key(4), ALU.mult))
                    link(v.tensor_tensor(W, val(sk), key(2), ALU.mult))
                    link(v.tensor_tensor(S, S, W, ALU.subtract))
                    link(v.tensor_tensor(W, val(SWV[:, 320:336]), key(3), ALU.mult))
                    link(v.tensor_tensor(S, S, W, ALU.add))
                    link(v.tensor_tensor(W, S, key(0), ALU.mult))
                    v.tensor_reduce(SWV[:, 0:16], W, AX.X, ALU.add).then_inc(smp_dve, 1)
                elif s == 3:
                    dve.wait_ge(*T_('oturn'))
                    link(v.tensor_tensor(BON[:, :, 0:NS], two(BK8[2], NS), MX[:, 4:6, 0:NS], ALU.mult))
                    rw_post(NS, V, T_, A, smp_dve, slice(SEQ, T), BK8[6][:, 0:16].rearrange("p (j t) -> p j t", j=2),
                            GT2[0])

            def rw_final():
                dve.wait_ge(fin_pe, 1)
                v.tensor_copy(FST[:, :, :].rearrange("v j k -> v (j k)"), BK8[3][0:64, 0:256])
                v.tensor_copy(FSH[:, 0:512], BK8[4][0:9, :])
                v.tensor_copy(FSH[:, 512:896], BK8[5][0:9, 0:384])
                v.tensor_copy(FCV[:, 0:512], BK8[6][0:11, :])
                v.tensor_copy(FCV[:, 512:768], BK8[7][0:11, 0:256]).then_inc(fin_dve, 1)

            for what, arg in PLAN1:
                if what == 'split':
                    if FIRSTQ[SPLIT[arg - 1]] < q_rw_end:
                        split_lo(arg)
                elif what == 'ev':
                    bring_out(arg)
                elif what == 'silu':
                    x = MIX[:, arg // 3, (arg % 3) * CH:(arg % 3 + 1) * CH]
                    dve.wait_ge(silu_s, arg + 1)
                    v.tensor_tensor(x, x, SGT[arg % 2][:, :], ALU.mult).then_inc(silu_m, 1)
                elif what == 'dt':
                    dve.wait_ge(st_turned, 1)
                    v.tensor_copy(SCV[:, :, :].rearrange("p t c -> p (t c)"), BK8[3][:, 0:144])
                    v.tensor_copy(SHF[:, :, :].rearrange("p t c -> p (t c)"), BK8[3][:, 160:216])
                    link(v.tensor_scalar(OMKA[:, :], par('rw_k_a', 0, 2), -1.0, 1.0, ALU.mult, ALU.add))
                    dve.wait_ge(dt_done, 1)
                    v.tensor_copy(DTZ[:, :, :].rearrange("p b h -> p (b h)"), BK8[4][:, 0:72]).then_inc(dt_read, 1)
                    dve.wait_ge(dt_read, 1)
                elif what[:3] == 'rw_' and what != 'rw_final':
                    rw(what[3:], arg)
                elif what == 'rws':
                    rws(arg)
                elif what == 'rw_final':
                    rw_final()
            end_phase(dve, 1)

            def pre():
                for t in range(6):
                    dve.wait_ge(silu_s, 18 + t + 1)
                    v.tensor_tensor(XB[t][:, :], XB[t][:, :], (SMT, STMP)[t % 2][:, 0:T], ALU.mult).then_inc(silu_m, 1)
                dve.wait_ge(silu_m, 24)
                for t in range(6):
                    v.tensor_copy(XBS[:, t, :], XB[t][:, SEQ:T])
                dve.wait_ge(pre_dma, 32)
                link(v.tensor_tensor(DTZ[:, :, :], DTZ[:, :, :], DTB[:, :].unsqueeze(1).broadcast_to([P, 9, 8]), ALU.add))
                v.scalar_tensor_tensor(DTN[:, :, :], DTZ[:, :, :], -1.0, DTZ[:, :, :], ALU.mult, ALU.min).then_inc(
                    pre_dve, 1)
                dve.wait_ge(pre_act, PRE_ACT.index('soft') + 1)
                link(v.scalar_tensor_tensor(DT[:, :, :], DTZ[:, :, :], 0.0, DTE[:, :, :], ALU.max, ALU.add))
                v.scalar_tensor_tensor(DTA[:, :, :], DT[:, :, :], -1.0, AEX[:, :].unsqueeze(1).broadcast_to([P, 9, 8]),
                                       ALU.mult, ALU.mult).then_inc(pre_dve, 1)
                dve.wait_ge(pre_pe, 1)
                link(v.tensor_copy(ACOL[:, :, :].rearrange("p b h -> p (b h)"), BK8[4][:, 0:64]))
                v.tensor_tensor(ES[:, :, :].rearrange("p b h -> p (b h)"), BK8[4][:, 64:128],
                                ACOL[:, :, :].rearrange("p b h -> p (b h)"), ALU.subtract).then_inc(pre_dve, 1)
                dve.wait_ge(pre_act, PRE_ACT.index('ed') + 1)
                for i, src in enumerate((DT, DTE)):
                    v.tensor_copy(DTW[:, i, :, :], src[:, 8, :].unsqueeze(2).broadcast_to([P, 8, 2]))
                for gr in range(2):
                    last = v.tensor_copy(EDG[HP[gr], :, :], ED[HP[gr], :, 4 * gr:4 * gr + 4])
                last.then_inc(pre_dve, 1)
                dve.wait_ge(pre_dve, PRE_DVE.index('twice') + 1)

            def hg_nabs(w, HB):
                f = HB[:, 2:4, 0:w]
                return v.scalar_tensor_tensor(HN[:, :, 0:w], f, -1.0, f, ALU.mult, ALU.min)

            def hg_logf(w, HB):
                f = HB[:, 2:4, 0:w]
                link(v.scalar_tensor_tensor(HF[:, :, 0:w], f, 0.0, HL[:, :, 0:w], ALU.min, ALU.subtract))
                return v.tensor_tensor(HK[:, :, 0:w], HF[:, :, 0:w], f, ALU.subtract)

            def hg_out(w, cols, s):
                link(v.tensor_tensor(HO[:, :, 0:w], HO[:, :, 0:w], HR[:, :, 0:w], ALU.mult))
                for j in range(2):
                    last = v.scalar_tensor_tensor(MIX[:, j, cols], HO[:, j, 0:w], par('hg_norm_g', j), MIX[:, j, cols],
                                                  ALU.mult, ALU.mult)
                last.then_inc(s, 1)

            def hg(stage, b):
                def V(name):
                    return hg_dve, step(HG_DVE, name, b)

                def T_(name):
                    return hg_pe, step(HG_PE, name, b)

                def A(name):
                    return hg_act, step(HG_ACT, name, b)

                H0, H1, H2, H3 = BK8[0:4]
                HB, HX = HB2[b % 2], HX2[b % 2]
                if stage == 'logits':
                    dve.wait_ge(hg_loaded[b % 2], 16 * (b // 2 + 1))
                    hg_nabs(BLK, HB).then_inc(hgf_dve, 1)
                elif stage == 'gate':
                    dve.wait_ge(hgf_act, step(HGF_ACT, 'soft', b))
                    if b:
                        dve.wait_ge(hg_pe, step(HG_PE, 'att', b - 1))
                    hg_logf(BLK, HB).then_inc(hgf_dve, 1)
                    dve.wait_ge(hgf_dve, step(HGF_DVE, 'logf', b))
                    for j in range(2):
                        link(v.tensor_tensor_scan(HBb[:, j, :], CM32[:, :], HF[:, j, :], 0.0, ALU.mult, ALU.add))
                    cum = HBb[:, :, :].rearrange("p j t -> p (j t)")
                    for lv, n in enumerate(HLEV):
                        x = cum.rearrange("p (b e r) -> p b e r", e=2, r=n)
                        d = HD[:, lv, :, :].rearrange("p j t -> p (j t)").rearrange("p (b e r) -> p b e r", e=2, r=n)
                        nb = 2 * BLK // (2 * n)
                        ref = x[:, :, 0, n - 1:n].broadcast_to([P, nb, n])
                        v.tensor_tensor(d[:, :, 0, :], ref, x[:, :, 0, :], ALU.subtract)
                        v.tensor_tensor(d[:, :, 1, :], x[:, :, 1, :], ref, ALU.subtract)
                    x = cum.rearrange("p (b r) -> p b r", r=32)
                    v.tensor_tensor(HD[:, 5, :, :].rearrange("p j t -> p (j t)").rearrange("p (b r) -> p b r", r=32),
                                    x[:, :, 31:32].broadcast_to([P, 8, 32]), x, ALU.subtract).then_inc(hgf_dve, 1)
                elif stage == 'levels':
                    dve.wait_ge(hgf_act, step(HGF_ACT, 'exps', b))
                    q = HB[:, 0:2, :].rearrange("p j t -> p (j t)")
                    k = HK[:, :, :].rearrange("p j t -> p (j t)")
                    for lv, n in enumerate(HLEV):
                        d = HD[:, lv, :, :].rearrange("p j t -> p (j t)").rearrange("p (b e r) -> p b e r", e=2, r=n)
                        for e, src in ((0, k), (1, q)):
                            v.tensor_tensor(d[:, :, e, :], d[:, :, e, :],
                                            src.rearrange("p (b e r) -> p b e r", e=2, r=n)[:, :, e, :], ALU.mult)
                    v.tensor_tensor(HD[:, 5, :, :], HD[:, 5, :, :], HK[:, :, :], ALU.mult)
                    if b:
                        dve.wait_ge(hg_pe, step(HG_PE, 'o', b - 1))
                    v.tensor_tensor(HQ[:, :, :], HB[:, 0:2, :], HX[:, :, :], ALU.mult).then_inc(hgf_dve, 1)
                elif stage == 'att':
                    dve.wait_ge(*T_('att'))
                    mask = HMK[:, :, :].unsqueeze(2).broadcast_to([P, 6, 2, 32])
                    for hp, bank in ((0, H1), (1, H2)):
                        last = v.tensor_tensor(HAS[:, hp, :, :, :],
                                               bank[:, 0:384].rearrange("p (l j t) -> p l j t", l=6, j=2), mask, ALU.mult)
                    last.then_inc(hg_dve, 1)
                    dve.wait_ge(*V('masked'))
                    for hp in range(2):
                        last = v.tensor_reduce(HAT[:, 2 * hp:2 * hp + 2, :].rearrange("p j t -> p (j t)"),
                                               HAS[:, hp, :, :, :].rearrange("p l j t -> p (j t) l"), AX.X, ALU.add)
                    link(last)
                    if b == 0:
                        dve.wait_ge(pre_pool, 1)
                    for s in range(4):
                        t = slice(32 * s, 32 * s + 32)
                        last = v.tensor_copy(HAD[t, :, t], HAT[t, :, :])
                    last.then_inc(hg_dve, 1)
                elif stage == 'state':
                    link(v.tensor_copy(HSH[:, 0, :, :], HSH[:, 4, :, :]))
                    dve.wait_ge(*T_('u'))
                    for s in range(4):
                        for j in range(2):
                            e = 32 * s + 31
                            last = v.scalar_tensor_tensor(HSH[:, s + 1, j, :], HSH[:, s, j, :], HX[:, j, e:e + 1],
                                                          H0[:, j * 256 + 64 * s:j * 256 + 64 * s + 64], ALU.mult, ALU.add)
                        if s < 3:
                            link(last)
                    last.then_inc(hg_dve, 1)
                elif stage == 'sq':
                    dve.wait_ge(*T_('o'))
                    v.tensor_copy(HO[:, :, :].rearrange("p j t -> p (j t)"), H2[:, 0:256]).then_inc(hg_dve, 1)
                    dve.wait_ge(*V('o'))
                    v.tensor_tensor(HT[:, :, :], HO[:, :, :], HO[:, :, :], ALU.mult).then_inc(hg_dve, 1)
                elif stage == 'out':
                    dve.wait_ge(*A('rs'))
                    hg_out(BLK, slice(b * BLK, (b + 1) * BLK), hg_dve)
                elif stage == 'x':
                    x_half(9 + b, XT)

            def mb_skip(w, x, ybank):
                for t in range(4):
                    last = v.scalar_tensor_tensor(YS[:, t, 0:w], x(t), par('mb_D', t), ybank(t), ALU.mult,
                                                  ALU.add)
                return last

            def mb_out(w, cols, s):
                for t in range(4):
                    last = v.scalar_tensor_tensor(MIX[:, 2 + t, cols], YS[:, t, 0:w], par('mb_norm_g', t),
                                                  RM[:, t // 2, 0:w], ALU.mult, ALU.mult)
                last.then_inc(s, 1)

            def mb(stage, b):
                def V(name):
                    return mb_dve, step(MB_DVE, name, b)

                def T_(name):
                    return mb_pe, step(MB_PE, name, b)

                def A(name):
                    return mb_act, step(MB_ACT, name, b)

                M0, M1, M2, M3 = BK8[4:8]
                cols = slice(b * BLK, (b + 1) * BLK)
                if stage == 'turn':
                    dve.wait_ge(mbf_pe, b + 1)
                    if b:
                        dve.wait_ge(mb_pool, step(MB_POOL, 'ce', b - 1))
                    v.tensor_tensor(XD[:, :, :], M0[:, :].rearrange("p (h x) -> p h x", h=8),
                                    DT[:, b, :].unsqueeze(2).broadcast_to([P, 8, 64]), ALU.mult).then_inc(mbf_dve, 1)
                    v.tensor_copy(BT[:, :], M1[:, 0:P])
                    v.tensor_tensor(CBM[:, 0, :], M1[:, P:2 * P], triu[:, :], ALU.mult)
                    v.tensor_tensor(CBM[:, 1, :], M2[:, 0:P], triu[:, :], ALU.mult).then_inc(mbf_dve, 1)
                elif stage == 'decay':
                    dve.wait_ge(*A('E2'))
                    for h in range(8):
                        last = v.tensor_scalar(SEG[:, h, :], (M2, M3)[h // 4][:, (h % 4) * P:(h % 4 + 1) * P],
                                               ACOL[:, b, h:h + 1], 0.0, ALU.subtract, ALU.min)
                    last.then_inc(mb_dve, 1)
                    dve.wait_ge(*A('L'))
                    for gr in range(2):
                        last = v.tensor_tensor(MM[:, 4 * gr:4 * gr + 4, :], SEG[:, 4 * gr:4 * gr + 4, :],
                                               CBM[:, gr, :].unsqueeze(1).broadcast_to([P, 4, P]), ALU.mult)
                    last.then_inc(mb_dve, 1)
                elif stage == 'prod':
                    dve.wait_ge(*T_('y'))
                    mb_skip(BLK, lambda t: XB[t][:, cols], lambda t: (M1, M2)[t // 2][:, (t % 2) * P:(t % 2 + 1) * P]).then_inc(mb_dve, 1)
                    dve.wait_ge(*T_('S'))
                    link(v.tensor_tensor(STt[:, :, :], STt[:, :, :], EDG[:, b, :].unsqueeze(2).broadcast_to([P, 4, 64]),
                                         ALU.mult))
                    v.tensor_tensor(STt[:, :, :], STt[:, :, :], M0[:, 0:256].rearrange("p (h x) -> p h x", h=4),
                                    ALU.add).then_inc(mb_dve, 1)
                    dve.wait_ge(*V('y'))
                    v.tensor_tensor(YS[:, :, :], YS[:, :, :], MIX[:, 2:6, cols], ALU.mult).then_inc(mb_dve, 1)
                elif stage == 'out':
                    dve.wait_ge(*A('rs'))
                    mb_out(BLK, cols, mb_dve)

            def smp_tok():
                HB = HB2[NB % 2]
                dve.wait_ge(hg_loaded[NB % 2], 16 * (NB // 2 + 1))
                hg_nabs(NS, HB).then_inc(hs_dve, 1)
                dve.wait_ge(hs_act, HS_ACT.index('soft') + 1)
                hg_logf(NS, HB).then_inc(hs_dve, 1)

            def smp_state():
                dve.wait_ge(hs_dma, 32)
                dve.wait_ge(hs_dma2, 2 * 16)
                S = SHG[:, :].rearrange("p (k v) -> p k v", k=16)
                W = SHT2[:, :].rearrange("p (k v) -> p k v", k=16)

                def key(i):
                    return SV1[:, 16 * i:16 * i + 16].unsqueeze(2).broadcast_to([P, 16, 64])

                link(v.tensor_tensor(S, S, key(1), ALU.mult))
                link(v.tensor_tensor(W, SV1[:, 64:128].unsqueeze(1).broadcast_to([P, 16, 64]), key(2), ALU.mult))
                v.tensor_tensor(S, S, W, ALU.add).then_inc(hs_dve, 1)
                dve.wait_ge(hs_dve, HS_DVE.index('state') + 1)
                link(v.tensor_tensor(W, S, key(0), ALU.mult))
                v.tensor_reduce(SO[:, :], W.rearrange("p k v -> p v k"), AX.X, ALU.add).then_inc(hs_dve, 1)
                dve.wait_ge(hs_pe, 2)
                v.tensor_copy(SO2[:, :], BK8[2][0:32, 0:64]).then_inc(hs_dve, 1)
                dve.wait_ge(ms_dma, 4 * 16)
                dve.wait_ge(ms_dma2, 4 * 16)
                S = SSM[:, :].rearrange("p (x n) -> p x n", x=32)
                W = SMT[:, :].rearrange("p (x n) -> p x n", x=32)
                link(v.tensor_scalar(SV2[:, 128:160], SV2[:, 128:160], SV2[:, 160:161], None, ALU.mult))
                link(v.tensor_scalar(SSM[:, :], SSM[:, :], SV2[:, 161:162], None, ALU.mult))
                link(v.tensor_tensor(W, SV2[:, 128:160].unsqueeze(2).broadcast_to([P, 32, 64]),
                                     SV2[:, 0:64].unsqueeze(1).broadcast_to([P, 32, 64]), ALU.mult))
                link(v.tensor_tensor(S, S, W, ALU.add))
                link(v.tensor_tensor(W, S, SV2[:, 64:128].unsqueeze(1).broadcast_to([P, 32, 64]), ALU.mult))
                v.tensor_reduce(SY[:, :], W, AX.X, ALU.add).then_inc(ms_dve, 1)

            def smp_out():
                dve.wait_ge(hs_pe, 3)
                link(v.tensor_copy(HO[:, :, 0:NS], BK8[3][:, 0:16].rearrange("p (j t) -> p j t", j=2)))
                v.tensor_tensor(HT[:, :, 0:NS], HO[:, :, 0:NS], HO[:, :, 0:NS], ALU.mult).then_inc(hs_dve, 1)
                dve.wait_ge(hs_act, HS_ACT.index('rs') + 1)
                hg_out(NS, slice(SEQ, T), hs_dve)
                dve.wait_ge(ms_pe, 2)
                link(mb_skip(NS, lambda t: XBS[:, t, :], lambda t: BK8[6][:, 8 * t:8 * t + 8]))
                v.tensor_tensor(YS[:, :, 0:NS], YS[:, :, 0:NS], MIX[:, 2:6, SEQ:T], ALU.mult).then_inc(ms_dve, 1)
                dve.wait_ge(ms_act, MS_ACT.index('rs') + 1)
                mb_out(NS, slice(SEQ, T), ms_dve)

            for what, arg in PLAN2:
                if what == 'pre':
                    pre()
                elif what[:3] == 'hg_':
                    hg(what[3:], arg)
                elif what[:3] == 'mb_':
                    mb(what[3:], arg)
                elif what == 'smp_tok':
                    smp_tok()
                elif what == 'smp_state':
                    smp_state()
                elif what == 'smp_out':
                    smp_out()
                elif what == 'mix_final':
                    dve.wait_ge(fin_pe, 2)
                    v.tensor_copy(STF[:, :, :].rearrange("p a x -> p (a x)"), BK8[0][:, 0:256]).then_inc(fin_dve, 1)
            end_phase(dve, 2)

            def gu_rest(n):
                u, c = QUANTA[UPS[n]]
                f = UNITS[u][1]
                cols = slice(c * CH, (c + 1) * CH)
                t = TILE_IN_GROUP[f]
                dve.wait_ge(gu_hi, n + 1)
                v.tensor_tensor(GLO[:, t, cols], GU[n % 2][:, :], GHI[:, t, cols].bitcast(F32), ALU.subtract).then_inc(
                    gu_lo, 1)

            summed = [0]

            def add_squares(upto):
                while summed[0] < upto:
                    i = summed[0]
                    c = QUANTA[SQUARED[i]][1]
                    ss = (SS2, SS3)[i // 24][c][:, :]
                    dve.wait_ge(t_sq, i + 1)
                    if i % 24 < NCH:
                        ins = v.tensor_copy(ss, SQT[i % 2][:, :])
                    else:
                        dve.wait_ge(t_sum, i)
                        ins = v.tensor_tensor(ss, ss, SQT[i % 2][:, :], ALU.add)
                    ins.then_inc(t_sum, 1)
                    summed[0] += 1

            for what, arg in PLAN3:
                if what == 'split':
                    split_lo(arg)
                elif what == 'ev':
                    bring_out(arg)
                    if arg in UPS:
                        gu_rest(UPS.index(arg))
                    if arg in SQUARED:
                        add_squares(SQUARED.index(arg))
                elif what == 'sum':
                    add_squares(24 * (arg // 6) + 18 + 2 * (arg % 3 + 1))
                elif what == 'scaled':
                    scaled(arg)
                elif what == 'rest':
                    rest(arg)
                elif what == 'normed':
                    c = arg % 3
                    cols = slice(c * CH, (c + 1) * CH)
                    dve.wait_ge(n_rs, arg + 1)
                    for k in range(KT):
                        last = v.scalar_tensor_tensor(XT[:, k, cols], XT[:, k, cols], par('g_final', k), RB3[c][:, :],
                                                      ALU.mult, ALU.mult)
                    last.then_inc(n_h, 1)
                elif what == 'y':
                    n = BLK if arg < NB else NS
                    dve.wait_ge(y_turned, arg + 1)
                    if arg >= 2:
                        dve.wait_ge(y_out[arg % 2], 16 * (arg // 2))
                    v.tensor_copy(OT[arg % 2][0:n, 512:D], BK8[YB[2 * (arg % 2) + 1]][0:n, :]).then_inc(y_dve, 1)
                elif what == 'mixsplit':
                    cols = slice(arg * CH, (arg + 1) * CH)
                    dve.wait_ge(mix_hi, arg + 1)
                    v.tensor_tensor(MLO[:, :, cols], MIX[:, :, cols], MHI[:, :, cols].bitcast(F32),
                                    ALU.subtract).then_inc(mix_lo, 1)


def kernel(**inputs):
    import numpy as np
    import concourse.bacc as bacc
    from concourse.bass_utils import run_bass_kernel_spmd

    nc = bacc.Bacc("TRN2", target_bir_lowering=False, num_devices=1)
    arrays, args = {}, []
    for name in IN_NAMES:
        arr = np.ascontiguousarray(inputs[name])
        arrays[f"in_{name}"] = arr
        args.append(nc.dram_tensor(f"in_{name}", arr.shape, mybir.dt.from_np(arr.dtype), kind="ExternalInput").ap())
    outs = [nc.dram_tensor(f"out_{i}", s, F32, kind="ExternalOutput").ap() for i, s in enumerate(OUT_SHAPES)]
    kernel_program(nc, args, outs)
    res = run_bass_kernel_spmd(nc, [arrays], core_ids=[0]).results[0]
    return tuple(res[f"out_{i}"] for i in range(len(OUT_SHAPES)))
```
